# Optimizing a Trainium2 kernel written in Bass

```python
import math
import jax, jax.numpy as jnp
from jax import lax
import numpy as np

D_MODEL = 1024
BATCH = 1
SEQ = 512
DEPTH = 2
DEC_BATCH = 8
DEC_SEQ = 1
PAST_LEN = 512
PAGE_SIZE = 128

HEAD_DIM = 64
HEADS_PER_GROUP = 8
DIL_WINDOWS = (128, 512, 2048)
DIL_RATES = (1, 4, 16)
N_DIL = len(DIL_WINDOWS)
ATTN_BLOCK = 128
ATTN_SCALE = HEAD_DIM ** -0.5
ROT_DIM = HEAD_DIM // 4
ROPE_THETA = 500000.0
ATTN_WIDTH = HEADS_PER_GROUP * HEAD_DIM
QKV_COLS = 3 * N_DIL * ATTN_WIDTH
CONV_CH = D_MODEL // 4
CONV_WIDTH = 31
IN_COLS = QKV_COLS + 2 * CONV_CH
MIX_OUT = ATTN_WIDTH + CONV_CH
POOL_WINDOWS = (2, 4, 8, 16)
POOL_GROUPS = len(POOL_WINDOWS)
POOL_CH = D_MODEL // POOL_GROUPS
POOL_PREFIX = max(POOL_WINDOWS) - 1
N_EXPERTS = 16
N_EXPERT_GROUPS = 4
EXPERTS_PER_GROUP = N_EXPERTS // N_EXPERT_GROUPS
TOP_K = 2
D_EXPERT = 256
N_EVEN = (DEPTH + 1) // 2
N_ODD = DEPTH // 2
DN_ALPHA = (2.0 * DEPTH) ** 0.25
DN_BETA = (8.0 * DEPTH) ** -0.25
LN_EPS = 1e-5

kernel_name = 'hybrid_dilated_conv_pool_moe_decoder_step'

def layer_norm(x, g, b):
    xf = x.astype(jnp.float32)
    mu = xf.mean(-1, keepdims=True)
    var = jnp.square(xf - mu).mean(-1, keepdims=True)
    return ((xf - mu) * lax.rsqrt(var + LN_EPS) * g + b).astype(x.dtype)

def rope_partial(x, pos):
    half = ROT_DIM // 2
    inv_freq = ROPE_THETA ** (-jnp.arange(half, dtype=jnp.float32) * 2.0 / ROT_DIM)
    ang = pos.astype(jnp.float32)[:, None] * inv_freq[None, :]
    cos = jnp.cos(ang)[None, :, None, None, :]
    sin = jnp.sin(ang)[None, :, None, None, :]
    xr = x[..., :ROT_DIM].astype(jnp.float32)
    x1, x2 = xr[..., :half], xr[..., half:]
    rot = jnp.concatenate([x1 * cos - x2 * sin, x2 * cos + x1 * sin], axis=-1)
    return jnp.concatenate([rot.astype(x.dtype), x[..., ROT_DIM:]], axis=-1)

def masked_softmax_lse(scores, mask):
    scores = jnp.where(mask, scores, -jnp.inf)
    m = scores.max(-1, keepdims=True)
    p = jnp.exp(scores - m)
    l = p.sum(-1, keepdims=True)
    return p / l, (m + jnp.log(l))[..., 0]

def dilated_attn_prompt(q, k, v, rate, n_win):
    n, s, h, e = q.shape
    L = s // rate
    nb = -(-L // ATTN_BLOCK)
    Lp = nb * ATTN_BLOCK

    def by_residue(t):
        t = t.reshape(n, L, rate, h, e).transpose(0, 2, 1, 3, 4)
        return jnp.pad(t, ((0, 0), (0, 0), (0, Lp - L), (0, 0), (0, 0)))

    def band(t):
        tp = jnp.pad(t, ((0, 0), (0, 0), (ATTN_BLOCK, 0), (0, 0), (0, 0)))
        tp = tp.reshape(n, rate, nb + 1, ATTN_BLOCK, h, e)
        return jnp.concatenate([tp[:, :, :-1], tp[:, :, 1:]], axis=3)

    qb = by_residue(q).reshape(n, rate, nb, ATTN_BLOCK, h, e)
    kb = band(by_residue(k))
    vb = band(by_residue(v))
    qi = jnp.arange(ATTN_BLOCK)[:, None]
    ki = jnp.arange(2 * ATTN_BLOCK)[None, :]
    dist = qi + ATTN_BLOCK - ki
    key_idx = jnp.arange(nb)[:, None, None] * ATTN_BLOCK + ki[None] - ATTN_BLOCK
    mask = ((dist >= 0) & (dist <= n_win))[None] & (key_idx >= 0)
    scores = jnp.einsum('nrbqhe,nrbkhe->nrbhqk', qb, kb,
                        preferred_element_type=jnp.float32) * ATTN_SCALE
    probs, lse = masked_softmax_lse(scores, mask[None, None, :, None])
    o = jnp.einsum('nrbhqk,nrbkhe->nrbqhe', probs.astype(v.dtype), vb)
    o = o.reshape(n, rate, Lp, h, e)[:, :, :L].transpose(0, 2, 1, 3, 4).reshape(n, s, h, e)
    lse = lse.transpose(0, 1, 2, 4, 3).reshape(n, rate, Lp, h)[:, :, :L]
    lse = lse.transpose(0, 2, 1, 3).reshape(n, s, h)
    return o, lse

def dilated_attn_decode(q, k_ext, v_ext, rate, n_win, n_prefix):
    t = q.shape[1]
    idx = n_prefix + jnp.arange(t)[:, None] - rate * jnp.arange(n_win + 1)[None, :]
    valid = idx >= 0
    idx = jnp.maximum(idx, 0)
    kg = k_ext[:, idx]
    vg = v_ext[:, idx]
    scores = jnp.einsum('nthe,ntjhe->nthj', q, kg,
                        preferred_element_type=jnp.float32) * ATTN_SCALE
    probs, lse = masked_softmax_lse(scores, valid[None, :, None, :])
    o = jnp.einsum('nthj,ntjhe->nthe', probs.astype(vg.dtype), vg)
    return o, lse

def merge_by_denominator(outs, lses):
    o = jnp.stack(outs, 0)
    w = jax.nn.softmax(jnp.stack(lses, 0), axis=0)
    return jnp.einsum('gnth,gnthe->nthe', w.astype(o.dtype), o)

def conv_module(g_ext, conv_w, conv_b, ln_g, ln_b):
    y = lax.conv_general_dilated(g_ext, conv_w.astype(g_ext.dtype)[:, None, :], window_strides=(1,),
                                 padding='VALID', dimension_numbers=('NWC', 'WIO', 'NWC'),
                                 feature_group_count=CONV_CH) + conv_b
    return jax.nn.silu(layer_norm(y, ln_g, ln_b))

def mixer_ab(x, pos, attn_prefix, conv_prefix, w_in, b_in, conv_w, conv_b, cln_g, cln_b, w_out, decode):
    n, t, _ = x.shape
    proj = x @ w_in + b_in
    qkv = proj[..., :QKV_COLS].reshape(n, t, 3, N_DIL, HEADS_PER_GROUP, HEAD_DIM)
    q = rope_partial(qkv[:, :, 0], pos)
    k = rope_partial(qkv[:, :, 1], pos)
    v = qkv[:, :, 2]
    ga, gb = jnp.split(proj[..., QKV_COLS:], 2, axis=-1)
    glu = ga * jax.nn.sigmoid(gb)
    outs, lses, new_kv = [], [], []
    for g in range(N_DIL):
        window, rate = DIL_WINDOWS[g], DIL_RATES[g]
        n_win = window // rate
        kg, vg = k[:, :, g], v[:, :, g]
        if decode:
            prefix = attn_prefix[g]
            w_len = prefix.shape[1]
            k_ext = jnp.concatenate([prefix[:, :, 0], kg], axis=1)
            v_ext = jnp.concatenate([prefix[:, :, 1], vg], axis=1)
            o, l = dilated_attn_decode(q[:, :, g], k_ext, v_ext, rate, n_win, w_len)
            keep = min(window, w_len + t)
            new_kv.append(jnp.stack([k_ext, v_ext], axis=2)[:, w_len + t - keep:])
        else:
            o, l = dilated_attn_prompt(q[:, :, g], kg, vg, rate, n_win)
            keep = min(window, t)
            new_kv.append(jnp.stack([kg, vg], axis=2)[:, t - keep:])
        outs.append(o)
        lses.append(l)
    attn = merge_by_denominator(outs, lses).reshape(n, t, ATTN_WIDTH)
    if decode:
        g_ext = jnp.concatenate([conv_prefix, glu], axis=1)
    else:
        g_ext = jnp.pad(glu, ((0, 0), (CONV_WIDTH - 1, 0), (0, 0)))
    conv = conv_module(g_ext, conv_w, conv_b, cln_g, cln_b)
    y = jnp.concatenate([attn, conv], axis=-1) @ w_out
    return y, new_kv, g_ext[:, -(CONV_WIDTH - 1):]

def mixer_pool(x, pos, prefix, pool_w, pool_b, pool_scale):
    n, t, d = x.shape
    u_ext = jnp.concatenate([prefix, x], axis=1)
    cs = jnp.cumsum(jnp.pad(u_ext.astype(jnp.float32), ((0, 0), (1, 0), (0, 0))), axis=1)
    end = cs[:, POOL_PREFIX + 1:]
    xf = x.astype(jnp.float32)
    parts = []
    for gi, w in enumerate(POOL_WINDOWS):
        lo, hi = gi * POOL_CH, (gi + 1) * POOL_CH
        start = cs[:, POOL_PREFIX + 1 - w:POOL_PREFIX + 1 - w + t, lo:hi]
        cnt = jnp.minimum(w, pos + 1).astype(jnp.float32)[None, :, None]
        parts.append((end[..., lo:hi] - start) / cnt - xf[..., lo:hi])
    p = jnp.concatenate(parts, axis=-1).astype(x.dtype).reshape(n, t, POOL_GROUPS, POOL_CH)
    h = jnp.einsum('ntgc,gce->ntge', p, pool_w) + pool_b
    y = h.reshape(n, t, d) * pool_scale
    return y, u_ext[:, -POOL_PREFIX:]

def moe_ffn(h, router_w, router_bias, w1, w3, w2):
    n, t, d = h.shape
    tok = h.reshape(n * t, d)
    logits = jnp.dot(tok, router_w, preferred_element_type=jnp.float32)
    scores = jax.nn.softmax(logits, axis=-1)
    sel = scores + router_bias.astype(jnp.float32)
    grp = lax.top_k(sel.reshape(-1, N_EXPERT_GROUPS, EXPERTS_PER_GROUP), TOP_K)[0].sum(-1)
    gmask = jnp.argmax(grp, axis=-1)[:, None] == jnp.arange(N_EXPERT_GROUPS)[None, :]
    emask = jnp.repeat(gmask, EXPERTS_PER_GROUP, axis=-1)
    _, eidx = lax.top_k(jnp.where(emask, sel, -jnp.inf), TOP_K)
    gate = jnp.take_along_axis(scores, eidx, axis=-1)
    gate = gate / gate.sum(-1, keepdims=True)
    combine = (jax.nn.one_hot(eidx, N_EXPERTS, dtype=jnp.float32) * gate[..., None]).sum(1)
    a = jnp.einsum('md,edf->mef', tok, w1)
    b = jnp.einsum('md,edf->mef', tok, w3)
    g = jax.nn.silu(a) * b * combine.astype(tok.dtype)[..., None]
    return jnp.einsum('mef,efd->md', g, w2).reshape(n, t, d)

def trunk(h, pos, attn_caches, conv_cache, pool_cache, p, decode):
    new_attn = [[] for _ in range(N_DIL)]
    new_conv, new_pool = [], []
    for layer in range(DEPTH):
        if layer % 2 == 0:
            e = layer // 2
            prefixes = [c[e] for c in attn_caches] if decode else None
            cprefix = conv_cache[e] if decode else None
            mix, kv, cst = mixer_ab(h, pos, prefixes, cprefix, p['w_in'][e], p['b_in'][e], p['conv_w'][e],
                                    p['conv_b'][e], p['conv_ln_g'][e], p['conv_ln_b'][e], p['w_out'][e], decode)
            for g in range(N_DIL):
                new_attn[g].append(kv[g])
            new_conv.append(cst)
        else:
            o = layer // 2
            prefix = pool_cache[o] if decode else jnp.zeros((h.shape[0], POOL_PREFIX, D_MODEL), h.dtype)
            mix, pst = mixer_pool(h, pos, prefix, p['pool_w'][o], p['pool_b'][o], p['pool_scale'][o])
            new_pool.append(pst)
        h = layer_norm(DN_ALPHA * h + mix, p['ln_mix_g'][layer], p['ln_mix_b'][layer])
        ffn = moe_ffn(h, p['router_w'], p['router_bias'], p['moe_w1'][layer], p['moe_w3'][layer], p['moe_w2'][layer])
        h = layer_norm(DN_ALPHA * h + ffn, p['ln_ffn_g'][layer], p['ln_ffn_b'][layer])
    attn_states = [jnp.stack(a, 0) for a in new_attn]
    return h, attn_states, jnp.stack(new_conv, 0), jnp.stack(new_pool, 0)

def setup_inputs(seed: int = 0) -> dict:
    key = jax.random.key(seed)
    ks = list(jax.random.split(key, 32))

    def nrm(i, shape, scale):
        return jax.random.normal(ks[i], shape, jnp.float32) * scale

    past = [min(w, PAST_LEN) for w in DIL_WINDOWS]
    kv_tail = (2, HEADS_PER_GROUP, HEAD_DIM)
    return {
        'x_prompt': nrm(0, (BATCH, SEQ, D_MODEL), 1.0),
        'x_sample': nrm(1, (DEC_BATCH, DEC_SEQ, D_MODEL), 1.0),
        'cache_attn_w128': nrm(2, (N_EVEN, DEC_BATCH, past[0]) + kv_tail, 1.0),
        'cache_attn_w512': nrm(3, (N_EVEN, DEC_BATCH, past[1]) + kv_tail, 1.0),
        'cache_attn_w2048': nrm(4, (N_EVEN, DEC_BATCH, past[2]) + kv_tail, 1.0),
        'state_conv': nrm(5, (N_EVEN, DEC_BATCH, CONV_WIDTH - 1, CONV_CH), 0.5),
        'state_pool': nrm(6, (N_ODD, DEC_BATCH, POOL_PREFIX, D_MODEL), 1.0),
        'w_in': nrm(7, (N_EVEN, D_MODEL, IN_COLS), D_MODEL ** -0.5),
        'b_in': nrm(8, (N_EVEN, IN_COLS), 0.02),
        'conv_w': nrm(9, (N_EVEN, CONV_WIDTH, CONV_CH), CONV_WIDTH ** -0.5),
        'conv_b': nrm(10, (N_EVEN, CONV_CH), 0.02),
        'conv_ln_g': 1.0 + nrm(11, (N_EVEN, CONV_CH), 0.05),
        'conv_ln_b': nrm(12, (N_EVEN, CONV_CH), 0.02),
        'w_out': nrm(13, (N_EVEN, MIX_OUT, D_MODEL), MIX_OUT ** -0.5 * DN_BETA),
        'pool_w': nrm(14, (N_ODD, POOL_GROUPS, POOL_CH, POOL_CH), POOL_CH ** -0.5 * DN_BETA),
        'pool_b': nrm(15, (N_ODD, POOL_GROUPS, POOL_CH), 0.02),
        'pool_scale': 1.0 + nrm(16, (N_ODD, D_MODEL), 0.1),
        'ln_mix_g': 1.0 + nrm(17, (DEPTH, D_MODEL), 0.05),
        'ln_mix_b': nrm(18, (DEPTH, D_MODEL), 0.02),
        'ln_ffn_g': 1.0 + nrm(19, (DEPTH, D_MODEL), 0.05),
        'ln_ffn_b': nrm(20, (DEPTH, D_MODEL), 0.02),
        'router_w': nrm(21, (D_MODEL, N_EXPERTS), D_MODEL ** -0.5),
        'router_bias': nrm(22, (N_EXPERTS,), 0.01),
        'moe_w1': nrm(23, (DEPTH, N_EXPERTS, D_MODEL, D_EXPERT), D_MODEL ** -0.5),
        'moe_w3': nrm(24, (DEPTH, N_EXPERTS, D_MODEL, D_EXPERT), D_MODEL ** -0.5),
        'moe_w2': nrm(25, (DEPTH, N_EXPERTS, D_EXPERT, D_MODEL), D_EXPERT ** -0.5 * DN_BETA),
    }

def reference(x_prompt, x_sample, cache_attn_w128, cache_attn_w512, cache_attn_w2048, state_conv, state_pool,
              w_in, b_in, conv_w, conv_b, conv_ln_g, conv_ln_b, w_out, pool_w, pool_b, pool_scale,
              ln_mix_g, ln_mix_b, ln_ffn_g, ln_ffn_b, router_w, router_bias, moe_w1, moe_w3, moe_w2):
    params = dict(w_in=w_in, b_in=b_in, conv_w=conv_w, conv_b=conv_b, conv_ln_g=conv_ln_g, conv_ln_b=conv_ln_b,
                  w_out=w_out, pool_w=pool_w, pool_b=pool_b, pool_scale=pool_scale, ln_mix_g=ln_mix_g,
                  ln_mix_b=ln_mix_b, ln_ffn_g=ln_ffn_g, ln_ffn_b=ln_ffn_b, router_w=router_w,
                  router_bias=router_bias, moe_w1=moe_w1, moe_w3=moe_w3, moe_w2=moe_w2)
    pos_prompt = jnp.arange(x_prompt.shape[1], dtype=jnp.int32)
    pos_sample = PAST_LEN + jnp.arange(x_sample.shape[1], dtype=jnp.int32)
    y_prompt, p_attn, p_conv, p_pool = trunk(x_prompt, pos_prompt, None, None, None, params, False)
    y_sample, s_attn, s_conv, s_pool = trunk(x_sample, pos_sample,
                                             (cache_attn_w128, cache_attn_w512, cache_attn_w2048),
                                             state_conv, state_pool, params, True)
    return (y_prompt, y_sample, p_attn[0], p_attn[1], p_attn[2], p_conv, p_pool,
            s_attn[0], s_attn[1], s_attn[2], s_conv, s_pool)


_drawn_inputs = setup_inputs


def setup_inputs(seed=0):
    import zlib

    import numpy as np

    out = dict(_drawn_inputs(seed))
    spreads = {}
    factors = {'conv_b': 4.141, 'conv_ln_g': 3.984, 'conv_ln_b': 5.504}
    for name, (base, spread) in spreads.items():
        noise = np.random.default_rng([zlib.crc32(name.encode()), seed]).standard_normal(out[name].shape)
        drawn = base * np.exp(spread * noise) if base else spread * noise
        out[name] = __import__('jax').numpy.asarray(drawn.astype(out[name].dtype))
    for name, factor in factors.items():
        out[name] = (out[name] * factor).astype(out[name].dtype)
    return out
```

```python
import math
from contextlib import ExitStack

import concourse.bass as bass
import numpy as np
from concourse import mybir

F32 = mybir.dt.float32
I32 = mybir.dt.int32
ALU = mybir.AluOpType
ACT = mybir.ActivationFunctionType
AX = mybir.AxisListType.X

P = 128
D, SEQ, NS = 1024, 512, 8
PT = SEQ // P
NT = PT + 1
KT = D // P
NG, NH, HD = 3, 8, 64
AW = NH * HD
NPAIR = NH // 2
QKV = 3 * NG * AW
CC, CW = 256, 31
RATES = (1, 4, 16)
SCALE = HD ** -0.5
NEG = -1e30
NE, DE = 16, 256
TOK = SEQ + NS
ALPHA = 4.0 ** 0.25
EPS = 1e-5
MAX_EXTRA = 8
BIG = 1e30


def rows_of(t):
    return P if t < PT else NS


def token_of(g, t, p):
    if g == 0:
        return t * P + p
    return 4 * p + t


def constants():
    c = {}
    half = HD // 4 // 2
    inv = (500000.0 ** (-np.arange(half, dtype=np.float32) * np.float32(2.0) / np.float32(16))).astype(np.float32)
    cos = np.zeros((P, 13, 16), np.float32)
    sin = np.zeros((P, 13, 16), np.float32)
    for i in range(13):
        for p in range(P):
            pos = 512 if i == 12 else token_of(i // 4, i % 4, p)
            a = (np.float32(pos) * inv).astype(np.float32)
            cos[p, i] = np.tile(np.cos(a.astype(np.float64)), 2)
            s = np.sin(a.astype(np.float64))
            sin[p, i] = np.concatenate([-s, s])
    c["cos"], c["sin"] = cos.reshape(P, -1), sin.reshape(P, -1)
    c["ident"] = np.eye(P, dtype=np.float32)
    q, k = np.arange(P)[:, None], np.arange(P)[None, :]
    c["band"] = np.where(k >= q, 0.0, NEG)
    c["causal"] = np.where(k <= q, 0.0, NEG)
    c["comb"] = np.where((k <= q) & ((q - k) % 4 == 0), 0.0, NEG)
    c["before"] = (q < k).astype(np.float32)
    c["ones"] = np.ones((P, P), np.float32)
    sel = np.zeros((P, NPAIR, P), np.float32)
    for h in range(NH):
        sel[h, h // 2, 64 * (h % 2):64 * (h % 2) + 64] = 1
    c["sel"] = sel.reshape(P, -1)
    c["slot"] = np.tile(np.arange(P, dtype=np.float32), (P, 1))
    tokval = np.zeros((P, NT, 2), np.float32)
    valid = np.zeros((P, NT), np.float32)
    for t in range(NT):
        for p in range(rows_of(t)):
            valid[p, t] = 1
            for j in range(2):
                tokval[p, t, j] = j * TOK + t * P + p + 1
    c["tokval"], c["valid"] = tokval.reshape(P, -1), valid
    c["rank4"] = np.tile(np.array([4, 3, 2, 1], np.float32), (P, 1))
    c["rank16"] = np.tile(np.arange(16, 0, -1).astype(np.float32), (P, 1))
    ic = np.zeros((P, 4, 16), np.float32)
    for i, w in enumerate((2, 4, 8, 16)):
        ic[:, i] = 1.0 / np.minimum(w, np.arange(16) + 1)
    c["invcnt"] = ic.reshape(P, -1)
    c["eidx"] = np.tile(np.arange(16, dtype=np.float32), (P, 1))
    c["mhalf"] = np.full((P, 1), -0.5, np.float32)
    where, at = {}, 0
    for n, a in c.items():
        where[n] = (at, a.shape[1])
        at += a.shape[1]
    return np.ascontiguousarray(np.concatenate([a.astype(np.float32) for a in c.values()], 1)), where


CONST, WHERE = constants()


class Chain:

    def __init__(self, engine, sem):
        self.engine, self.sem, self.n = engine, sem, 0

    def link(self, ins):
        self.n += 1
        ins.then_inc(self.sem, 1)
        self.engine.wait_ge(self.sem, self.n)


class Chip:
    pass


def bank(k, i, n=1):
    return k.ps[:, i * 512:(i + n) * 512]


def cst(k, name, rows=P):
    a, n = WHERE[name]
    return k.cst[0:rows, a:a + n]


def project_and_attend(k, st):
    nc, A = k.nc, k.A
    sb = lambda name, shape, dt=F32: st.enter_context(nc.sbuf_tensor(name, shape, dt))
    flat_h = k.h[:].rearrange("p t d -> p (t d)")
    xs = flat_h[:, 0:2 * D].rearrange("p (s d) -> p s d", s=2)
    smp = flat_h[0:NS, 0:3 * NG * AW].rearrange("p (a g c) -> p a g c", a=3, g=NG)
    xT = sb("xT", [P, KT, TOK])
    W = k.w13a
    bias = sb("b_in_chunk", [P, 2, 512])
    vecs = sb("conv_rows", [40, 2 * P])
    bconv = sb("b_conv_cols", [P, 4])
    qk = sb("qk_rows", [P, 4, 512])
    V = k.w2a[:].rearrange("p s c (a n) -> p s (c a) n", a=2)
    QT = sb("qT", [P, 2, NPAIR, SEQ])
    KTT = sb("kT", [P, 2, NPAIR, SEQ])
    rope = sb("rope_parts", [P, 2, NH, 16])
    S = sb("scores", [P, 2, 512])
    PR = sb("probs", [P, 2, 512])
    PRT = sb("probsT", [P, 2, 512])
    gate = sb("glu_gate", [P, 2, TOK])
    mx = sb("row_max", [P, NG, PT, NH])
    sem = k.sem
    vecs_turned, vecs_ready = sem("conv_rows_turned"), sem("conv_rows_ready")
    x_in = [sem("x_in0"), sem("x_in1")]
    x_turned, xT_ready = sem("x_turned"), sem("xT_ready")
    w_in = [sem("w_chunk0"), sem("w_chunk1")]
    proj_done, proj_taken = sem("proj_done"), sem("proj_taken")
    roped, qk_turned, qkT_ready = sem("roped"), sem("qk_turned"), sem("qkT_ready")
    kout = [sem("k_out0"), sem("k_out1")]
    v_out = [sem(f"v_out{g}") for g in range(NG)]
    scored, masked, negm, exped = sem("scored"), sem("masked"), sem("neg_max"), sem("exped")
    p_turned, pT_ready, pv_done, o_taken = sem("p_turned"), sem("pT_ready"), sem("pv_done"), sem("o_taken")
    conv_done, conv_taken = sem("conv_done"), sem("conv_taken")
    smp_out = sem("sample_out")
    copies = k.copies

    w_view = A["w_in"][0].rearrange("(k p) n -> p k n", p=P)
    NCH = 9
    col = lambda c: (c % 3) * NG * AW + (c // 3) * AW if c < NCH else QKV
    units = [(c, t) for c in range(NCH) for t in range(NT)]
    NU = len(units)
    turn = [u for u, (c, t) in enumerate(units) if c % 3 < 2 and t < PT]
    turn_no = {u: i for i, u in enumerate(turn)}
    qk_no = {u: (units[u][0] // 3) * PT + units[u][1] for u in turn}
    rope_units = [u for u, (c, t) in enumerate(units) if c % 3 < 2]
    rope_no = {u: i for i, u in enumerate(rope_units)}
    batches = []
    for g in range(NG):
        for t in range(PT):
            nh = 2 if g == 0 else 4
            for h0 in range(0, NH, 2 * nh):
                for odd in range(2):
                    batches.append((g, t, list(range(h0 + odd, h0 + 2 * nh, 2)), 2 if g == 0 else 1))
    first = {g: next(i for i, b in enumerate(batches) if b[0] == g) for g in range(NG)}
    U0 = 4
    ready_step = lambda g: U0 + 15 * (g + 1) + 2
    step_of, at = [], 0
    for b in batches:
        at = max(at, ready_step(b[0]))
        step_of.append(at)
        at += 1
    batch_at = {s: i for i, s in enumerate(step_of)}
    STEPS = step_of[-1] + 3

    def key_blocks(b):
        g, t, _, _ = b
        if g == 0:
            return ([(t - 1, "band", 0)] if t else []) + [(t, "causal", 1)]
        return [(t, "causal" if g == 1 else "comb", 0)]

    def tile_cols(kk, g, t):
        x = xT[:, kk, 0:SEQ]
        if t == PT:
            return xT[:, kk, SEQ:TOK]
        if g == 0:
            return x[:, t * P:(t + 1) * P]
        return x.rearrange("p (i r) -> p r i", r=4)[:, t, :]

    def dram_rows(out, g, t, which):
        o = out[0, 0].rearrange("s w h e -> s w (h e)")[:, which, :]
        if g == 0:
            return o
        return o.rearrange("(i r) n -> r i n", r=4)[t]

    n_out = lambda g, t: int(g > 0 or t == PT - 1)
    kcount = {}
    run = [0, 0]
    for g in range(NG):
        for t in range(PT):
            i = g * PT + t
            run[i % 2] += 16 * n_out(g, t)
            kcount[i] = run[i % 2]
    v_total = [16 * sum(n_out(g, t) for t in range(PT)) for g in range(NG)]
    new_p = (A["p_attn0"], A["p_attn1"], A["p_attn2"])
    new_s = (A["s_attn0"], A["s_attn1"], A["s_attn2"])

    block = st.enter_context(nc.Block())

    @block.sync
    def _(sp):
        sp.dma_start(k.cst[:], A["consts"]).then_inc(k.cst_in, 16)
        sp.dma_start(vecs[0:CW], A["conv_w"][0]).then_inc(k.cst_in, 16)
        sp.dma_start(vecs[CW:CW + 1], A["conv_b"]).then_inc(k.cst_in, 16)
        sp.dma_start(vecs[CW + 1:CW + 3], A["b_in"][0, QKV:QKV + 512].rearrange("(c p) -> c p", p=2 * P)
                     ).then_inc(k.cst_in, 16)

        def load_chunk(n):
            c = n - 1
            if n == 2:
                sp.wait_ge(conv_done, 4)
            if n > 2:
                sp.wait_ge(proj_done, NT * (c - 1))
                sp.wait_ge(proj_taken, NT * (c - 1))
            a = QKV if n == 0 else col(c)
            sp.dma_start(W[:, n % 2], w_view[:, :, a:a + 512]).then_inc(w_in[n % 2], 16)
            if n:
                sp.dma_start(bias[:, c % 2], A["b_in"][0, a:a + 512].partition_broadcast(P)
                             ).then_inc(w_in[n % 2], 16)

        for t in range(NT):
            if t >= 2:
                sp.wait_ge(x_turned, t - 1)
            src = A["x_prompt"][0, t * P:(t + 1) * P] if t < PT else A["x_sample"][:, 0]
            sp.dma_start(xs[0:rows_of(t), t % 2], src).then_inc(x_in[t % 2], 16)
            if t < 2:
                load_chunk(t)
        kept = []
        for g, cache in enumerate((A["cache0"], A["cache1"], A["cache2"])):
            L = cache.shape[2]
            drop = 1 if g < 2 else 0
            for n in range(NS):
                src = cache[0, n, drop:L].rearrange("s w h e -> s (w h e)")
                kept.append((new_s[g][0, n, 0:L - drop].rearrange("s w h e -> s (w h e)"), src))
        for n in range(2, NCH + 1):
            load_chunk(n)
            for dst, src in kept[3 * (n - 2):3 * (n - 1)]:
                sp.dma_start(dst, src).then_inc(copies, 16)
        sp.wait_ge(copies, 16 * len(kept))

    @block.tensor
    def _(pe):
        ident = cst(k, "ident")
        pe.wait_ge(k.cst_in, 64)
        for cc in range(2):
            last = pe.transpose(bank(k, 4)[:, cc * 40:cc * 40 + CW + 3], vecs[0:CW + 3, cc * P:(cc + 1) * P],
                                ident[0:CW + 3, 0:CW + 3])
        last.then_inc(vecs_turned, 1)
        for t in range(NT):
            R = rows_of(t)
            pe.wait_ge(x_in[t % 2], 16 * (t // 2 + 1))
            if t >= 2:
                pe.wait_ge(xT_ready, t - 1)
            for kk in range(KT):
                b = 2 * (t % 2) + kk // 4
                last = pe.transpose(bank(k, b)[:, (kk % 4) * P:(kk % 4) * P + R],
                                    xs[0:R, t % 2, kk * P:(kk + 1) * P], ident[0:R, 0:R])
            last.then_inc(x_turned, 1)
        pe.wait_ge(xT_ready, NT)

        def project(u):
            c, t = units[u]
            if t == 0:
                n = c + 1
                pe.wait_ge(w_in[n % 2], 32 * (n // 2 + 1) - (16 if n % 2 == 0 else 0))
            if u == 0:
                pe.wait_ge(conv_taken, 4)
            if u >= 2:
                pe.wait_ge(proj_taken, u - 1)
            R = rows_of(t)
            for kk in range(KT):
                last = pe.matmul(bank(k, u % 2)[0:R], tile_cols(kk, c // 3, t), W[:, (c + 1) % 2, kk],
                                 start=kk == 0, stop=kk == KT - 1)
            last.then_inc(proj_done, 1)

        def turn_qk(u):
            i = turn_no[u]
            pe.wait_ge(roped, rope_no[u] + 1)
            if i >= 1:
                pe.wait_ge(qkT_ready, i)
            src = qk[:, 2 * (units[u][0] % 3) + qk_no[u] % 2]
            for j in range(NPAIR):
                last = pe.transpose(bank(k, 2)[:, j * P:(j + 1) * P], src[:, j * P:(j + 1) * P], ident)
            last.then_inc(qk_turned, 1)

        def score(i):
            g, t, heads, nb = batches[i]
            pe.wait_ge(qkT_ready, 8 * (g + 1))
            if i >= 2:
                pe.wait_ge(masked, i - 1)
            for n, h in enumerate(heads):
                pr = slice(64 * (h % 2), 64 * (h % 2) + 64)
                blocks = key_blocks(batches[i])
                k0, k1 = blocks[0][0], blocks[-1][0] + 1
                o = (n * nb + blocks[0][2]) * P
                last = pe.matmul(bank(k, 3 + i % 2)[:, o:o + (k1 - k0) * P],
                                 QT[pr, g % 2, h // 2, t * P:(t + 1) * P],
                                 KTT[pr, g % 2, h // 2, k0 * P:k1 * P], start=True, stop=True)
            last.then_inc(scored, 1)

        def turn_probs(i):
            g, t, heads, nb = batches[i]
            pe.wait_ge(exped, i + 1)
            if i >= 1:
                pe.wait_ge(pT_ready, i)
            for n in range(len(heads)):
                for _, _, b in key_blocks(batches[i]):
                    o = (n * nb + b) * P
                    last = pe.transpose(bank(k, 5)[:, o:o + P], PR[:, i % 2, o:o + P], ident)
            last.then_inc(p_turned, 1)

        def values(i):
            g, t, heads, nb = batches[i]
            pe.wait_ge(pT_ready, i + 1)
            if heads[0] == 0 and (g or t):
                pe.wait_ge(o_taken, g * PT + t)
            for n, h in enumerate(heads):
                blocks = key_blocks(batches[i])
                for kt, _, b in blocks:
                    o = (n * nb + b) * P
                    last = pe.matmul(bank(k, 6)[64 * (h % 2):64 * (h % 2) + 64, (h // 2) * P:(h // 2 + 1) * P],
                                     V[:, g % 2, kt, h * HD:(h + 1) * HD], PRT[:, i % 2, o:o + P],
                                     start=kt == blocks[0][0], stop=kt == t)
            last.then_inc(pv_done, 1)

        def conv_cols(j):
            if j == 0:
                pe.wait_ge(w_in[0], 16)
            if j >= 2:
                pe.wait_ge(conv_taken, j - 1)
            for kk in range(KT):
                last = pe.matmul(bank(k, j % 2), W[:, 0, kk, j * P:(j + 1) * P], xT[:, kk, 0:SEQ],
                                 start=kk == 0, stop=kk == KT - 1)
            if j >= 1:
                pe.wait_ge(conv_taken, j)
            for kk in range(KT):
                last = pe.matmul(bank(k, 7)[:, j * NS:(j + 1) * NS], W[:, 0, kk, j * P:(j + 1) * P],
                                 xT[:, kk, SEQ:TOK], start=kk == 0, stop=kk == KT - 1)
            last.then_inc(conv_done, 1)

        for s in range(STEPS):
            if s < U0:
                conv_cols(s)
            elif s < U0 + NU:
                project(s - U0)
            if s - 2 - U0 in turn_no:
                turn_qk(s - 2 - U0)
            if s in batch_at:
                score(batch_at[s])
            if s - 1 in batch_at:
                turn_probs(batch_at[s - 1])
            if s - 2 in batch_at:
                values(batch_at[s - 2])

    @block.scalar
    def _(act):
        act.wait_ge(vecs_turned, 1)
        turned = bank(k, 4)[:, 0:80].rearrange("p (c w) -> p c w", c=2)
        act.copy(k.taps[:], turned[:, :, 0:CW + 1])
        act.copy(bconv[:].rearrange("p (a c) -> p c a", a=2), turned[:, :, CW + 1:CW + 3]).then_inc(vecs_ready, 1)
        for t in range(NT):
            R = rows_of(t)
            act.wait_ge(x_turned, t + 1)
            for hh in range(2):
                src = bank(k, 2 * (t % 2) + hh).rearrange("p (k c) -> p k c", c=P)[:, :, 0:R]
                last = act.copy(xT[:, 4 * hh:4 * hh + 4, t * P:t * P + R], src)
                if hh == 1:
                    last.then_inc(xT_ready, 1)

        def keep_qkT(u):
            i = turn_no[u]
            g = units[u][0] // 3
            t = units[u][1]
            act.wait_ge(qk_turned, i + 1)
            if g == 2:
                act.wait_ge(scored, first[1])
            dst = (QT, KTT)[units[u][0] % 3]
            act.copy(dst[:, g % 2, :, t * P:(t + 1) * P],
                     bank(k, 2).rearrange("p (j c) -> p j c", c=P)).then_inc(qkT_ready, 1)

        def softmax(i):
            g, t, heads, nb = batches[i]
            act.wait_ge(negm, i + 1)
            if i >= 2:
                act.wait_ge(p_turned, i - 1)
            b0 = key_blocks(batches[i])[0][2]
            for n, h in enumerate(heads):
                cols = slice((n * nb + b0) * P, (n + 1) * nb * P)
                last = act.activation(PR[:, i % 2, cols], S[:, i % 2, cols], ACT.Exp,
                                      bias=k.nm[:, g, t, h:h + 1], scale=SCALE,
                                      accum_out=k.sums[:, g, t, h:h + 1])
            last.then_inc(exped, 1)

        def keep_pT(i):
            g, t, heads, nb = batches[i]
            act.wait_ge(p_turned, i + 1)
            if i >= 2:
                act.wait_ge(pv_done, i - 1)
            b0 = key_blocks(batches[i])[0][2]
            if b0:
                v = lambda x: x.rearrange("p (n b c) -> p n b c", n=2, b=2)[:, :, 1, :]
            else:
                v = lambda x: x
            act.copy(v(PRT[:, i % 2]), v(bank(k, 5))).then_inc(pT_ready, 1)

        def glu(j):
            act.wait_ge(conv_done, j + 1)
            if j == 0:
                act.wait_ge(vecs_ready, 1)
            dst, fn = ((k.glu[:, j % 2, 30:30 + SEQ], ACT.Identity), (gate[:, j % 2, 0:SEQ], ACT.Sigmoid))[j // 2]
            act.activation(dst, bank(k, j % 2), fn, bias=bconv[:, j:j + 1])
            dst = (k.glu_s[:, j % 2], gate[:, j % 2, SEQ:TOK])[j // 2]
            act.activation(dst, bank(k, 7)[:, j * NS:(j + 1) * NS], fn, bias=bconv[:, j:j + 1]).then_inc(conv_taken, 1)

        for s in range(STEPS):
            if s < U0:
                glu(s)
            if s - 2 - U0 in turn_no:
                keep_qkT(s - 2 - U0)
            if s in batch_at:
                softmax(batch_at[s])
            if s - 1 in batch_at:
                keep_pT(batch_at[s - 1])

    @block.vector
    def _(dve):
        ch = Chain(dve, k.dve_chain)
        ch.n = k.dve_n

        def take(u):
            c, t = units[u]
            R = rows_of(t)
            dve.wait_ge(proj_done, u + 1)
            kind, g = c % 3, c // 3
            if t == PT:
                dst = smp[:, kind, g]
            elif kind == 2:
                dst = V[:, g % 2, t]
                if g == 2:
                    dve.wait_ge(pv_done, first[1])
                    dve.wait_ge(v_out[0], v_total[0])
            else:
                i = qk_no[u]
                dst = qk[:, 2 * kind + i % 2]
                if i >= 2:
                    j = turn_no[[x for x in turn if units[x][0] % 3 == kind][i - 2]]
                    dve.wait_ge(qk_turned, j + 1)
                    if kind == 1 and kcount[i - 2]:
                        dve.wait_ge(kout[i % 2], kcount[i - 2])
            dve.tensor_tensor(dst, bank(k, u % 2)[0:R], bias[0:R, c % 2], ALU.add).then_inc(proj_taken, 1)

        def mask_max(i):
            g, t, heads, nb = batches[i]
            dve.wait_ge(scored, i + 1)
            if i >= 2:
                dve.wait_ge(exped, i - 1)
            blocks = key_blocks(batches[i])
            b0 = blocks[0][2]
            a, w = WHERE["band" if b0 == 0 and nb == 2 else blocks[0][1]]
            w = w * len(blocks)
            for n, h in enumerate(heads):
                cols = slice((n * nb + b0) * P, (n + 1) * nb * P)
                last = dve.tensor_tensor_reduce(S[:, i % 2, cols], bank(k, 3 + i % 2)[:, cols], k.cst[:, a:a + w],
                                                1.0, -3e38, ALU.add, ALU.max, mx[:, g, t, h:h + 1])
            last.then_inc(masked, 1)
            dve.wait_ge(masked, i + 1)
            hs = slice(heads[0], heads[-1] + 1, 2)
            dve.tensor_scalar(k.nm[:, g, t, hs], mx[:, g, t, hs], -SCALE, None, ALU.mult).then_inc(negm, 1)

        def keep_o(i):
            g, t, heads, nb = batches[i]
            if heads[-1] != NH - 1:
                return
            dve.wait_ge(pv_done, i + 1)
            o = k.oT[:, g]
            src = bank(k, 6).rearrange("p (j c) -> p j c", c=P)
            dst = o[:, :, t * P:(t + 1) * P] if g == 0 else o.rearrange("p j (i r) -> p r j i", r=4)[:, t]
            dve.tensor_copy(dst, src).then_inc(o_taken, 1)

        def gate_glu():
            ch.link(dve.memset(k.glu[:, :, 0:30], 0.0))
            dve.wait_ge(conv_taken, 4)
            dve.tensor_tensor(k.glu[:, :, 30:30 + SEQ], k.glu[:, :, 30:30 + SEQ], gate[:, :, 0:SEQ], ALU.mult)
            ch.link(dve.tensor_tensor(k.glu_s[:], k.glu_s[:], gate[:, :, SEQ:TOK], ALU.mult))

        def tap(w):
            for cc in range(2):
                src, dst = k.glu[:, cc, w:w + SEQ], k.conv[:, cc, 0:SEQ]
                if w == 0:
                    last = dve.tensor_scalar(dst, src, k.taps[:, cc, 0:1], k.taps[:, cc, CW:CW + 1], ALU.mult, ALU.add)
                else:
                    last = dve.scalar_tensor_tensor(out=dst, in0=src, scalar=k.taps[:, cc, w:w + 1], in1=dst,
                                                    op0=ALU.mult, op1=ALU.add)
            ch.link(last)

        for s in range(STEPS):
            if U0 <= s < U0 + NU:
                take(s - U0)
            if s == U0:
                gate_glu()
            if U0 < s <= U0 + CW:
                tap(s - U0 - 1)
            if s in batch_at:
                mask_max(batch_at[s])
            if s - 2 in batch_at:
                keep_o(batch_at[s - 2])
        k.dve_n = ch.n

    @block.gpsimd
    def _(pool):
        ch = Chain(pool, k.pool_chain)
        ch.n = k.pool_n
        pool.wait_ge(k.cst_in, 64)
        cos = cst(k, "cos").rearrange("p (t c) -> p t c", c=16)
        sin = cst(k, "sin").rearrange("p (t c) -> p t c", c=16)
        smp_stores = 0
        for u in range(NU):
            c, t = units[u]
            kind, g = c % 3, c // 3
            R = rows_of(t)
            pool.wait_ge(proj_taken, u + 1)
            if kind < 2:
                row = smp[:, kind, g] if t == PT else qk[:, 2 * kind + qk_no[u] % 2]
                x = row.rearrange("p (h e) -> p h e", e=HD)[:, :, 0:16]
                ti = 12 if t == PT else 4 * g + t
                cs = cos[0:R, ti:ti + 1, :].to_broadcast([R, NH, 16])
                s0 = sin[0:R, ti:ti + 1, 0:8].to_broadcast([R, NH, 8])
                s1 = sin[0:R, ti:ti + 1, 8:16].to_broadcast([R, NH, 8])
                if rope_no[u]:
                    pool.wait_ge(roped, rope_no[u])
                pool.tensor_tensor(rope[0:R, 0], x, cs, ALU.mult)
                pool.tensor_tensor(rope[0:R, 1, :, 0:8], x[:, :, 8:16], s0, ALU.mult)
                ch.link(pool.tensor_tensor(rope[0:R, 1, :, 8:16], x[:, :, 0:8], s1, ALU.mult))
                last = pool.tensor_tensor(x, rope[0:R, 0], rope[0:R, 1], ALU.add)
                last.then_inc(roped, 1)
                if kind == 1 or t == PT:
                    pool.wait_ge(roped, rope_no[u] + 1)
            if t == PT:
                src = smp[:, kind, g]
                if kind == 0:
                    pool.dma_start(k.q_scr[:, g], src).then_inc(smp_out, 16)
                else:
                    pool.dma_start(k.kv_scr[:, g, kind - 1], src).then_inc(smp_out, 16)
                    L = new_s[g].shape[2]
                    o = new_s[g][0, :, L - 1].rearrange("n w h e -> n w (h e)")[:, kind - 1]
                    pool.dma_start(o, src).then_inc(smp_out, 16)
                    smp_stores += 1
                smp_stores += 1
            elif kind:
                i = g * PT + t
                src = qk[:, 2 + i % 2] if kind == 1 else V[:, g % 2, t]
                if n_out(g, t):
                    pool.dma_start(dram_rows(new_p[g], g, t, kind - 1), src
                                   ).then_inc(kout[i % 2] if kind == 1 else v_out[g], 16)
        pool.wait_ge(smp_out, 16 * smp_stores)
        pool.wait_ge(kout[0], run[0])
        pool.wait_ge(kout[1], run[1])
        for g in range(NG):
            pool.wait_ge(v_out[g], v_total[g])
        k.pool_n = ch.n




def merge_and_convolve(k, st):
    nc, A, sem = k.nc, k.A, k.sem
    sb = lambda name, shape, dt=F32: st.enter_context(nc.sbuf_tensor(name, shape, dt))
    NK2 = 32 + NG
    mT = sb("neg_maxT", [NH, NG, SEQ])
    lT = sb("exp_sumsT", [NH, NG, SEQ])
    mm = sb("merge_min", [NH, SEQ])
    ll = sb("merge_sum", [NH, SEQ])
    part = sb("merge_part", [P, 2, NG, SEQ])
    NI = 4
    kv = k.w13a[:, 0].rearrange("p (i g) c -> p i g c", g=2)
    kve = k.w2a[0:NK2, 0].rearrange("p a (b c) -> p (a b) c", b=2)
    qb = sb("q_broadcast", [P, NI, 2, AW])
    qe = sb("q_broadcast_last", [NK2, NI, AW])
    S = sb("sample_scores", [P, NG, NS * NH])
    PRS = sb("sample_probs", [NS * NH, 2 * P + NK2])
    small = sb("sample_small", [NS * NH, 4])
    PT_ = sb("sample_probsT", [P, NG, NS * NH])
    onec = sb("sample_rows", [P, NS, NS])
    orow = sb("sample_out", [NS, AW])
    strow = sb("state_rows", [120, 2, CC])
    stT = sb("stateT", [P, 2, NS, CW - 1])
    ssum = sb("state_sum", [P, 2, NS])
    crow = sb("conv_out_rows", [P, CC])
    grow = sb("glu_out_rows", [30, 2, CC])
    lng = sb("conv_ln", [P, 2, CC])
    stats = sb("conv_stats", [P, 2, 8])
    y = sb("conv_rows_y", [P, 2, CC])
    k_in = [sem(f"k_cached{i}") for i in range(NI)]
    v_in = [sem(f"v_cached{i}") for i in range(NI)]
    st_in = sem("state_in")
    prod, s_ready, s_turned, sp_ready, sp_turned, spT = (sem(n) for n in (
        "k_times_q", "s_scored", "s_scores_turned", "s_probs_ready", "s_probs_turned", "s_probsT_ready"))
    vprod_d = sem("p_times_v_last")
    vprod, v_summed, o_row, o_rowT, o_rowT_kept = (sem(n) for n in ("p_times_v", "v_summed", "o_row", "o_row_turned", "o_row_kept"))
    e_neg, e_exp = sem("merge_shift"), sem("merge_exp")
    m_turned, m_kept, f_ready, f_spread, f_used = (sem(n) for n in ("max_turned", "max_kept", "weights_ready", "weights_spread", "weights_used"))
    c_turned, c_kept, c_var, c_pow, c_lin, c_act, c_back, c_backk = (sem(n) for n in (
        "conv_turned", "conv_kept", "conv_var", "conv_rstd", "conv_lin", "conv_silu", "conv_back", "conv_back_kept"))
    st_turned, st_kept, g_turned, g_kept, out2, ones_in = (sem(n) for n in (
        "state_turned", "state_kept", "glu_turned", "glu_kept", "stage2_out", "sample_rows_in"))
    caches = (A["cache0"], A["cache1"], A["cache2"])


    def keep_heads(copy, dst, bank0):
        for g in range(NG):
            d = dst[:, g] if g == 0 else dst[:, g].rearrange("p (i r) -> p r i", r=4)
            s_ = bank(k, bank0 + g)[0:NH]
            s_ = s_ if g == 0 else s_.rearrange("p (r i) -> p r i", r=4)
            copy(d, s_).then_inc(m_kept, 1)

    block = st.enter_context(nc.Block())

    @block.sync
    def _(sp):
        sp.dma_start(lng[:, 0], A["conv_ln_g"][0].partition_broadcast(P)).then_inc(st_in, 16)
        sp.dma_start(lng[:, 1], A["conv_ln_b"][0].partition_broadcast(P)).then_inc(st_in, 16)
        for i in range(2):
            sp.dma_start(strow[:, i], A["state_conv"][0, 4 * i:4 * i + 4].rearrange("n w c -> (n w) c")
                         ).then_inc(st_in, 16)
        for which in range(2):
            for n in range(NS):
                i = n % NI
                done = (k_in, v_in)[which][i]
                if which == 0 and n >= NI:
                    sp.wait_ge(s_ready, 2 * (n - NI + 1))
                if which == 1 and n < NI:
                    sp.wait_ge(s_ready, 2 * (NS - NI + n + 1))
                if which == 1 and n >= NI:
                    sp.wait_ge(vprod, n - NI + 1)
                    sp.wait_ge(vprod_d, 2 * (n - NI + 1))
                for g in range(2):
                    src = caches[g][0, n].rearrange("s w h e -> s w (h e)")[:, which]
                    if g:
                        src = src.rearrange("(i r) c -> r i c", r=RATES[g])[0]
                    sp.dma_start(kv[:, i, g], src).then_inc(done, 16)
                src = caches[2][0, n].rearrange("s w h e -> s w (h e)")[:, which]
                sp.dma_start(kve[0:32, i], src.rearrange("(i r) c -> r i c", r=RATES[2])[0]).then_inc(done, 16)
                sp.dma_start(kve[32:NK2, i], k.kv_scr[n, :, which]).then_inc(done, 16)
                if which == 0:
                    sp.dma_start(qb[:, i], k.q_scr[n, 0:2].partition_broadcast(P)).then_inc(done, 16)
                    sp.dma_start(qe[0:32, i], k.q_scr[n, 2].partition_broadcast(32)).then_inc(done, 16)
                    sp.dma_start(qe[32:NK2, i], k.q_scr[n]).then_inc(done, 16)
            if which == 0:
                src = A["w_out"][0].rearrange("(k p) n -> p k n", p=P)
                sp.dma_start(k.wo[0], src[:, 0:4]).then_inc(k.wo_in, 16)
                sp.dma_start(k.wo[1], src[:, 4:6]).then_inc(k.wo_in, 16)
                sp.dma_start(k.h[:, 0:PT], A["x_prompt"][0].rearrange("(t p) d -> p t d", p=P)).then_inc(k.x_again_in, 16)
                sp.dma_start(k.h[0:NS, PT], A["x_sample"][:, 0]).then_inc(k.x_again_in, 16)
        sp.dma_start(A["s_conv"][0, :, 0:CW - 2], A["state_conv"][0, :, 1:CW - 1]).then_inc(out2, 16)
        sp.wait_ge(g_kept, 2)
        sp.dma_start(A["p_conv"][0, 0], grow[:, 0]).then_inc(out2, 16)
        sp.dma_start(A["s_conv"][0, :, CW - 2], grow[0:NS, 1]).then_inc(out2, 16)
        sp.wait_ge(out2, 48)

    @block.tensor
    def _(pe):
        ident = cst(k, "ident")
        for j, src in enumerate((k.nm, k.sums)):
            for g in range(NG):
                for t in range(PT):
                    last = pe.transpose(bank(k, 3 * j + g)[0:NH, t * P:(t + 1) * P], src[:, g, t], ident)
        last.then_inc(m_turned, 1)
        for cc in range(2):
            pe.transpose(bank(k, 6)[0:30, cc * P:(cc + 1) * P], k.glu[:, cc, SEQ:SEQ + 30], ident)
            last = pe.transpose(bank(k, 6)[0:NS, CC + cc * P:CC + (cc + 1) * P], k.glu_s[:, cc], ident)
        last.then_inc(g_turned, 1)
        pe.wait_ge(st_in, 64)
        for cc in range(2):
            for i in range(2):
                last = pe.transpose(bank(k, 7)[:, cc * 256 + i * 120:cc * 256 + (i + 1) * 120],
                                    strow[:, i, cc * P:(cc + 1) * P], ident[0:120, 0:120])
        last.then_inc(st_turned, 1)
        pe.wait_ge(m_kept, 6)
        pe.wait_ge(g_kept, 2)
        pe.wait_ge(st_kept, 1)

        def conv_row(t):
            R = rows_of(t)
            if t >= 2:
                pe.wait_ge(c_kept, t - 1)
            for cc in range(2):
                last = pe.transpose(bank(k, t % 2)[0:R, cc * P:(cc + 1) * P],
                                    k.conv[:, cc, t * P:t * P + R], ident)
            last.then_inc(c_turned, 1)

        def conv_back(t):
            R = rows_of(t)
            pe.wait_ge(c_act, t + 1)
            if t >= 2:
                pe.wait_ge(c_backk, t - 1)
            for cc in range(2):
                last = pe.transpose(bank(k, 2 + t % 2)[:, cc * P:cc * P + R], y[0:R, t % 2, cc * P:(cc + 1) * P],
                                    ident[0:R, 0:R])
            last.then_inc(c_back, 1)

        for t in range(NT + 1):
            if t < NT:
                conv_row(t)
            if t:
                conv_back(t - 1)
        pe.wait_ge(s_ready, 2 * NS)
        for g in range(NG):
            n = P if g < 2 else NK2
            last = pe.transpose(bank(k, 4)[0:NS * NH, g * P:g * P + n], S[0:n, g], ident[0:n, 0:n])
        last.then_inc(s_turned, 1)
        pe.wait_ge(f_ready, 1)
        for j in range(NPAIR):
            if j == 1:
                pe.wait_ge(c_backk, NT)
            for g in range(NG):
                b = (5, 6, 7, 0, 1, 2)[3 * (j % 2) + g]
                if j >= 2:
                    pe.wait_ge(f_used, NG * (j - 2) + g + 1)
                pe.matmul(bank(k, b), cst(k, "sel", NH)[:, j * P:(j + 1) * P], lT[:, g], start=True, stop=True
                          ).then_inc(f_spread, 1)
        pe.wait_ge(sp_ready, 1)
        for g in range(NG):
            n = P if g < 2 else NK2
            last = pe.transpose(bank(k, 3)[0:n, g * 64:(g + 1) * 64], PRS[:, g * P:g * P + n], ident[0:64, 0:64])
        last.then_inc(sp_turned, 1)
        pe.wait_ge(ones_in, 1 + NS)
        for n in range(NS):
            pe.wait_ge(vprod, n + 1)
            pe.wait_ge(vprod_d, 2 * (n + 1))
            i = n % NI
            for g in range(2):
                pe.matmul(bank(k, 4)[0:NS], onec[:, n], qb[:, i, g], start=n == 0 and g == 0, stop=False)
            pe.matmul(bank(k, 4)[0:NS], onec[0:NK2, n], qe[:, i], start=False, stop=n == NS - 1).then_inc(v_summed, 1)
        pe.wait_ge(o_row, 1)
        for j in range(NPAIR):
            last = pe.transpose(bank(k, 3)[:, 192 + j * NS:192 + (j + 1) * NS], orow[:, j * P:(j + 1) * P],
                                ident[0:NS, 0:NS])
        last.then_inc(o_rowT, 1)

    @block.scalar
    def _(act):
        act.wait_ge(m_turned, 1)
        keep_heads(act.copy, lT, 3)
        act.wait_ge(g_turned, 1)
        act.copy(grow[:, 0], bank(k, 6)[0:30, 0:CC]).then_inc(g_kept, 1)
        act.copy(grow[0:NS, 1], bank(k, 6)[0:NS, CC:2 * CC]).then_inc(g_kept, 1)
        act.wait_ge(e_neg, 1)
        act.activation(mT[:], mT[:], ACT.Exp).then_inc(e_exp, 1)
        for t in range(NT):
            R = rows_of(t)
            act.wait_ge(c_lin, t + 1)
            if t >= 2:
                act.wait_ge(c_back, t - 1)
            act.activation(y[0:R, t % 2], crow[0:R], ACT.Silu).then_inc(c_act, 1)
            act.wait_ge(c_back, t + 1)
            src = bank(k, 2 + t % 2)[:, 0:CC].rearrange("p (c n) -> p c n", c=2)[:, :, 0:R]
            act.copy(k.mixT[:, 4:6, t * P:t * P + R], src).then_inc(c_backk, 1)
        act.wait_ge(e_neg, 2)
        act.activation(PRS[:], bank(k, 4)[0:64, 0:2 * P + NK2], ACT.Exp, bias=small[:, 1:2], scale=SCALE,
                       accum_out=small[:, 2:3]).then_inc(e_exp, 1)

    @block.vector
    def _(dve):
        ch = Chain(dve, k.dve_chain)
        ch.n = k.dve_n
        dve.wait_ge(m_turned, 1)
        keep_heads(dve.tensor_copy, mT, 0)
        dve.wait_ge(m_kept, 6)
        dve.wait_ge(st_turned, 1)
        dve.tensor_copy(stT[:], bank(k, 7).rearrange("p (c m) -> p c m", c=2)[:, :, 0:240]
                        .rearrange("p c (n w) -> p c n w", n=NS)).then_inc(st_kept, 1)
        dve.wait_ge(st_kept, 1)

        def sample_conv():
            for cc in range(2):
                last = dve.tensor_tensor(stT[:, cc], stT[:, cc], k.taps[:, cc:cc + 1, 0:CW - 1].to_broadcast([P, NS, CW - 1]),
                                         ALU.mult)
            ch.link(last)
            ch.link(dve.tensor_reduce(ssum[:], stT[:], AX, ALU.add))
            for cc in range(2):
                last = dve.scalar_tensor_tensor(out=ssum[:, cc], in0=k.glu_s[:, cc], scalar=k.taps[:, cc, CW - 1:CW],
                                                in1=ssum[:, cc], op0=ALU.mult, op1=ALU.add)
            ch.link(last)
            for cc in range(2):
                last = dve.tensor_scalar(k.conv[:, cc, SEQ:TOK], ssum[:, cc], k.taps[:, cc, CW:CW + 1], None, ALU.add)
            last.then_inc(st_kept, 1)

        def merge_shift():
            ch.link(dve.tensor_tensor(mm[:], mT[:, 0], mT[:, 1], ALU.min))
            ch.link(dve.tensor_tensor(mm[:], mm[:], mT[:, 2], ALU.min))
            for g in range(NG):
                last = dve.tensor_tensor(mT[:, g], mm[:], mT[:, g], ALU.subtract)
            last.then_inc(e_neg, 1)

        def merge_weights():
            dve.wait_ge(e_exp, 1)
            ch.link(dve.tensor_tensor(lT[:], lT[:], mT[:], ALU.mult))
            ch.link(dve.tensor_tensor(ll[:], lT[:, 0], lT[:, 1], ALU.add))
            ch.link(dve.tensor_tensor(ll[:], ll[:], lT[:, 2], ALU.add))
            ch.link(dve.reciprocal(ll[:], ll[:]))
            for g in range(NG):
                last = dve.tensor_tensor(lT[:, g], mT[:, g], ll[:], ALU.mult)
            last.then_inc(f_ready, 1)

        def conv_norm(t):
            R = rows_of(t)
            dve.wait_ge(c_turned, t + 1)
            row = bank(k, t % 2)[0:R, 0:CC]
            ch.link(dve.bn_stats(stats[0:R, t % 2, 0:6], row))
            ch.link(dve.bn_aggr(stats[0:R, t % 2, 6:8], stats[0:R, t % 2, 0:6]))
            dve.tensor_scalar(stats[0:R, t % 2, 7:8], stats[0:R, t % 2, 7:8], EPS, None, ALU.add).then_inc(c_var, 1)
            dve.wait_ge(c_pow, t + 1)
            if t:
                dve.wait_ge(c_act, t)
            ch.link(dve.tensor_scalar(crow[0:R], row, stats[0:R, t % 2, 6:7], stats[0:R, t % 2, 0:1],
                                      ALU.subtract, ALU.mult))
            dve.engine_nop().then_inc(c_kept, 1)
            ch.link(dve.tensor_tensor(crow[0:R], crow[0:R], lng[0:R, 0], ALU.mult))
            dve.tensor_tensor(crow[0:R], crow[0:R], lng[0:R, 1], ALU.add).then_inc(c_lin, 1)

        def sample_scores(n):
            i = n % NI
            dve.wait_ge(k_in[i], 7 * 16 * (n // NI + 1))
            ch.link(dve.tensor_tensor(qe[:, i], kve[:, i], qe[:, i], ALU.mult))
            dve.wait_ge(prod, n + 1)
            dve.tensor_reduce(S[:, 0:2, n * NH:(n + 1) * NH], qb[:, i].rearrange("p g (h e) -> p g h e", e=HD), AX,
                              ALU.add).then_inc(s_ready, 1)
            dve.tensor_reduce(S[0:NK2, 2, n * NH:(n + 1) * NH], qe[:, i].rearrange("p (h e) -> p h e", e=HD), AX,
                              ALU.add).then_inc(s_ready, 1)

        for n in range(NS):
            sample_scores(n)
            if n == 0:
                sample_conv()
            if n == 1:
                merge_shift()
            if n == 2:
                merge_weights()
                dve.wait_ge(st_in, 64)
            if n >= NS - NT:
                conv_norm(n - (NS - NT))
        dve.wait_ge(s_turned, 1)
        ch.link(dve.tensor_reduce(small[:, 0:1], bank(k, 4)[0:64, 0:2 * P + NK2], AX, ALU.max))
        dve.tensor_scalar(small[:, 1:2], small[:, 0:1], -SCALE, None, ALU.mult).then_inc(e_neg, 1)
        for j in range(NPAIR):
            for g in range(NG):
                dve.wait_ge(f_spread, NG * j + g + 1)
                b = (5, 6, 7, 0, 1, 2)[3 * (j % 2) + g]
                last = dve.tensor_tensor(part[:, j % 2, g], bank(k, b), k.oT[:, g, j], ALU.mult)
                last.then_inc(f_used, 1)
            dve.wait_ge(f_used, NG * (j + 1))
            ch.link(dve.tensor_tensor(part[:, j % 2, 0], part[:, j % 2, 0], part[:, j % 2, 1], ALU.add))
            ch.link(dve.tensor_tensor(k.mixT[:, j, 0:SEQ], part[:, j % 2, 0], part[:, j % 2, 2], ALU.add))
            if j == 0:
                dve.wait_ge(e_exp, 2)
                ch.link(dve.reciprocal(small[:, 3:4], small[:, 2:3]))
                dve.tensor_scalar(PRS[:], PRS[:], small[:, 3:4], None, ALU.mult).then_inc(sp_ready, 1)
        dve.wait_ge(sp_turned, 1)
        dve.tensor_copy(PT_[:, 0:2], bank(k, 3)[:, 0:128].rearrange("p (g m) -> p g m", g=2)).then_inc(spT, 1)
        dve.tensor_copy(PT_[0:NK2, 2], bank(k, 3)[0:NK2, 128:192]).then_inc(spT, 1)
        dve.wait_ge(spT, 2)
        for n in range(NS):
            i = n % NI
            dve.wait_ge(v_in[i], 4 * 16 * (n // NI + 1))
            if n >= NI:
                dve.wait_ge(v_summed, n - NI + 1)
            w = PT_[:, 1, n * NH:(n + 1) * NH].unsqueeze(2).to_broadcast([P, NH, HD])
            dve.tensor_tensor(qb[:, i, 1].rearrange("p (h e) -> p h e", e=HD),
                              kv[:, i, 1].rearrange("p (h e) -> p h e", e=HD), w, ALU.mult).then_inc(vprod_d, 1)
            w = PT_[0:NK2, 2, n * NH:(n + 1) * NH].unsqueeze(2).to_broadcast([NK2, NH, HD])
            dve.tensor_tensor(qe[:, i].rearrange("p (h e) -> p h e", e=HD),
                              kve[:, i].rearrange("p (h e) -> p h e", e=HD), w, ALU.mult).then_inc(vprod_d, 1)
        dve.wait_ge(v_summed, NS)
        dve.tensor_copy(orow[:], bank(k, 4)[0:NS]).then_inc(o_row, 1)
        dve.wait_ge(o_rowT, 1)
        dve.tensor_copy(k.mixT[:, 0:4, SEQ:TOK], bank(k, 3)[:, 192:192 + NPAIR * NS].rearrange("p (j n) -> p j n", n=NS)
                        ).then_inc(o_rowT_kept, 1)
        k.dve_n = ch.n

    @block.gpsimd
    def _(pool):
        pool.memset(onec[:], 0.0).then_inc(ones_in, 1)
        pool.wait_ge(ones_in, 1)
        for n in range(NS):
            pool.memset(onec[:, n, n:n + 1], 1.0).then_inc(ones_in, 1)

        def times_q(n):
            i = n % NI
            pool.wait_ge(k_in[i], 7 * 16 * (n // NI + 1))
            pool.tensor_tensor(qb[:, i], kv[:, i], qb[:, i], ALU.mult).then_inc(prod, 1)

        def rstd(t):
            R = rows_of(t)
            pool.wait_ge(c_var, t + 1)
            pool.tensor_tensor(stats[0:R, t % 2, 0:1], stats[0:R, t % 2, 7:8], cst(k, "mhalf", R), ALU.pow).then_inc(c_pow, 1)

        for n in range(NS + 1):
            if n < NS:
                times_q(n)
            if n > NS - NT:
                rstd(n - (NS - NT) - 1)
        pool.wait_ge(spT, 2)
        for n in range(NS):
            i = n % NI
            pool.wait_ge(v_in[i], 4 * 16 * (n // NI + 1))
            pool.wait_ge(s_ready, 2 * NS)
            if n >= NI:
                pool.wait_ge(v_summed, n - NI + 1)
            w = PT_[:, 0, n * NH:(n + 1) * NH].unsqueeze(2).to_broadcast([P, NH, HD])
            pool.tensor_tensor(qb[:, i, 0].rearrange("p (h e) -> p h e", e=HD),
                               kv[:, i, 0].rearrange("p (h e) -> p h e", e=HD), w, ALU.mult).then_inc(vprod, 1)


class RowNorm:

    def __init__(self, k, st, name, g_dram, b_dram):
        self.k, self.name, self.g_dram, self.b_dram = k, name, g_dram, b_dram
        sb = lambda n, shape: st.enter_context(k.nc.sbuf_tensor(f"{name}_{n}", shape, F32))
        self.gb = sb("gain_shift", [P, 2, D])
        self.stats = sb("stats", [P, NT, 16])
        (self.gb_in, self.var, self.rstd, self.shift, self.normed, self.scaled, self.done) = (
            k.sem(f"{name}_{n}") for n in ("gain_in", "var", "rstd", "shift", "normed", "scaled", "done"))

    def load(self, sp):
        sp.dma_start(self.gb[:, 0], self.g_dram.partition_broadcast(P)).then_inc(self.gb_in, 16)
        sp.dma_start(self.gb[:, 1], self.b_dram.partition_broadcast(P)).then_inc(self.gb_in, 16)

    def moments(self, dve, ch, t):
        R, s = rows_of(t), self.stats
        for hh in range(2):
            last = dve.bn_stats(s[0:R, t, 6 * hh:6 * hh + 6], self.k.h[0:R, t, 512 * hh:512 * hh + 512])
        ch.link(last)
        ch.link(dve.bn_aggr(s[0:R, t, 12:14], s[0:R, t, 0:12]))
        dve.tensor_scalar(s[0:R, t, 13:14], s[0:R, t, 13:14], EPS, None, ALU.add).then_inc(self.var, 1)
        dve.wait_ge(self.rstd, t + 1)
        dve.scalar_tensor_tensor(out=s[0:R, t, 15:16], in0=s[0:R, t, 12:13], scalar=-1.0, in1=s[0:R, t, 14:15],
                                 op0=ALU.mult, op1=ALU.mult).then_inc(self.shift, 1)

    def power(self, pool, t):
        R, s = rows_of(t), self.stats
        pool.wait_ge(self.var, t + 1)
        pool.tensor_tensor(s[0:R, t, 14:15], s[0:R, t, 13:14], cst(self.k, "mhalf", R), ALU.pow).then_inc(self.rstd, 1)

    def normalise(self, act, t):
        R, s, h = rows_of(t), self.stats, self.k.h
        act.wait_ge(self.shift, t + 1)
        act.activation(h[0:R, t], h[0:R, t], ACT.Identity, bias=s[0:R, t, 15:16], scale=s[0:R, t, 14:15]
                       ).then_inc(self.normed, 1)

    def gain(self, dve, t):
        R, h = rows_of(t), self.k.h
        if t == 0:
            dve.wait_ge(self.gb_in, 32)
        dve.wait_ge(self.normed, t + 1)
        dve.tensor_tensor(h[0:R, t], h[0:R, t], self.gb[0:R, 0], ALU.mult).then_inc(self.scaled, 1)

    def offset(self, pool, t):
        R, h = rows_of(t), self.k.h
        pool.wait_ge(self.scaled, t + 1)
        if t == 0:
            pool.wait_ge(self.gb_in, 32)
        pool.tensor_tensor(h[0:R, t], h[0:R, t], self.gb[0:R, 1], ALU.add).then_inc(self.done, 1)


class Router:

    def __init__(self, k, st, l):
        self.k, self.l = k, l
        sb = lambda n, shape, dt=F32: st.enter_context(k.nc.sbuf_tensor(f"route{l}_{n}", shape, dt))
        F16 = mybir.dt.float16
        self.rw, self.rb = sb("w", [P, KT, NE]), sb("bias", [P, NE])
        self.hT = sb("hT", [P, KT, TOK])
        self.LG = sb("logits", [P, NT, NE])
        self.sc, self.sel, self.tmp = sb("scores", [P, NT, NE]), sb("selection", [P, NT, NE]), sb("tmp", [P, NT, NE])
        self.pairs, self.grp, self.gw = sb("pairs", [P, NT * 4, 6]), sb("groups", [P, NT, 4]), sb("group_pick", [P, NT, 4])
        self.oh, self.A = sb("one_hot", [P, 2, NT, NE]), sb("chosen", [P, NT, NE])
        self.C, self.tot = sb("earlier", [P, NT, NE]), sb("all_chosen", [P, NE])
        self.m5, self.rank = sb("per_token", [P, 4, NT]), sb("rank", [P, 5, 2, NT])
        self.val = sb("token_value", [P, 2, NT, NE], F16)
        self.SL = sb("slot_one_hot", [P, 2, 2 * NT, P], F16)
        self.T = sb("table", [P, 5 * NE + MAX_EXTRA])
        self.flag = sb("flags", [P, 2, 5 * NE + MAX_EXTRA])
        self.ex, self.cum, self.M = sb("exists", [P, 2, 4 * NE]), sb("cumulated", [P, 4 * NE]), sb("pick", [P, MAX_EXTRA, 4 * NE])
        self.M2, self.xf, self.cnt = sb("pick2", [P, MAX_EXTRA, 4 * NE]), sb("extras_f", [P, MAX_EXTRA + 1]), sb("counts", [P, NE])
        (self.w_in, self.turned, self.kept, self.lg, self.shifted, self.exped, self.chosen,
         self.ranked, self.slots, self.tabled, self.ready) = (k.sem(f"route{l}_{n}") for n in (
             "w_in", "turned", "kept", "logits_ready", "shifted", "exped", "chosen_ready",
             "ranked", "slots", "tabled", "ready"))

    def load(self, sp):
        sp.dma_start(self.rw[:], self.k.A["router_w"].rearrange("(k p) e -> p k e", p=P)).then_inc(self.w_in, 16)
        sp.dma_start(self.rb[:], self.k.A["router_bias"].partition_broadcast(P)).then_inc(self.w_in, 16)

    def turn(self, pe, t, done):
        k, R = self.k, rows_of(t)
        pe.wait_ge(done, t + 1)
        if t:
            pe.wait_ge(self.kept, 2 * t)
        for kk in range(KT):
            last = pe.transpose(bank(k, 4 + kk // 4)[:, (kk % 4) * P:(kk % 4) * P + R],
                                k.h[0:R, t, kk * P:(kk + 1) * P], cst(k, "ident", R)[:, 0:R])
        last.then_inc(self.turned, 1)

    def keep(self, engine_copy, wait, t, half):
        k, R = self.k, rows_of(t)
        wait(self.turned, t + 1)
        src = bank(k, 4 + half).rearrange("p (k c) -> p k c", c=P)[:, :, 0:R]
        engine_copy(self.hT[:, 4 * half:4 * half + 4, t * P:t * P + R], src).then_inc(self.kept, 1)

    def logits(self, pe, t):
        k, R = self.k, rows_of(t)
        pe.wait_ge(self.kept, 2 * (t + 1))
        if t == 0:
            pe.wait_ge(self.w_in, 32)
        for kk in range(KT):
            last = pe.matmul(bank(k, 7)[0:R, t * NE:(t + 1) * NE], self.hT[:, kk, t * P:t * P + R], self.rw[:, kk],
                             start=kk == 0, stop=kk == KT - 1)
        last.then_inc(self.lg, 1)

    def pe_tables(self, pe):
        k = self.k
        pe.wait_ge(self.chosen, 1)
        flat = lambda x: x[:].rearrange("p t e -> p (t e)")
        pe.matmul(bank(k, 6)[:, 0:NT * NE], cst(k, "before"), flat(self.A), start=True, stop=False)
        pe.matmul(bank(k, 6)[:, 0:NT * NE], cst(k, "ones"), flat(self.C), start=False, stop=True)
        pe.matmul(bank(k, 6)[:, NT * NE:(NT + 1) * NE], cst(k, "ones"), self.tot[:], start=True, stop=True
                  ).then_inc(self.ranked, 1)
        for r in range(5):
            pe.wait_ge(self.slots, r + 1)
            for j in range(2):
                for t in range(NT):
                    last = pe.matmul(bank(k, 7)[:, 256 + r * NE:256 + (r + 1) * NE], self.SL[:, r % 2, j * NT + t],
                                     self.val[:, j, t], start=j == 0 and t == 0, stop=j == 1 and t == NT - 1)
            last.then_inc(self.tabled, 1)

    def act(self, act):
        act.wait_ge(self.shifted, 1)
        act.activation(self.sc[:], self.sc[:], ACT.Exp).then_inc(self.exped, 1)

    def dve(self, dve, ch):
        k, l, L = self.k, self.l, ch.link
        tt = dve.tensor_tensor
        b3 = lambda x, n: x.unsqueeze(2).to_broadcast([P, x.shape[1], n])
        tokens = lambda name, n: cst(k, name).unsqueeze(1).to_broadcast([P, NT, n])
        m5 = self.m5
        L(dve.memset(self.LG[:], 0.0))
        dve.wait_ge(self.lg, NT)
        dve.tensor_copy(self.LG[:, 0:PT], bank(k, 7)[:, 0:PT * NE].rearrange("p (t e) -> p t e", e=NE))
        L(dve.tensor_copy(self.LG[0:NS, PT], bank(k, 7)[0:NS, PT * NE:NT * NE]))
        L(dve.tensor_reduce(m5[:, 0], self.LG[:], AX, ALU.max))
        tt(self.sc[:], self.LG[:], b3(m5[:, 0], NE), ALU.subtract).then_inc(self.shifted, 1)
        dve.wait_ge(self.exped, 1)
        L(dve.tensor_reduce(m5[:, 1], self.sc[:], AX, ALU.add))
        L(dve.reciprocal(m5[:, 1], m5[:, 1]))
        L(tt(self.sc[:], self.sc[:], b3(m5[:, 1], NE), ALU.mult))
        dve.wait_ge(self.w_in, 32)
        L(tt(self.sel[:], self.sc[:], self.rb[:].unsqueeze(1).to_broadcast([P, NT, NE]), ALU.add))
        s4 = self.sel[:].rearrange("p t (g e) -> p (t g) e", e=4)
        tt(self.pairs[:, :, 0:3], s4[:, :, 0:3], s4[:, :, 1:4], ALU.add)
        tt(self.pairs[:, :, 3:5], s4[:, :, 0:2], s4[:, :, 2:4], ALU.add)
        L(tt(self.pairs[:, :, 5:6], s4[:, :, 0:1], s4[:, :, 3:4], ALU.add))
        L(dve.tensor_reduce(self.grp[:].rearrange("p t g -> p (t g)"), self.pairs[:], AX, ALU.max))

        def first_max(vals, pick, tmp, order, n):
            L(dve.tensor_reduce(m5[:, 2], vals, AX, ALU.max))
            L(tt(tmp, vals, b3(m5[:, 2], n), ALU.is_equal))
            L(tt(tmp, tmp, tokens(order, n), ALU.mult))
            L(dve.tensor_reduce(m5[:, 3], tmp, AX, ALU.max))
            L(tt(pick, tmp, b3(m5[:, 3], n), ALU.is_equal))

        first_max(self.grp[:], self.gw[:], self.grp[:], "rank4", 4)
        g4 = self.gw[:].unsqueeze(3).to_broadcast([P, NT, 4, 4])
        L(tt(self.sel[:].rearrange("p t (g e) -> p t g e", e=4), self.sel[:].rearrange("p t (g e) -> p t g e", e=4), g4,
             ALU.mult))
        L(dve.tensor_scalar(self.gw[:], self.gw[:], BIG, -BIG, ALU.mult, ALU.add))
        L(tt(self.sel[:].rearrange("p t (g e) -> p t g e", e=4), self.sel[:].rearrange("p t (g e) -> p t g e", e=4), g4,
             ALU.add))
        first_max(self.sel[:], self.oh[:, 0], self.tmp[:], "rank16", NE)
        L(dve.scalar_tensor_tensor(out=self.sel[:], in0=self.oh[:, 0], scalar=-4 * BIG, in1=self.sel[:], op0=ALU.mult,
                                   op1=ALU.add))
        first_max(self.sel[:], self.oh[:, 1], self.tmp[:], "rank16", NE)
        valid = cst(k, "valid").unsqueeze(2).to_broadcast([P, NT, NE])
        for j in range(2):
            last = tt(self.oh[:, j], self.oh[:, j], valid, ALU.mult)
        L(last)
        L(tt(self.A[:], self.oh[:, 0], self.oh[:, 1], ALU.add))
        L(dve.memset(self.C[:, 0], 0.0))
        for t in range(1, NT):
            L(tt(self.C[:, t], self.C[:, t - 1], self.A[:, t - 1], ALU.add))
        tt(self.tot[:], self.C[:, NT - 1], self.A[:, NT - 1], ALU.add).then_inc(self.chosen, 1)
        for j in range(2):
            L(tt(self.tmp[:], self.sc[:], self.oh[:, j], ALU.mult))
            L(dve.tensor_reduce(k.gates[l][:, j], self.tmp[:], AX, ALU.add))
        L(tt(m5[:, 0], k.gates[l][:, 0], k.gates[l][:, 1], ALU.add))
        L(dve.tensor_scalar(m5[:, 1], cst(k, "valid"), -1.0, 1.0, ALU.mult, ALU.add))
        L(tt(m5[:, 0], m5[:, 0], m5[:, 1], ALU.add))
        L(dve.reciprocal(m5[:, 0], m5[:, 0]))
        for j in range(2):
            last = tt(k.gates[l][:, j], k.gates[l][:, j], m5[:, 0], ALU.mult)
        L(last)
        tv = cst(k, "tokval").rearrange("p (t j) -> p j t", j=2)
        for j in range(2):
            last = tt(self.val[:, j], self.oh[:, j], tv[:, j].unsqueeze(2).to_broadcast([P, NT, NE]), ALU.mult)
        L(last)
        dve.wait_ge(self.ranked, 1)
        rk = bank(k, 6)[:, 0:NT * NE].rearrange("p (t e) -> p t e", e=NE)
        for j in range(2):
            L(tt(self.tmp[:], self.oh[:, j], rk, ALU.mult))
            L(dve.tensor_reduce(self.rank[:, 0, j], self.tmp[:], AX, ALU.add))
        L(dve.tensor_copy(self.cnt[:], bank(k, 6)[:, NT * NE:(NT + 1) * NE]))
        for r in range(1, 5):
            last = dve.tensor_scalar(self.rank[:, r], self.rank[:, 0], float(-P * r), None, ALU.add)
        L(last)
        for r in range(5):
            if r >= 2:
                dve.wait_ge(self.tabled, r - 1)
            tt(self.SL[:, r % 2], cst(k, "slot").unsqueeze(1).to_broadcast([P, 2 * NT, P]),
               self.rank[:, r].rearrange("p j t -> p (j t)").unsqueeze(2).to_broadcast([P, 2 * NT, P]), ALU.is_equal
               ).then_inc(self.slots, 1)
        ex, cum = self.ex, self.cum
        for r in range(1, 5):
            last = dve.tensor_scalar(ex[:, 0, (r - 1) * NE:r * NE], self.cnt[:], float(P * r), None, ALU.is_gt)
        L(last)
        L(dve.tensor_tensor_scan(cum[:], cst(k, "ones")[:, 0:4 * NE], ex[:, 0], 0.0, ALU.mult, ALU.add))
        L(tt(ex[:, 1], cum[:], ex[:, 0], ALU.subtract))
        over_j = lambda x: x.unsqueeze(1).to_broadcast([P, MAX_EXTRA, 4 * NE])
        L(tt(self.M[:], over_j(ex[:, 1]), b3(cst(k, "slot")[:, 0:MAX_EXTRA], 4 * NE), ALU.is_equal))
        L(tt(self.M[:], self.M[:], over_j(ex[:, 0]), ALU.mult))
        eidx = cst(k, "eidx").unsqueeze(1).unsqueeze(1).to_broadcast([P, MAX_EXTRA, 4, NE])
        L(tt(self.M2[:].rearrange("p j (r e) -> p j r e", e=NE), self.M[:].rearrange("p j (r e) -> p j r e", e=NE), eidx,
             ALU.mult))
        L(dve.tensor_reduce(self.xf[:, 0:MAX_EXTRA], self.M2[:], AX, ALU.add))
        L(dve.tensor_copy(self.xf[:, MAX_EXTRA:MAX_EXTRA + 1], cum[:, 4 * NE - 1:4 * NE]))
        dve.tensor_copy(k.extras[l][:], self.xf[:]).then_inc(self.ready, 1)
        dve.wait_ge(self.tabled, 5)
        N5 = 5 * NE
        L(dve.tensor_copy(self.T[:, 0:N5], bank(k, 7)[:, 256:256 + N5]))
        L(tt(self.M[:], self.M[:], over_j(self.T[:, NE:N5]), ALU.mult))
        L(dve.tensor_reduce(self.T[:, N5:N5 + MAX_EXTRA], self.M[:], AX, ALU.add))
        f = self.flag
        dve.tensor_scalar(f[:, 0], self.T[:], 0.0, 8192.0, ALU.is_equal, ALU.mult)
        L(dve.tensor_scalar(f[:, 1], self.T[:], TOK + 0.5, float(TOK), ALU.is_gt, ALU.mult))
        L(dve.scalar_tensor_tensor(out=self.T[:], in0=self.T[:], scalar=-1.0, in1=f[:, 0], op0=ALU.add, op1=ALU.add))
        L(tt(f[:, 1], self.T[:], f[:, 1], ALU.subtract))
        L(dve.memset(k.get[l][:], 2 * 4096))
        for dst, src in ((k.put[l], self.T), (k.get[l], f[:, 1])):
            dve.tensor_copy(dst[:, 0:NE], src[:, 0:NE])
            last = dve.tensor_copy(dst[:, NE:NE + MAX_EXTRA], src[:, N5:N5 + MAX_EXTRA])
        last.then_inc(self.ready, 1)


def project_out(k, st):
    nc, A, sem = k.nc, k.A, k.sem
    wo = k.wo
    norm = RowNorm(k, st, "mixnorm0", A["ln_mix_g"][0], A["ln_mix_b"][0])
    route = Router(k, st, 0)
    mixed, taken, stored = (sem(n) for n in ("mixed0", "mixed0_taken", "h0_stored"))
    block = st.enter_context(nc.Block())

    @block.sync
    def _(sp):
        norm.load(sp)
        route.load(sp)
        load_expert(k, sp, 0, 0, 0, k.w_moe[0][0])
        for t in range(NT):
            if t == NT - 1:
                sp.wait_ge(mixed, 2 * NT)
                load_expert(k, sp, 0, 1, 1, k.w_moe[0][1])
            sp.wait_ge(norm.done, t + 1)
            sp.dma_start(k.h_scr[0][t * P:t * P + rows_of(t)], k.h[0:rows_of(t), t]).then_inc(stored, 16)
        sp.wait_ge(stored, 16 * NT)

    @block.tensor
    def _(pe):
        pe.wait_ge(k.wo_in, 32)
        for t in range(NT + 1):
            if t < NT:
                R = rows_of(t)
                if t >= 2:
                    pe.wait_ge(taken, 2 * (t - 1))
                for hh in range(2):
                    for kk in range(6):
                        last = pe.matmul(bank(k, 2 * (t % 2) + hh)[0:R], k.mixT[:, kk, t * P:t * P + R],
                                         wo[kk // 4][:, kk % 4, 512 * hh:512 * hh + 512], start=kk == 0, stop=kk == 5)
                    last.then_inc(mixed, 1)
            if t:
                route.turn(pe, t - 1, norm.done)
            if t >= 2:
                route.logits(pe, t - 2)
        route.logits(pe, NT - 1)
        route.pe_tables(pe)

    @block.scalar
    def _(act):
        for t in range(NT):
            norm.normalise(act, t)
            route.keep(act.copy, act.wait_ge, t, 0)
        route.act(act)

    @block.vector
    def _(dve):
        ch = Chain(dve, k.dve_chain)
        ch.n = k.dve_n
        dve.wait_ge(k.x_again_in, 32)
        for t in range(NT + 1):
            if t < NT:
                R = rows_of(t)
                for hh in range(2):
                    dve.wait_ge(mixed, 2 * t + hh + 1)
                    z = k.h[0:R, t, 512 * hh:512 * hh + 512]
                    dve.scalar_tensor_tensor(out=z, in0=z, scalar=ALPHA, in1=bank(k, 2 * (t % 2) + hh)[0:R],
                                             op0=ALU.mult, op1=ALU.add).then_inc(taken, 1)
                dve.wait_ge(taken, 2 * t + 2)
                norm.moments(dve, ch, t)
                norm.gain(dve, t)
            if t:
                route.keep(dve.tensor_copy, dve.wait_ge, t - 1, 1)
        route.dve(dve, ch)
        k.dve_n = ch.n

    @block.gpsimd
    def _(pool):
        for t in range(NT):
            norm.power(pool, t)
            norm.offset(pool, t)


NW = 4


def load_expert(k, sp, l, slot, e, done):
    A = k.A
    w13, w2 = (k.w13a, k.w2a) if slot < 2 else (k.w13b, k.w2b)
    slot %= 2
    sp.dma_start(w13[:, slot, :, 0:DE], A["moe_w1"][l, e].rearrange("(k p) f -> p k f", p=P)).then_inc(done, 16)
    sp.dma_start(w13[:, slot, :, DE:2 * DE], A["moe_w3"][l, e].rearrange("(k p) f -> p k f", p=P)).then_inc(done, 16)
    sp.dma_start(w2[:, slot], A["moe_w2"][l, e].rearrange("(k p) n -> p k n", p=P)).then_inc(done, 16)


def first_experts(k, sp, l):
    for e in range(k.n_ahead[l]):
        load_expert(k, sp, l, e, e, k.w_moe[l][e])


def experts(k, st, l):
    nc, A = k.nc, k.A
    sb = lambda name, shape, dt=F32: st.enter_context(nc.sbuf_tensor(f"moe{l}_{name}", shape, dt))
    XG, XT = sb("rows", [P, NW, D]), sb("rowsT", [P, KT, P])
    HS, G, GT = sb("silu", [P, DE]), sb("gated", [P, DE]), sb("gatedT", [P, 2, P])
    Y = sb("results", [P, NW, D])
    gi, pi = sb("get_column", [P, NW], I32), sb("put_column", [P, NW], I32)
    sem = lambda n: k.sem(f"moe{l}_{n}")
    got, put = [sem(f"got{i}") for i in range(NW)], [sem(f"put{i}") for i in range(NW)]
    (cleared, columns, fetches, stores, x_turned, x_kept, h_done, silu_done, g_ready, g_turned, gT_kept, y_done, y_kept) = (
        sem(n) for n in ("cleared", "columns", "fetches", "stores", "x_turned", "x_kept", "h_done", "silu_done", "g_ready", "g_turned", "gT_kept",
                         "y_done", "y_kept"))
    (e_w, e_got, e_put, e_columns, e_x_turned, e_x_kept, e_h, e_silu, e_g, e_g_turned, e_gT, e_y, e_y_kept, e_free) = (
        sem("e_" + n) for n in ("w", "got", "put", "columns", "x_turned", "x_kept", "h_done", "silu_done", "g_ready",
                                "g_turned", "gT_kept", "y_done", "y_kept", "slot_free"))
    pass_sem = sem("carried")
    w_in = k.w_moe[l]
    w13 = lambda s: (k.w13a, k.w13b)[s // 2][:, s % 2]
    w2 = lambda s: (k.w2a, k.w2b)[s // 2][:, s % 2]
    block = st.enter_context(nc.Block())

    def extra_passes(engine, body):
        n = engine.value_load(k.extras[l][0:1, MAX_EXTRA:MAX_EXTRA + 1], min_val=0, max_val=MAX_EXTRA)
        with engine.If(n > 0):
            with engine.Fori(0, n) as j:
                body(j)

    @block.sync
    def _(sp):
        for i in range(NW):
            sp.wait_ge(got[i], 16)
        for e in range(k.n_ahead[l], NW):
            load_expert(k, sp, l, e, e, w_in[e])
        with sp.Fori(1, NE // NW) as q:
            for c in range(NW):
                rows = [A[n][l, bass.ds(4 * q + c, 1)].rearrange("o (k p) f -> p (o k) f", p=P)
                        for n in ("moe_w1", "moe_w3", "moe_w2")]
                b, s = (k.w13a, k.w13b)[c // 2], c % 2
                sp.wait_ge(y_done, 4 * q + (c - 3))
                sp.dma_start(b[:, s, :, 0:DE], rows[0]).then_inc(w_in[c], 16)
                sp.dma_start(b[:, s, :, DE:2 * DE], rows[1]).then_inc(w_in[c], 16)
                sp.dma_start(w2(c), rows[2]).then_inc(w_in[c], 16)
        sp.wait_ge(y_done, NE - 3)
        sp.sem_inc(e_free, 1)

        def body(j):
            e = sp.value_load(k.extras[l][0:1, bass.ds(j, 1)], min_val=0, max_val=NE - 1)
            rows = [A[n][l, bass.ds(e, 1)].rearrange("o (k p) f -> p (o k) f", p=P)
                    for n in ("moe_w1", "moe_w3", "moe_w2")]
            sp.wait_ge(e_free, j + 1)
            sp.dma_start(k.w13a[:, 0, :, 0:DE], rows[0]).then_inc(e_w, 16)
            sp.dma_start(k.w13a[:, 0, :, DE:2 * DE], rows[1]).then_inc(e_w, 16)
            sp.dma_start(w2(0), rows[2]).then_inc(e_w, 16)
        extra_passes(sp, body)

    @block.tensor
    def _(pe):
        ident = cst(k, "ident")

        def turn_x(slot):
            for kk in range(KT):
                last = pe.transpose(bank(k, kk // 4)[:, (kk % 4) * P:(kk % 4 + 1) * P],
                                    XG[:, slot, kk * P:(kk + 1) * P], ident)
            return last

        def up(slot, b):
            for kk in range(KT):
                last = pe.matmul(bank(k, 2 + b), XT[:, kk], w13(slot)[:, kk], start=kk == 0, stop=kk == KT - 1)
            return last

        def turn_g():
            for f in range(2):
                last = pe.transpose(bank(k, 4)[:, f * P:(f + 1) * P], G[:, f * P:(f + 1) * P], ident)
            return last

        def down(slot):
            for hh in range(2):
                for f in range(2):
                    last = pe.matmul(bank(k, 5 + hh), GT[:, f], w2(slot)[:, f, 512 * hh:512 * hh + 512],
                                     start=f == 0, stop=f == 1)
            return last

        def step(q, c):
            i = 4 * q + c
            pe.wait_ge(x_kept, 2 * (i + 1))
            pe.wait_ge(w_in[c % 4], 48 * (q + c // 4 + 1))
            if not isinstance(i, int) or i >= 2:
                pe.wait_ge(g_ready, i - 1)
            up(c % 4, c % 2).then_inc(h_done, 1)
            if c < NE - 1:
                pe.wait_ge(got[(c + 1) % NW], 16 * (q + (c + 1) // NW + 1))
                turn_x((c + 1) % NW).then_inc(x_turned, 1)
            if not isinstance(i, int) or i >= 1:
                pe.wait_ge(gT_kept, i)
                if not isinstance(i, int) or i >= 2:
                    pe.wait_ge(y_kept, 2 * (i - 1))
                down((c - 1) % 4).then_inc(y_done, 1)
            pe.wait_ge(g_ready, i + 1)
            turn_g().then_inc(g_turned, 1)

        pe.wait_ge(got[0], 16)
        turn_x(0).then_inc(x_turned, 1)
        for c in range(3):
            step(0, c)
        with pe.Fori(0, 3) as q:
            for c in range(3, 7):
                step(q, c)
        step(0, NE - 1)
        pe.wait_ge(gT_kept, NE)
        pe.wait_ge(y_kept, 2 * (NE - 1))
        down((NE - 1) % 4).then_inc(y_done, 1)

        def body(j):
            pe.wait_ge(e_got, 16 * j + 16)
            turn_x(0).then_inc(e_x_turned, 1)
            pe.wait_ge(e_x_kept, 2 * j + 2)
            pe.wait_ge(e_w, 48 * j + 48)
            up(0, 0).then_inc(e_h, 1)
            pe.wait_ge(e_g, j + 1)
            turn_g().then_inc(e_g_turned, 1)
            pe.wait_ge(e_gT, j + 1)
            down(0).then_inc(e_y, 1)
            pe.sem_inc(e_free, 1)
        extra_passes(pe, body)

    @block.scalar
    def _(act):
        def keep_x():
            return act.copy(XT[:, 0:4], bank(k, 0))

        def silu(b):
            return act.activation(HS[:], bank(k, 2 + b)[:, 0:DE], ACT.Silu)

        def keep_y(slot):
            return act.copy(Y[:, slot, 0:512], bank(k, 5))

        def keep_last_y(q, c):
            i = 4 * q + c
            act.wait_ge(y_done, i)
            if not isinstance(i, int) or i >= NW + 1:
                act.wait_ge(put[(c - 1) % NW], 16 * (q + (c - 1) // NW))
            keep_y((c - 1) % NW).then_inc(y_kept, 1)

        def step(q, c):
            i = 4 * q + c
            act.wait_ge(h_done, i + 1)
            if not isinstance(i, int) or i >= 1:
                act.wait_ge(g_ready, i)
            silu(c % 2).then_inc(silu_done, 1)
            if c < NE - 1:
                act.wait_ge(x_turned, i + 2)
                keep_x().then_inc(x_kept, 1)
            if not isinstance(i, int) or i >= 1:
                keep_last_y(q, c)

        act.wait_ge(x_turned, 1)
        keep_x().then_inc(x_kept, 1)
        for c in range(3):
            step(0, c)
        with act.Fori(0, 3) as q:
            for c in range(3, 7):
                step(q, c)
        step(0, NE - 1)
        keep_last_y(0, NE)
        act.wait_ge(put[0], 16 * (NE // NW))

        def body(j):
            act.wait_ge(e_x_turned, j + 1)
            keep_x().then_inc(e_x_kept, 1)
            act.wait_ge(e_h, j + 1)
            silu(0).then_inc(e_silu, 1)
            act.wait_ge(e_y, j + 1)
            keep_y(0).then_inc(e_y_kept, 1)
        extra_passes(act, body)

    @block.vector
    def _(dve):
        def keep_x():
            return dve.tensor_copy(XT[:, 4:8], bank(k, 1))

        def gate(b):
            return dve.tensor_tensor(G[:], HS[:], bank(k, 2 + b)[:, DE:2 * DE], ALU.mult)

        def keep_g():
            return dve.tensor_copy(GT[:], bank(k, 4)[:, 0:2 * P])

        def keep_y(slot):
            return dve.tensor_copy(Y[:, slot, 512:1024], bank(k, 6))

        def keep_last_y(q, c):
            i = 4 * q + c
            dve.wait_ge(y_done, i)
            if not isinstance(i, int) or i >= NW + 1:
                dve.wait_ge(put[(c - 1) % NW], 16 * (q + (c - 1) // NW))
            keep_y((c - 1) % NW).then_inc(y_kept, 1)

        def step(q, c):
            i = 4 * q + c
            dve.wait_ge(silu_done, i + 1)
            if not isinstance(i, int) or i >= 1:
                dve.wait_ge(g_turned, i)
            gate(c % 2).then_inc(g_ready, 1)
            if c < NE - 1:
                dve.wait_ge(x_turned, i + 2)
                keep_x().then_inc(x_kept, 1)
            if not isinstance(i, int) or i >= 1:
                keep_last_y(q, c)
            dve.wait_ge(g_turned, i + 1)
            keep_g().then_inc(gT_kept, 1)

        for i in range(NW):
            dve.memset(XG[:, i], 0.0).then_inc(cleared, 1)
        dve.wait_ge(x_turned, 1)
        keep_x().then_inc(x_kept, 1)
        for c in range(3):
            step(0, c)
        with dve.Fori(0, 3) as q:
            for c in range(3, 7):
                step(q, c)
        step(0, NE - 1)
        keep_last_y(0, NE)
        dve.wait_ge(put[0], 16 * (NE // NW))

        def body(j):
            dve.wait_ge(e_x_turned, j + 1)
            keep_x().then_inc(e_x_kept, 1)
            dve.wait_ge(e_silu, j + 1)
            gate(0).then_inc(e_g, 1)
            dve.wait_ge(e_g_turned, j + 1)
            keep_g().then_inc(e_gT, 1)
            dve.wait_ge(e_y, j + 1)
            keep_y(0).then_inc(e_y_kept, 1)
        extra_passes(dve, body)

    @block.gpsimd
    def _(pool):
        def hold(s, value):
            pool.wait_ge(s, value)
            pool.sem_inc(pass_sem, 1)

        def take_get(col, slot, signal):
            pool.tensor_copy(gi[:, slot:slot + 1], k.get[l][:, col]).then_inc(signal, 1)

        def take_put(col, slot, signal):
            pool.tensor_copy(pi[:, slot:slot + 1], k.put[l][:, col]).then_inc(signal, 1)

        def gather(slot, signal):
            pool.indirect_dma_start(out=XG[:, slot], out_offset=None, in_=k.h_scr[l],
                                    in_offset=bass.IndirectOffsetOnAxis(ap=gi[:, slot:slot + 1], axis=0),
                                    bounds_check=TOK - 1, oob_is_err=False).then_inc(signal, 16)

        def scatter(slot, signal):
            pool.indirect_dma_start(out=k.y_scr[l], out_offset=bass.IndirectOffsetOnAxis(ap=pi[:, slot:slot + 1], axis=0),
                                    in_=Y[:, slot], in_offset=None, bounds_check=2 * TOK - 1, oob_is_err=False
                                    ).then_inc(signal, 16)

        for i in range(NW):
            take_get(slice(i, i + 1), i, columns)
        pool.wait_ge(columns, NW)
        for i in range(NW):
            pool.wait_ge(cleared, i + 1)
            gather(i, got[i])

        def step(q, c):
            i = NW * q + c
            if not isinstance(i, int) or i + NW <= NE:
                hold(x_turned, i + 1)
                take_get(bass.ds(i + NW, 1), c, fetches)
                hold(fetches, i + 1)
                gather(c, e_got if isinstance(i, int) and i + NW == NE else got[c])
            if not isinstance(i, int) or i >= NW:
                hold(put[c], 16 * q)
            take_put(bass.ds(i, 1), c, stores)
            hold(stores, i + 1)
            hold(y_kept, 2 * i + 2)
            scatter(c, put[c])

        for c in range(NW):
            step(0, c)
        with pool.Fori(1, NE // NW - 1) as q:
            for c in range(NW):
                step(q, c)
        for c in range(NW):
            step(NE // NW - 1, c)
        for i in range(NW):
            pool.wait_ge(put[i], 16 * (NE // NW))
        pool.wait_ge(e_got, 16)

        def body(j):
            take_put(bass.ds(j + NE, 1), 0, e_columns)
            hold(e_columns, 2 * j + 1)
            hold(e_x_turned, j + 1)
            take_get(bass.ds(j + NE + 1, 1), 0, e_columns)
            hold(e_columns, 2 * j + 2)
            gather(0, e_got)
            hold(e_y_kept, 2 * j + 2)
            scatter(0, e_put)
            hold(e_put, 16 * j + 16)
            hold(e_got, 16 * j + 32)
        extra_passes(pool, body)


class Combine:

    def __init__(self, k, st, l):
        self.k, self.l = k, l
        self.y = st.enter_context(k.nc.sbuf_tensor(f"join{l}_results", [P, 2, 2, D], F32))
        self.y_in = [k.sem(f"join{l}_in0"), k.sem(f"join{l}_in1")]
        self.scaled, self.joined = k.sem(f"join{l}_scaled"), k.sem(f"join{l}_joined")

    def load(self, sp, t):
        R = rows_of(t)
        if t >= 2:
            sp.wait_ge(self.joined, t - 1)
        for j in range(2):
            a = j * TOK + t * P
            sp.dma_start(self.y[0:R, t % 2, j], self.k.y_scr[self.l][a:a + R]).then_inc(self.y_in[t % 2], 16)

    def scale(self, act, t):
        h = self.k.h[0:rows_of(t), t]
        act.mul(h, h, ALPHA).then_inc(self.scaled, 1)

    def join(self, dve, ch, t):
        R, k = rows_of(t), self.k
        dve.wait_ge(self.y_in[t % 2], 32 * (t // 2 + 1))
        dve.wait_ge(self.scaled, t + 1)
        for j in range(2):
            last = dve.scalar_tensor_tensor(out=k.h[0:R, t], in0=self.y[0:R, t % 2, j],
                                            scalar=k.gates[self.l][0:R, j, t:t + 1], in1=k.h[0:R, t],
                                            op0=ALU.mult, op1=ALU.add)
            if j == 0:
                ch.link(last)
        last.then_inc(self.joined, 1)
        dve.wait_ge(self.joined, t + 1)


def pool_mixer(k, st):
    nc, A, sem = k.nc, k.A, k.sem
    sb = lambda name, shape, dt=F32: st.enter_context(nc.sbuf_tensor(name, shape, dt))
    PRE = 16
    WINDOWS = (2, 4, 8, 16)
    dT = sb("pooledT", [P, KT, TOK])
    with ExitStack() as early:
        esb = lambda name, shape: early.enter_context(nc.sbuf_tensor(name, shape, F32))
        join = Combine(k, early, 0)
        norm = RowNorm(k, early, "ffnnorm0", A["ln_ffn_g"][0], A["ln_ffn_b"][0])
        hT = esb("h1T", [P, KT, PRE + SEQ])
        hS = esb("h1T_samples", [P, KT, NS])
        srow = esb("pool_state_rows", [120, D])
        sT = esb("pool_stateT", [P, KT, NS, 15])
        ssum = esb("pool_state_sum", [P, KT, NS])
        s = esb("window_sums", [P, 2, 2, 2, PRE + SEQ])
        turned, kept, s_in, s_turned, s_kept, ended, zeros = (sem(n) for n in (
            "h1_turned", "h1_kept", "pool_state_in", "pool_state_turned", "pool_state_kept", "pool_out", "h1_zeros"))
        block = early.enter_context(nc.Block())

        @block.sync
        def _(sp):
            norm.load(sp)
            sp.dma_start(srow[:], A["state_pool"][0].rearrange("n w d -> (n w) d")).then_inc(s_in, 16)
            for t in range(NT):
                join.load(sp, t)
            first_experts(k, sp, 1)
            sp.dma_start(A["s_pool"][0, :, 0:14], A["state_pool"][0, :, 1:15]).then_inc(ended, 16)
            sp.wait_ge(norm.done, NT)
            sp.dma_start(A["p_pool"][0, 0], k.h[P - 15:P, PT - 1]).then_inc(ended, 16)
            sp.dma_start(A["s_pool"][0, :, 14], k.h[0:NS, PT]).then_inc(ended, 16)
            sp.wait_ge(ended, 48)

        @block.tensor
        def _(pe):
            ident = cst(k, "ident")
            pe.wait_ge(s_in, 16)
            for kk in range(KT):
                last = pe.transpose(bank(k, 6 + kk // 4)[:, (kk % 4) * P:(kk % 4) * P + 120],
                                    srow[:, kk * P:(kk + 1) * P], ident[0:120, 0:120])
            last.then_inc(s_turned, 1)
            for t in range(NT):
                R = rows_of(t)
                pe.wait_ge(norm.done, t + 1)
                if t >= 2:
                    pe.wait_ge(kept, 2 * (t - 1))
                for kk in range(KT):
                    last = pe.transpose(bank(k, 2 * (t % 2) + kk // 4)[:, (kk % 4) * P:(kk % 4) * P + R],
                                        k.h[0:R, t, kk * P:(kk + 1) * P], ident[0:R, 0:R])
                last.then_inc(turned, 1)

        @block.scalar
        def _(act):
            for t in range(NT):
                join.scale(act, t)
            for t in range(NT):
                norm.normalise(act, t)
            act.wait_ge(s_turned, 1)
            for hh in range(2):
                src = bank(k, 6 + hh).rearrange("p (k c) -> p k c", c=P)[:, :, 0:120].rearrange(
                    "p k (n w) -> p k n w", w=15)
                act.copy(sT[:, 4 * hh:4 * hh + 4], src).then_inc(s_kept, 1)
            for t in range(NT):
                R = rows_of(t)
                act.wait_ge(turned, t + 1)
                for hh in range(2):
                    src = bank(k, 2 * (t % 2) + hh).rearrange("p (k c) -> p k c", c=P)[:, :, 0:R]
                    dst = (hT[:, 4 * hh:4 * hh + 4, PRE + t * P:PRE + t * P + R] if t < PT else
                           hS[:, 4 * hh:4 * hh + 4])
                    act.copy(dst, src).then_inc(kept, 1)

        def windows(eng, ch, gi, side):
            w, cc = WINDOWS[gi], slice(2 * gi, 2 * gi + 2)
            cur, width, n = hT[:, cc], 1, 0
            while width < w:
                lo = PRE - (w - 2 * width)
                nxt = s[:, side, n % 2]
                ch.link(eng.tensor_tensor(nxt[:, :, lo:], cur[:, :, lo:], cur[:, :, lo - width:PRE + SEQ - width],
                                          ALU.add))
                cur, width, n = nxt, 2 * width, n + 1
            x = hT[:, cc, PRE:]
            ic = cst(k, "invcnt").rearrange("p (i c) -> p i c", c=16)[:, gi:gi + 1].to_broadcast([P, 2, 16])
            other = s[:, side, n % 2]
            ch.link(eng.tensor_tensor(other[:, :, 0:16], cur[:, :, PRE:PRE + 16], ic, ALU.mult))
            eng.tensor_tensor(dT[:, cc, 0:16], other[:, :, 0:16], x[:, :, 0:16], ALU.subtract)
            if side == 0:
                last = eng.scalar_tensor_tensor(out=dT[:, cc, 16:SEQ], in0=cur[:, :, PRE + 16:], scalar=1.0 / w,
                                                in1=x[:, :, 16:SEQ], op0=ALU.mult, op1=ALU.subtract)
            else:
                ch.link(eng.tensor_scalar(other[:, :, PRE + 16:], cur[:, :, PRE + 16:], 1.0 / w, None, ALU.mult))
                last = eng.tensor_tensor(dT[:, cc, 16:SEQ], other[:, :, PRE + 16:], x[:, :, 16:SEQ], ALU.subtract)
            ch.link(last)

        @block.vector
        def _(dve):
            ch = Chain(dve, k.dve_chain)
            ch.n = k.dve_n
            dve.memset(hT[:, :, 0:PRE], 0.0).then_inc(zeros, 1)
            for t in range(NT + 1):
                if t < NT:
                    join.join(dve, ch, t)
                    norm.moments(dve, ch, t)
                if t:
                    norm.gain(dve, t - 1)
            dve.wait_ge(kept, 2 * NT)
            dve.wait_ge(s_kept, 2)
            dve.wait_ge(zeros, 1)
            for gi, w in enumerate(WINDOWS):
                last = dve.tensor_reduce(ssum[:, 2 * gi:2 * gi + 2], sT[:, 2 * gi:2 * gi + 2, :, 16 - w:15], AX, ALU.add)
            ch.link(last)
            ch.link(dve.tensor_tensor(ssum[:], ssum[:], hS[:], ALU.add))
            for gi, w in enumerate(WINDOWS):
                cc = slice(2 * gi, 2 * gi + 2)
                last = dve.scalar_tensor_tensor(out=dT[:, cc, SEQ:TOK], in0=ssum[:, cc], scalar=1.0 / w, in1=hS[:, cc],
                                                op0=ALU.mult, op1=ALU.subtract)
            ch.link(last)
            windows(dve, ch, 0, 0)
            windows(dve, ch, 2, 0)
            windows(dve, ch, 3, 0)
            k.dve_n = ch.n

        @block.gpsimd
        def _(pool):
            ch = Chain(pool, k.pool_chain)
            ch.n = k.pool_n
            for t in range(NT + 1):
                if t < NT:
                    norm.power(pool, t)
                if t:
                    norm.offset(pool, t - 1)
            pool.wait_ge(kept, 2 * NT)
            pool.wait_ge(zeros, 1)
            windows(pool, ch, 1, 1)
            k.pool_n = ch.n

    k.end_stage()
    norm1 = RowNorm(k, st, "mixnorm1", A["ln_mix_g"][1], A["ln_mix_b"][1])
    route = Router(k, st, 1)
    pw = sb("pool_w", [P, 4, 2, 256])
    vec = sb("pool_bias_scale", [P, 2, D])
    tmp = sb("pool_rows", [P, 2, D])
    v_in, mixed, biased, scaled, joined, stored = (sem(n) for n in (
        "pool_w_in", "mixed1", "pool_biased", "pool_scaled", "mixed1_joined", "h1_stored"))
    block = st.enter_context(nc.Block())

    @block.sync
    def _(sp):
        sp.dma_start(pw[:], A["pool_w"][0].rearrange("g (c p) n -> p g c n", p=P)).then_inc(v_in, 16)
        sp.dma_start(vec[:, 0], A["pool_b"][0].rearrange("g n -> (g n)").partition_broadcast(P)).then_inc(v_in, 16)
        sp.dma_start(vec[:, 1], A["pool_scale"][0].partition_broadcast(P)).then_inc(v_in, 16)
        norm1.load(sp)
        route.load(sp)
        for t in range(NT):
            sp.wait_ge(norm1.done, t + 1)
            sp.dma_start(k.h_scr[1][t * P:t * P + rows_of(t)], k.h[0:rows_of(t), t]).then_inc(stored, 16)
        sp.wait_ge(stored, 16 * NT)

    @block.tensor
    def _(pe):
        pe.wait_ge(v_in, 48)
        for t in range(NT + 1):
            if t < NT:
                R = rows_of(t)
                if t >= 2:
                    pe.wait_ge(biased, t - 1)
                for g in range(4):
                    for c in range(2):
                        last = pe.matmul(bank(k, 2 * (t % 2) + g // 2)[0:R, (g % 2) * 256:(g % 2 + 1) * 256],
                                         dT[:, 2 * g + c, t * P:t * P + R], pw[:, g, c], start=c == 0, stop=c == 1)
                last.then_inc(mixed, 1)
            if t:
                route.turn(pe, t - 1, norm1.done)
            if t >= 2:
                route.logits(pe, t - 2)
        route.logits(pe, NT - 1)
        route.pe_tables(pe)

    @block.scalar
    def _(act):
        for t in range(NT):
            norm1.normalise(act, t)
            route.keep(act.copy, act.wait_ge, t, 0)
        route.act(act)

    @block.vector
    def _(dve):
        ch = Chain(dve, k.dve_chain)
        ch.n = k.dve_n
        dve.wait_ge(v_in, 48)
        for t in range(NT + 2):
            if t < NT:
                R = rows_of(t)
                dve.wait_ge(mixed, t + 1)
                if t >= 2:
                    dve.wait_ge(joined, t - 1)
                dve.tensor_tensor(tmp[0:R, t % 2], k.ps[0:R, 1024 * (t % 2):1024 * (t % 2) + D], vec[0:R, 0], ALU.add
                                  ).then_inc(biased, 1)
            if 1 <= t <= NT:
                R = rows_of(t - 1)
                h = k.h[0:R, t - 1]
                dve.wait_ge(scaled, t)
                dve.scalar_tensor_tensor(out=h, in0=h, scalar=ALPHA, in1=tmp[0:R, (t - 1) % 2], op0=ALU.mult, op1=ALU.add
                                         ).then_inc(joined, 1)
                dve.wait_ge(joined, t)
                norm1.moments(dve, ch, t - 1)
                norm1.gain(dve, t - 1)
            if t >= 2:
                route.keep(dve.tensor_copy, dve.wait_ge, t - 2, 1)
        route.dve(dve, ch)
        k.dve_n = ch.n

    @block.gpsimd
    def _(pool):
        pool.wait_ge(v_in, 48)
        for t in range(NT):
            R = rows_of(t)
            pool.wait_ge(biased, t + 1)
            pool.tensor_tensor(tmp[0:R, t % 2], tmp[0:R, t % 2], vec[0:R, 1], ALU.mult).then_inc(scaled, 1)
            norm1.power(pool, t)
            norm1.offset(pool, t)


def finish(k, st):
    nc, A = k.nc, k.A
    join = Combine(k, st, 1)
    norm = RowNorm(k, st, "ffnnorm1", A["ln_ffn_g"][1], A["ln_ffn_b"][1])
    stored = k.sem("y_stored")
    block = st.enter_context(nc.Block())

    @block.sync
    def _(sp):
        norm.load(sp)
        for t in range(NT):
            join.load(sp, t)
        for t in range(NT):
            sp.wait_ge(norm.done, t + 1)
            dst = A["y_prompt"][0, t * P:(t + 1) * P] if t < PT else A["y_sample"][:, 0]
            sp.dma_start(dst, k.h[0:rows_of(t), t]).then_inc(stored, 16)
        sp.wait_ge(stored, 16 * NT)

    @block.scalar
    def _(act):
        for t in range(NT):
            join.scale(act, t)
        for t in range(NT):
            norm.normalise(act, t)

    @block.vector
    def _(dve):
        ch = Chain(dve, k.dve_chain)
        ch.n = k.dve_n
        for t in range(NT + 1):
            if t < NT:
                join.join(dve, ch, t)
                norm.moments(dve, ch, t)
            if t:
                norm.gain(dve, t - 1)

    @block.gpsimd
    def _(pool):
        for t in range(NT + 1):
            if t < NT:
                norm.power(pool, t)
            if t:
                norm.offset(pool, t - 1)

def program(nc, A, stages=9):
    with ExitStack() as top:
        k = Chip()
        k.nc, k.A, k.top = nc, A, top
        stage_sems = []

        def stage_sem(name):
            stage_sems.append(nc.alloc_semaphore(name=name))
            return stage_sems[-1]

        def end_stage():
            nc.clear_and_free_semaphores(stage_sems)
            stage_sems.clear()
            nc.all_engine_barrier()

        k.end_stage = end_stage
        k.sem = lambda name: top.enter_context(nc.semaphore(name))
        sb = lambda name, shape, dt=F32: top.enter_context(nc.sbuf_tensor(name, shape, dt))
        k.ps = top.enter_context(nc.psum_tensor("banks", [P, 8 * 512], F32))
        k.cst = sb("constants", [P, CONST.shape[1]])
        k.q_scr = nc.dram_tensor("sample_q", [NS, NG, AW], F32).ap()
        k.kv_scr = nc.dram_tensor("sample_kv", [NS, NG, 2, AW], F32).ap()
        k.h_scr = [nc.dram_tensor(f"rows{l}", [TOK, D], F32).ap() for l in range(2)]
        k.h = sb("h", [P, NT, D])
        k.n_ahead = (2, NW)
        k.y_scr = [nc.dram_tensor(f"results{l}", [2 * TOK, D], F32).ap() for l in range(2)]
        k.w13a = sb("expert_w13_a", [P, 2, KT, 2 * DE])
        k.w2a = sb("expert_w2_a", [P, 2, 2, D])
        k.w_moe = [[k.sem(f"experts{l}_in{i}") for i in range(NW)] for l in range(2)]
        k.gates = [sb(f"gates{l}", [P, 2, NT]) for l in range(2)]
        k.put = [sb(f"result_rows{l}", [P, NE + MAX_EXTRA], I32) for l in range(2)]
        k.get = [sb(f"token_rows{l}", [P, NE + MAX_EXTRA + 1], I32) for l in range(2)]
        k.extras = [sb(f"extra_experts{l}", [P, MAX_EXTRA + 1], I32) for l in range(2)]
        k.cst_in, k.copies = k.sem("constants_in"), k.sem("cache_copies")
        k.wo_in, k.x_again_in = k.sem("w_out_in"), k.sem("x_again_in")
        k.dve_chain, k.pool_chain, k.act_chain = k.sem("dve_chain"), k.sem("pool_chain"), k.sem("act_chain")
        k.dve_n = k.pool_n = k.act_n = 0
        k.sem = stage_sem
        with ExitStack() as mid:
            msb = lambda name, shape, dt=F32: mid.enter_context(nc.sbuf_tensor(name, shape, dt))
            k.oT = msb("oT", [P, NG, NPAIR, SEQ])
            k.glu = msb("gluT", [P, 2, 30 + SEQ])
            k.glu_s = msb("gluT_samples", [P, 2, NS])
            k.taps = msb("conv_taps", [P, 2, CW + 1])
            k.conv = msb("convT", [P, 2, TOK])
            k.nm = msb("neg_max", [P, NG, PT, NH])
            k.sums = msb("exp_sums", [P, NG, PT, NH])
            with ExitStack() as st:
                project_and_attend(k, st)
            end_stage()
            k.mixT = msb("mixT", [P, 6, TOK])
            k.wo = [k.w13a[:, 1].rearrange("p (a b) c -> p a (b c)", b=2), k.w2a[:, 1]]
            if stages > 1:
                with ExitStack() as st:
                    merge_and_convolve(k, st)
                end_stage()
            if stages > 2:
                with ExitStack() as st:
                    project_out(k, st)
                end_stage()
        with ExitStack() as mid:
            k.w13b = mid.enter_context(nc.sbuf_tensor("expert_w13_b", [P, 2, KT, 2 * DE], F32))
            k.w2b = mid.enter_context(nc.sbuf_tensor("expert_w2_b", [P, 2, 2, D], F32))
            for n, stage in ((4, lambda st: experts(k, st, 0)), (5, lambda st: pool_mixer(k, st)),
                             (6, lambda st: experts(k, st, 1)), (7, lambda st: finish(k, st))):
                if stages >= n:
                    with ExitStack() as st:
                        stage(st)
                    end_stage()


_INS = ["x_prompt", "x_sample", "cache_attn_w128", "cache_attn_w512", "cache_attn_w2048", "state_conv",
        "state_pool", "w_in", "b_in", "conv_w", "conv_b", "conv_ln_g", "conv_ln_b", "w_out", "pool_w", "pool_b",
        "pool_scale", "ln_mix_g", "ln_mix_b", "ln_ffn_g", "ln_ffn_b", "router_w", "router_bias", "moe_w1",
        "moe_w3", "moe_w2"]
_SHORT = {"cache_attn_w128": "cache0", "cache_attn_w512": "cache1", "cache_attn_w2048": "cache2"}
_OUTS = [("y_prompt", (1, 512, 1024)), ("y_sample", (8, 1, 1024)),
         ("p_attn0", (1, 1, 128, 2, 8, 64)), ("p_attn1", (1, 1, 512, 2, 8, 64)), ("p_attn2", (1, 1, 512, 2, 8, 64)),
         ("p_conv", (1, 1, 30, 256)), ("p_pool", (1, 1, 15, 1024)),
         ("s_attn0", (1, 8, 128, 2, 8, 64)), ("s_attn1", (1, 8, 512, 2, 8, 64)), ("s_attn2", (1, 8, 513, 2, 8, 64)),
         ("s_conv", (1, 8, 30, 256)), ("s_pool", (1, 8, 15, 1024))]


def kernel(**inputs):
    import numpy as _np
    import concourse.bacc as _bacc
    from concourse.bass_utils import run_bass_kernel_spmd as _run

    nc = _bacc.Bacc("TRN2", target_bir_lowering=False, num_devices=1)
    arrays, A = {}, {}
    for name in _INS:
        a = _np.ascontiguousarray(inputs[name])
        arrays[f"in_{name}"] = a
        A[_SHORT.get(name, name)] = nc.dram_tensor(f"in_{name}", a.shape, F32, kind="ExternalInput").ap()
    arrays["in_consts"] = CONST
    A["consts"] = nc.dram_tensor("in_consts", CONST.shape, F32, kind="ExternalInput").ap()
    for name, shape in _OUTS:
        A[name] = nc.dram_tensor(f"out_{name}", shape, F32, kind="ExternalOutput").ap()
    program(nc, A)
    r = _run(nc, [arrays], core_ids=[0])
    return tuple(r.results[0][f"out_{name}"] for name, _ in _OUTS)
```

```python
import math
from contextlib import ExitStack

import concourse.bass as bass
import numpy as np
from concourse import mybir

F32 = mybir.dt.float32
I32 = mybir.dt.int32
ALU = mybir.AluOpType
ACT = mybir.ActivationFunctionType
AX = mybir.AxisListType.X

P = 128
D, SEQ, NS = 1024, 512, 8
PT = SEQ // P
NT = PT + 1
KT = D // P
NG, NH, HD = 3, 8, 64
AW = NH * HD
NPAIR = NH // 2
QKV = 3 * NG * AW
CC, CW = 256, 31
RATES = (1, 4, 16)
SCALE = HD ** -0.5
NEG = -1e30
NE, DE = 16, 256
TOK = SEQ + NS
ALPHA = 4.0 ** 0.25
EPS = 1e-5
MAX_EXTRA = 8
BIG = 1e30


def rows_of(t):
    return P if t < PT else NS


def token_of(g, t, p):
    if g == 0:
        return t * P + p
    return 4 * p + t


def constants():
    c = {}
    half = HD // 4 // 2
    inv = (500000.0 ** (-np.arange(half, dtype=np.float32) * np.float32(2.0) / np.float32(16))).astype(np.float32)
    cos = np.zeros((P, 13, 16), np.float32)
    sin = np.zeros((P, 13, 16), np.float32)
    for i in range(13):
        for p in range(P):
            pos = 512 if i == 12 else token_of(i // 4, i % 4, p)
            a = (np.float32(pos) * inv).astype(np.float32)
            cos[p, i] = np.tile(np.cos(a.astype(np.float64)), 2)
            s = np.sin(a.astype(np.float64))
            sin[p, i] = np.concatenate([-s, s])
    c["cos"], c["sin"] = cos.reshape(P, -1), sin.reshape(P, -1)
    c["ident"] = np.eye(P, dtype=np.float32)
    q, k = np.arange(P)[:, None], np.arange(P)[None, :]
    c["band"] = np.where(k >= q, 0.0, NEG)
    c["causal"] = np.where(k <= q, 0.0, NEG)
    c["comb"] = np.where((k <= q) & ((q - k) % 4 == 0), 0.0, NEG)
    c["before"] = (q < k).astype(np.float32)
    c["ones"] = np.ones((P, P), np.float32)
    sel = np.zeros((P, NPAIR, P), np.float32)
    for h in range(NH):
        sel[h, h // 2, 64 * (h % 2):64 * (h % 2) + 64] = 1
    c["sel"] = sel.reshape(P, -1)
    c["slot"] = np.tile(np.arange(P, dtype=np.float32), (P, 1))
    tokval = np.zeros((P, NT, 2), np.float32)
    valid = np.zeros((P, NT), np.float32)
    for t in range(NT):
        for p in range(rows_of(t)):
            valid[p, t] = 1
            for j in range(2):
                tokval[p, t, j] = j * TOK + t * P + p + 1
    c["tokval"], c["valid"] = tokval.reshape(P, -1), valid
    c["rank4"] = np.tile(np.array([4, 3, 2, 1], np.float32), (P, 1))
    c["rank16"] = np.tile(np.arange(16, 0, -1).astype(np.float32), (P, 1))
    c["eidx"] = np.tile(np.arange(16, dtype=np.float32), (P, 1))
    c["mhalf"] = np.full((P, 1), -0.5, np.float32)
    where, at = {}, 0
    for n, a in c.items():
        where[n] = (at, a.shape[1])
        at += a.shape[1]
    return np.ascontiguousarray(np.concatenate([a.astype(np.float32) for a in c.values()], 1)), where



def pool_bands():
    p, j = np.arange(P)[:, None], np.arange(P)[None, :]
    out = np.zeros((P, len(WINDOWS), BAND), np.float32)
    for i, w in enumerate(WINDOWS):
        inside = (p <= j) & (p > j - w)
        first = np.where(inside, 1.0 / np.minimum(w, j + 1), 0.0) - (p == j)
        later = np.where(inside, 1.0 / w, 0.0) - (p == j)
        before = np.where(p - P > j - w, 1.0 / w, 0.0)[:, 0:16]
        n = np.arange(NS)[None, :]
        state = np.where((p // 15 == n) & (p % 15 >= 16 - w), 1.0 / w, 0.0)
        new = np.where(p == n, 1.0 / w - 1.0, 0.0)
        out[:, i] = np.concatenate([first, later, before, state, new], 1)
    return out.reshape(P, -1)


BAND = 2 * P + 16 + 2 * NS
WINDOWS = (2, 4, 8, 16)
CONST, WHERE = constants()
NCONST = CONST.shape[1]
CONST = np.ascontiguousarray(np.concatenate([CONST, pool_bands()], 1))


class Chain:

    def __init__(self, engine, sem):
        self.engine, self.sem, self.n = engine, sem, 0

    def link(self, ins):
        self.n += 1
        ins.then_inc(self.sem, 1)
        self.engine.wait_ge(self.sem, self.n)


class Chip:
    pass


def bank(k, i, n=1):
    return k.ps[:, i * 512:(i + n) * 512]


def cst(k, name, rows=P):
    a, n = WHERE[name]
    return k.cst[0:rows, a:a + n]


def project_and_attend(k, st):
    nc, A = k.nc, k.A
    sb = lambda name, shape, dt=F32: st.enter_context(nc.sbuf_tensor(name, shape, dt))
    flat_h = k.h[:].rearrange("p t d -> p (t d)")
    xs = k.h
    smp = flat_h[0:NS, 0:3 * NG * AW].rearrange("p (a g c) -> p a g c", a=3, g=NG)
    xT = sb("xT", [P, KT, TOK])
    W = k.w13a
    bias = sb("b_in_chunk", [P, 2, 512])
    vecs = sb("conv_rows", [40, 2 * P])
    bconv = sb("b_conv_cols", [P, 4])
    qk = sb("qk_rows", [P, 4, 512])
    V = k.w2a[:].rearrange("p s c (a n) -> p s (c a) n", a=2)
    QT = sb("qT", [P, 2, NPAIR, SEQ])
    KTT = sb("kT", [P, 2, NPAIR, SEQ])
    rope = sb("rope_parts", [P, 2, NH, 16])
    S = sb("scores", [P, 2, 512])
    PR = sb("probs", [P, 2, 512])
    PRT = sb("probsT", [P, 2, 512])
    gate = sb("glu_gate", [P, 2, TOK])
    mx = sb("row_max", [P, NG, PT, NH])
    sem = k.sem
    vecs_turned, vecs_ready = sem("conv_rows_turned"), sem("conv_rows_ready")
    x_in = [sem(f"x_in{t}") for t in range(NT)]
    x_turned, xT_ready = sem("x_turned"), sem("xT_ready")
    w_in = [sem("w_chunk0"), sem("w_chunk1")]
    proj_done, proj_taken = sem("proj_done"), sem("proj_taken")
    roped, qk_turned, qkT_ready = sem("roped"), sem("qk_turned"), sem("qkT_ready")
    kout = [sem("k_out0"), sem("k_out1")]
    v_out = [sem(f"v_out{g}") for g in range(NG)]
    scored, masked, negm, exped = sem("scored"), sem("masked"), sem("neg_max"), sem("exped")
    p_turned, pT_ready, pv_done, o_taken = sem("p_turned"), sem("pT_ready"), sem("pv_done"), sem("o_taken")
    conv_done, conv_taken = sem("conv_done"), sem("conv_taken")
    smp_out = sem("sample_out")
    copies = k.copies

    w_view = A["w_in"][0].rearrange("(k p) n -> p k n", p=P)
    NCH = 9
    col = lambda c: (c % 3) * NG * AW + (c // 3) * AW if c < NCH else QKV
    units = [(c, t) for c in range(NCH) for t in range(NT)]
    NU = len(units)
    turn = [u for u, (c, t) in enumerate(units) if c % 3 < 2 and t < PT]
    turn_no = {u: i for i, u in enumerate(turn)}
    qk_no = {u: (units[u][0] // 3) * PT + units[u][1] for u in turn}
    rope_units = [u for u, (c, t) in enumerate(units) if c % 3 < 2]
    rope_no = {u: i for i, u in enumerate(rope_units)}
    batches = []
    for g in range(NG):
        for t in range(PT):
            nh = 2 if g == 0 else 4
            for h0 in range(0, NH, 2 * nh):
                for odd in range(2):
                    batches.append((g, t, list(range(h0 + odd, h0 + 2 * nh, 2)), 2 if g == 0 else 1))
    first = {g: next(i for i, b in enumerate(batches) if b[0] == g) for g in range(NG)}
    U0 = 4
    ready_step = lambda g: U0 + 3 * NT * g + 2 * NT + 2
    step_of, at = [], 0
    for b in batches:
        at = max(at, ready_step(b[0]))
        step_of.append(at)
        at += 1
    batch_at = {s: i for i, s in enumerate(step_of)}
    STEPS = step_of[-1] + 3

    def key_blocks(b):
        g, t, _, _ = b
        if g == 0:
            return ([(t - 1, "band", 0)] if t else []) + [(t, "causal", 1)]
        return [(t, "causal" if g == 1 else "comb", 0)]

    def tile_cols(kk, g, t):
        x = xT[:, kk, 0:SEQ]
        if t == PT:
            return xT[:, kk, SEQ:TOK]
        if g == 0:
            return x[:, t * P:(t + 1) * P]
        return x.rearrange("p (i r) -> p r i", r=4)[:, t, :]

    def dram_rows(out, g, t, which):
        o = out[0, 0].rearrange("s w h e -> s w (h e)")[:, which, :]
        if g == 0:
            return o
        return o.rearrange("(i r) n -> r i n", r=4)[t]

    n_out = lambda g, t: int(g > 0 or t == PT - 1)
    kcount = {}
    run = [0, 0]
    for g in range(NG):
        for t in range(PT):
            i = g * PT + t
            run[i % 2] += 16 * n_out(g, t)
            kcount[i] = run[i % 2]
    v_total = [16 * sum(n_out(g, t) for t in range(PT)) for g in range(NG)]
    new_p = (A["p_attn0"], A["p_attn1"], A["p_attn2"])
    new_s = (A["s_attn0"], A["s_attn1"], A["s_attn2"])

    block = st.enter_context(nc.Block())

    @block.sync
    def _(sp):
        sp.dma_start(k.cst[:], A["consts"][:, 0:NCONST]).then_inc(k.cst_in, 16)
        sp.dma_start(vecs[0:CW], A["conv_w"][0]).then_inc(k.cst_in, 16)
        sp.dma_start(vecs[CW:CW + 1], A["conv_b"]).then_inc(k.cst_in, 16)
        sp.dma_start(vecs[CW + 1:CW + 3], A["b_in"][0, QKV:QKV + 512].rearrange("(c p) -> c p", p=2 * P)
                     ).then_inc(k.cst_in, 16)

        def load_chunk(n):
            c = n - 1
            if n == 2:
                sp.wait_ge(conv_done, 4)
            if n > 2:
                sp.wait_ge(proj_done, NT * (c - 1))
                sp.wait_ge(proj_taken, NT * (c - 1))
            a = QKV if n == 0 else col(c)
            sp.dma_start(W[:, n % 2], w_view[:, :, a:a + 512]).then_inc(w_in[n % 2], 16)
            if n:
                sp.dma_start(bias[:, c % 2], A["b_in"][0, a:a + 512].partition_broadcast(P)
                             ).then_inc(w_in[n % 2], 16)

        for t in range(NT):
            src = A["x_prompt"][0, t * P:(t + 1) * P] if t < PT else A["x_sample"][:, 0]
            sp.dma_start(xs[0:rows_of(t), t], src).then_inc(x_in[t], 16)
        load_chunk(0)
        load_chunk(1)
        kept = []
        for g, cache in enumerate((A["cache0"], A["cache1"], A["cache2"])):
            L = cache.shape[2]
            drop = 1 if g < 2 else 0
            for n in range(NS):
                src = cache[0, n, drop:L].rearrange("s w h e -> s (w h e)")
                kept.append((new_s[g][0, n, 0:L - drop].rearrange("s w h e -> s (w h e)"), src))
        for n in range(2, NCH + 1):
            load_chunk(n)
            for dst, src in kept[3 * (n - 2):3 * (n - 1)]:
                sp.dma_start(dst, src).then_inc(copies, 16)
        sp.wait_ge(copies, 16 * len(kept))

    @block.tensor
    def _(pe):
        ident = cst(k, "ident")
        pe.wait_ge(k.cst_in, 64)
        for cc in range(2):
            last = pe.transpose(bank(k, 4)[:, cc * 40:cc * 40 + CW + 3], vecs[0:CW + 3, cc * P:(cc + 1) * P],
                                ident[0:CW + 3, 0:CW + 3])
        last.then_inc(vecs_turned, 1)
        for t in range(NT):
            R = rows_of(t)
            pe.wait_ge(x_in[t], 16)
            if t >= 2:
                pe.wait_ge(xT_ready, t - 1)
            for kk in range(KT):
                b = 2 * (t % 2) + kk // 4
                last = pe.transpose(bank(k, b)[:, (kk % 4) * P:(kk % 4) * P + R],
                                    xs[0:R, t, kk * P:(kk + 1) * P], ident[0:R, 0:R])
            last.then_inc(x_turned, 1)
        pe.wait_ge(xT_ready, NT)

        def project(u):
            c, t = units[u]
            if t == 0:
                n = c + 1
                pe.wait_ge(w_in[n % 2], 32 * (n // 2 + 1) - (16 if n % 2 == 0 else 0))
            if u == 0:
                pe.wait_ge(conv_taken, 4)
            if u >= 2:
                pe.wait_ge(proj_taken, u - 1)
            R = rows_of(t)
            for kk in range(KT):
                last = pe.matmul(bank(k, u % 2)[0:R], tile_cols(kk, c // 3, t), W[:, (c + 1) % 2, kk],
                                 start=kk == 0, stop=kk == KT - 1)
            last.then_inc(proj_done, 1)

        def turn_qk(u):
            i = turn_no[u]
            pe.wait_ge(roped, rope_no[u] + 1)
            if i >= 1:
                pe.wait_ge(qkT_ready, i)
            src = qk[:, 2 * (units[u][0] % 3) + qk_no[u] % 2]
            for j in range(NPAIR):
                last = pe.transpose(bank(k, 2)[:, j * P:(j + 1) * P], src[:, j * P:(j + 1) * P], ident)
            last.then_inc(qk_turned, 1)

        def score(i):
            g, t, heads, nb = batches[i]
            pe.wait_ge(qkT_ready, 8 * (g + 1))
            if i >= 2:
                pe.wait_ge(masked, i - 1)
            for n, h in enumerate(heads):
                pr = slice(64 * (h % 2), 64 * (h % 2) + 64)
                blocks = key_blocks(batches[i])
                k0, k1 = blocks[0][0], blocks[-1][0] + 1
                o = (n * nb + blocks[0][2]) * P
                last = pe.matmul(bank(k, 3 + i % 2)[:, o:o + (k1 - k0) * P],
                                 QT[pr, g % 2, h // 2, t * P:(t + 1) * P],
                                 KTT[pr, g % 2, h // 2, k0 * P:k1 * P], start=True, stop=True)
            last.then_inc(scored, 1)

        def turn_probs(i):
            g, t, heads, nb = batches[i]
            pe.wait_ge(exped, i + 1)
            if i >= 1:
                pe.wait_ge(pT_ready, i)
            for n in range(len(heads)):
                for _, _, b in key_blocks(batches[i]):
                    o = (n * nb + b) * P
                    last = pe.transpose(bank(k, 5)[:, o:o + P], PR[:, i % 2, o:o + P], ident)
            last.then_inc(p_turned, 1)

        def values(i):
            g, t, heads, nb = batches[i]
            pe.wait_ge(pT_ready, i + 1)
            if heads[0] == 0 and (g or t):
                pe.wait_ge(o_taken, g * PT + t)
            for n, h in enumerate(heads):
                blocks = key_blocks(batches[i])
                for kt, _, b in blocks:
                    o = (n * nb + b) * P
                    last = pe.matmul(bank(k, 6)[64 * (h % 2):64 * (h % 2) + 64, (h // 2) * P:(h // 2 + 1) * P],
                                     V[:, g % 2, kt, h * HD:(h + 1) * HD], PRT[:, i % 2, o:o + P],
                                     start=kt == blocks[0][0], stop=kt == t)
            last.then_inc(pv_done, 1)

        def conv_cols(j):
            if j == 0:
                pe.wait_ge(w_in[0], 16)
            if j >= 2:
                pe.wait_ge(conv_taken, j - 1)
            for half in range(2):
                for kk in range(KT):
                    last = pe.matmul(bank(k, 2 * (j % 2) + half)[:, 0:TOK // 2], W[:, 0, kk, j * P:(j + 1) * P],
                                     xT[:, kk, half * (TOK // 2):(half + 1) * (TOK // 2)], start=kk == 0, stop=kk == KT - 1)
            last.then_inc(conv_done, 1)

        for s in range(STEPS):
            if s < U0:
                conv_cols(s)
            elif s < U0 + NU:
                project(s - U0)
            if s - 2 - U0 in turn_no:
                turn_qk(s - 2 - U0)
            if s in batch_at:
                score(batch_at[s])
            if s - 1 in batch_at:
                turn_probs(batch_at[s - 1])
            if s - 2 in batch_at:
                values(batch_at[s - 2])

    @block.scalar
    def _(act):
        act.wait_ge(vecs_turned, 1)
        turned = bank(k, 4)[:, 0:80].rearrange("p (c w) -> p c w", c=2)
        act.copy(k.taps[:], turned[:, :, 0:CW + 1])
        act.copy(bconv[:].rearrange("p (a c) -> p c a", a=2), turned[:, :, CW + 1:CW + 3]).then_inc(vecs_ready, 1)
        for t in range(NT):
            R = rows_of(t)
            act.wait_ge(x_turned, t + 1)
            for hh in range(2):
                src = bank(k, 2 * (t % 2) + hh).rearrange("p (k c) -> p k c", c=P)[:, :, 0:R]
                last = act.copy(xT[:, 4 * hh:4 * hh + 4, t * P:t * P + R], src)
                if hh == 1:
                    last.then_inc(xT_ready, 1)

        def keep_qkT(u):
            i = turn_no[u]
            g = units[u][0] // 3
            t = units[u][1]
            act.wait_ge(qk_turned, i + 1)
            if g == 2:
                act.wait_ge(scored, first[1])
            dst = (QT, KTT)[units[u][0] % 3]
            act.copy(dst[:, g % 2, :, t * P:(t + 1) * P],
                     bank(k, 2).rearrange("p (j c) -> p j c", c=P)).then_inc(qkT_ready, 1)

        def softmax(i):
            g, t, heads, nb = batches[i]
            act.wait_ge(negm, i + 1)
            if i >= 2:
                act.wait_ge(p_turned, i - 1)
            b0 = key_blocks(batches[i])[0][2]
            for n, h in enumerate(heads):
                cols = slice((n * nb + b0) * P, (n + 1) * nb * P)
                last = act.activation(PR[:, i % 2, cols], S[:, i % 2, cols], ACT.Exp,
                                      bias=k.nm[:, g, t, h:h + 1], scale=SCALE,
                                      accum_out=k.sums[:, g, t, h:h + 1])
            last.then_inc(exped, 1)

        def keep_pT(i):
            g, t, heads, nb = batches[i]
            act.wait_ge(p_turned, i + 1)
            if i >= 2:
                act.wait_ge(pv_done, i - 1)
            b0 = key_blocks(batches[i])[0][2]
            if b0:
                v = lambda x: x.rearrange("p (n b c) -> p n b c", n=2, b=2)[:, :, 1, :]
            else:
                v = lambda x: x
            act.copy(v(PRT[:, i % 2]), v(bank(k, 5))).then_inc(pT_ready, 1)

        def glu(j):
            act.wait_ge(conv_done, j + 1)
            if j == 0:
                act.wait_ge(vecs_ready, 1)
            fn, b, H = (ACT.Identity, ACT.Sigmoid)[j // 2], 2 * (j % 2), TOK // 2
            prompt = (k.glu[:, j % 2, 30:30 + SEQ], gate[:, j % 2, 0:SEQ])[j // 2]
            samples = (k.glu_s[:, j % 2], gate[:, j % 2, SEQ:TOK])[j // 2]
            act.activation(prompt[:, 0:H], bank(k, b)[:, 0:H], fn, bias=bconv[:, j:j + 1])
            act.activation(prompt[:, H:SEQ], bank(k, b + 1)[:, 0:SEQ - H], fn, bias=bconv[:, j:j + 1])
            act.activation(samples, bank(k, b + 1)[:, SEQ - H:H], fn, bias=bconv[:, j:j + 1]).then_inc(conv_taken, 1)

        for s in range(STEPS):
            if s < U0:
                glu(s)
            if s - 2 - U0 in turn_no:
                keep_qkT(s - 2 - U0)
            if s in batch_at:
                softmax(batch_at[s])
            if s - 1 in batch_at:
                keep_pT(batch_at[s - 1])

    @block.vector
    def _(dve):
        ch = Chain(dve, k.dve_chain)
        ch.n = k.dve_n

        def take(u):
            c, t = units[u]
            R = rows_of(t)
            dve.wait_ge(proj_done, u + 1)
            kind, g = c % 3, c // 3
            if t == PT:
                dst = smp[:, kind, g]
            elif kind == 2:
                dst = V[:, g % 2, t]
                if g == 2:
                    dve.wait_ge(pv_done, first[1])
                    dve.wait_ge(v_out[0], v_total[0])
            else:
                i = qk_no[u]
                dst = qk[:, 2 * kind + i % 2]
                if i >= 2:
                    j = turn_no[[x for x in turn if units[x][0] % 3 == kind][i - 2]]
                    dve.wait_ge(qk_turned, j + 1)
                    if kind == 1 and kcount[i - 2]:
                        dve.wait_ge(kout[i % 2], kcount[i - 2])
            dve.tensor_tensor(dst, bank(k, u % 2)[0:R], bias[0:R, c % 2], ALU.add).then_inc(proj_taken, 1)

        def mask_max(i):
            g, t, heads, nb = batches[i]
            dve.wait_ge(scored, i + 1)
            if i >= 2:
                dve.wait_ge(exped, i - 1)
            blocks = key_blocks(batches[i])
            b0 = blocks[0][2]
            a, w = WHERE["band" if b0 == 0 and nb == 2 else blocks[0][1]]
            w = w * len(blocks)
            for n, h in enumerate(heads):
                cols = slice((n * nb + b0) * P, (n + 1) * nb * P)
                last = dve.tensor_tensor_reduce(S[:, i % 2, cols], bank(k, 3 + i % 2)[:, cols], k.cst[:, a:a + w],
                                                1.0, -3e38, ALU.add, ALU.max, mx[:, g, t, h:h + 1])
            last.then_inc(masked, 1)
            dve.wait_ge(masked, i + 1)
            hs = slice(heads[0], heads[-1] + 1, 2)
            dve.tensor_scalar(k.nm[:, g, t, hs], mx[:, g, t, hs], -SCALE, None, ALU.mult).then_inc(negm, 1)

        def keep_o(i):
            g, t, heads, nb = batches[i]
            if heads[-1] != NH - 1:
                return
            dve.wait_ge(pv_done, i + 1)
            o = k.oT[:, g]
            src = bank(k, 6).rearrange("p (j c) -> p j c", c=P)
            dst = o[:, :, t * P:(t + 1) * P] if g == 0 else o.rearrange("p j (i r) -> p r j i", r=4)[:, t]
            dve.tensor_copy(dst, src).then_inc(o_taken, 1)

        def gate_glu():
            ch.link(dve.memset(k.glu[:, :, 0:30], 0.0))
            dve.wait_ge(conv_taken, 4)
            dve.tensor_tensor(k.glu[:, :, 30:30 + SEQ], k.glu[:, :, 30:30 + SEQ], gate[:, :, 0:SEQ], ALU.mult)
            ch.link(dve.tensor_tensor(k.glu_s[:], k.glu_s[:], gate[:, :, SEQ:TOK], ALU.mult))

        def tap(w):
            for cc in range(2):
                src, dst = k.glu[:, cc, w:w + SEQ], k.conv[:, cc, 0:SEQ]
                if w == 0:
                    last = dve.tensor_scalar(dst, src, k.taps[:, cc, 0:1], k.taps[:, cc, CW:CW + 1], ALU.mult, ALU.add)
                else:
                    last = dve.scalar_tensor_tensor(out=dst, in0=src, scalar=k.taps[:, cc, w:w + 1], in1=dst,
                                                    op0=ALU.mult, op1=ALU.add)
            ch.link(last)

        for s in range(STEPS):
            if U0 <= s < U0 + NU:
                take(s - U0)
            if s == U0:
                gate_glu()
            if U0 < s <= U0 + CW:
                tap(s - U0 - 1)
            if s in batch_at:
                mask_max(batch_at[s])
            if s - 2 in batch_at:
                keep_o(batch_at[s - 2])
        k.dve_n = ch.n

    @block.gpsimd
    def _(pool):
        ch = Chain(pool, k.pool_chain)
        ch.n = k.pool_n
        pool.wait_ge(k.cst_in, 64)
        cos = cst(k, "cos").rearrange("p (t c) -> p t c", c=16)
        sin = cst(k, "sin").rearrange("p (t c) -> p t c", c=16)
        smp_stores = 0
        for u in range(NU):
            c, t = units[u]
            kind, g = c % 3, c // 3
            R = rows_of(t)
            pool.wait_ge(proj_taken, u + 1)
            if kind < 2:
                row = smp[:, kind, g] if t == PT else qk[:, 2 * kind + qk_no[u] % 2]
                x = row.rearrange("p (h e) -> p h e", e=HD)[:, :, 0:16]
                ti = 12 if t == PT else 4 * g + t
                cs = cos[0:R, ti:ti + 1, :].to_broadcast([R, NH, 16])
                s0 = sin[0:R, ti:ti + 1, 0:8].to_broadcast([R, NH, 8])
                s1 = sin[0:R, ti:ti + 1, 8:16].to_broadcast([R, NH, 8])
                if rope_no[u]:
                    pool.wait_ge(roped, rope_no[u])
                pool.tensor_tensor(rope[0:R, 0], x, cs, ALU.mult)
                pool.tensor_tensor(rope[0:R, 1, :, 0:8], x[:, :, 8:16], s0, ALU.mult)
                ch.link(pool.tensor_tensor(rope[0:R, 1, :, 8:16], x[:, :, 0:8], s1, ALU.mult))
                last = pool.tensor_tensor(x, rope[0:R, 0], rope[0:R, 1], ALU.add)
                last.then_inc(roped, 1)
                if kind == 1 or t == PT:
                    pool.wait_ge(roped, rope_no[u] + 1)
            if t == PT:
                src = smp[:, kind, g]
                if kind == 0:
                    pool.dma_start(k.q_scr[:, g], src).then_inc(smp_out, 16)
                else:
                    pool.dma_start(k.kv_scr[:, g, kind - 1], src).then_inc(smp_out, 16)
                    L = new_s[g].shape[2]
                    o = new_s[g][0, :, L - 1].rearrange("n w h e -> n w (h e)")[:, kind - 1]
                    pool.dma_start(o, src).then_inc(smp_out, 16)
                    smp_stores += 1
                smp_stores += 1
            elif kind:
                i = g * PT + t
                src = qk[:, 2 + i % 2] if kind == 1 else V[:, g % 2, t]
                if n_out(g, t):
                    pool.dma_start(dram_rows(new_p[g], g, t, kind - 1), src
                                   ).then_inc(kout[i % 2] if kind == 1 else v_out[g], 16)
        pool.wait_ge(smp_out, 16 * smp_stores)
        pool.wait_ge(kout[0], run[0])
        pool.wait_ge(kout[1], run[1])
        for g in range(NG):
            pool.wait_ge(v_out[g], v_total[g])
        k.pool_n = ch.n




def merge_and_convolve(k, st):
    nc, A, sem = k.nc, k.A, k.sem
    sb = lambda name, shape, dt=F32: st.enter_context(nc.sbuf_tensor(name, shape, dt))
    NK2 = 32 + NG
    mT = sb("neg_maxT", [NH, NG, SEQ])
    lT = sb("exp_sumsT", [NH, NG, SEQ])
    mm = sb("merge_min", [NH, SEQ])
    ll = sb("merge_sum", [NH, SEQ])
    part = sb("merge_part", [P, 2, NG, SEQ])
    NI = 4
    kv = k.w13a[:, 0].rearrange("p (i g) c -> p i g c", g=2)
    kve = k.w2a[0:NK2, 0].rearrange("p a (b c) -> p (a b) c", b=2)
    qb = sb("q_broadcast", [P, NI, 2, AW])
    qe = sb("q_broadcast_last", [NK2, NI, AW])
    S = sb("sample_scores", [P, NG, NS * NH])
    PRS = sb("sample_probs", [NS * NH, 2 * P + NK2])
    small = sb("sample_small", [NS * NH, 4])
    PT_ = sb("sample_probsT", [P, NG, NS * NH])
    onec = sb("sample_rows", [P, NS, NS])
    orow = sb("sample_out", [NS, AW])
    strow = sb("state_rows", [120, 2, CC])
    stT = sb("stateT", [P, 2, NS, CW - 1])
    ssum = sb("state_sum", [P, 2, NS])
    crow = sb("conv_out_rows", [P, CC])
    grow = sb("glu_out_rows", [30, 2, CC])
    lng = sb("conv_ln", [P, 2, CC])
    stats = sb("conv_stats", [P, 2, 8])
    y = sb("conv_rows_y", [P, 2, CC])
    k_in = [sem(f"k_cached{i}") for i in range(NI)]
    v_in = [sem(f"v_cached{i}") for i in range(NI)]
    st_in = sem("state_in")
    prod, s_ready, s_turned, sp_ready, sp_turned, spT = (sem(n) for n in (
        "k_times_q", "s_scored", "s_scores_turned", "s_probs_ready", "s_probs_turned", "s_probsT_ready"))
    merged, mixed, taken = sem("pairs_merged"), sem("prompt_mixed"), sem("prompt_mixed_taken")
    vprod_g, vprod_d = sem("p_times_v_group1"), sem("p_times_v_joined")
    vprod, v_summed, o_row, o_rowT, o_rowT_kept = (sem(n) for n in ("p_times_v", "v_summed", "o_row", "o_row_turned", "o_row_kept"))
    e_neg, e_exp = sem("merge_shift"), sem("merge_exp")
    m_turned, m_kept, f_ready, f_spread, f_used = (sem(n) for n in ("max_turned", "max_kept", "weights_ready", "weights_spread", "weights_used"))
    c_turned, c_kept, c_var, c_pow, c_lin, c_act, c_back, c_backk = (sem(n) for n in (
        "conv_turned", "conv_kept", "conv_var", "conv_rstd", "conv_lin", "conv_silu", "conv_back", "conv_back_kept"))
    st_turned, st_kept, g_turned, g_kept, out2, ones_in = (sem(n) for n in (
        "state_turned", "state_kept", "glu_turned", "glu_kept", "stage2_out", "sample_rows_in"))
    caches = (A["cache0"], A["cache1"], A["cache2"])


    def keep_heads(copy, dst, bank0):
        for g in range(NG):
            d = dst[:, g] if g == 0 else dst[:, g].rearrange("p (i r) -> p r i", r=4)
            s_ = bank(k, bank0 + g)[0:NH]
            s_ = s_ if g == 0 else s_.rearrange("p (r i) -> p r i", r=4)
            copy(d, s_).then_inc(m_kept, 1)

    block = st.enter_context(nc.Block())

    @block.sync
    def _(sp):
        sp.dma_start(lng[:, 0], A["conv_ln_g"][0].partition_broadcast(P)).then_inc(st_in, 16)
        sp.dma_start(lng[:, 1], A["conv_ln_b"][0].partition_broadcast(P)).then_inc(st_in, 16)
        for i in range(2):
            sp.dma_start(strow[:, i], A["state_conv"][0, 4 * i:4 * i + 4].rearrange("n w c -> (n w) c")
                         ).then_inc(st_in, 16)
        for which in range(2):
            for n in range(NS):
                i = n % NI
                done = (k_in, v_in)[which][i]
                if which == 0 and n >= NI:
                    sp.wait_ge(s_ready, 2 * (n - NI + 1))
                if which == 1 and n < NI:
                    sp.wait_ge(s_ready, 2 * (NS - NI + n + 1))
                if which == 1 and n >= NI:
                    sp.wait_ge(vprod, n - NI + 1)
                    sp.wait_ge(vprod_d, 2 * (n - NI + 1))
                for g in range(2):
                    src = caches[g][0, n].rearrange("s w h e -> s w (h e)")[:, which]
                    if g:
                        src = src.rearrange("(i r) c -> r i c", r=RATES[g])[0]
                    sp.dma_start(kv[:, i, g], src).then_inc(done, 16)
                src = caches[2][0, n].rearrange("s w h e -> s w (h e)")[:, which]
                sp.dma_start(kve[0:32, i], src.rearrange("(i r) c -> r i c", r=RATES[2])[0]).then_inc(done, 16)
                sp.dma_start(kve[32:NK2, i], k.kv_scr[n, :, which]).then_inc(done, 16)
                if which == 0:
                    sp.dma_start(qb[:, i], k.q_scr[n, 0:2].partition_broadcast(P)).then_inc(done, 16)
                    sp.dma_start(qe[0:32, i], k.q_scr[n, 2].partition_broadcast(32)).then_inc(done, 16)
                    sp.dma_start(qe[32:NK2, i], k.q_scr[n]).then_inc(done, 16)
                if (which, n) != (0, NI - 1):
                    continue
                src = A["w_out"][0].rearrange("(k p) n -> p k n", p=P)
                sp.dma_start(k.wo[0], src[:, 0:4]).then_inc(k.wo_in, 16)
                sp.dma_start(k.wo[1], src[:, 4:6]).then_inc(k.wo_in, 16)
                sp.dma_start(k.h[:, 0:PT], A["x_prompt"][0].rearrange("(t p) d -> p t d", p=P)).then_inc(k.x_again_in, 16)
                sp.dma_start(k.h[0:NS, PT], A["x_sample"][:, 0]).then_inc(k.x_again_in, 16)
        sp.dma_start(A["s_conv"][0, :, 0:CW - 2], A["state_conv"][0, :, 1:CW - 1]).then_inc(out2, 16)
        sp.wait_ge(g_kept, 2)
        sp.dma_start(A["p_conv"][0, 0], grow[:, 0]).then_inc(out2, 16)
        sp.dma_start(A["s_conv"][0, :, CW - 2], grow[0:NS, 1]).then_inc(out2, 16)
        sp.wait_ge(out2, 48)

    @block.tensor
    def _(pe):
        ident = cst(k, "ident")
        for j, src in enumerate((k.nm, k.sums)):
            for g in range(NG):
                for t in range(PT):
                    last = pe.transpose(bank(k, 3 * j + g)[0:NH, t * P:(t + 1) * P], src[:, g, t], ident)
        last.then_inc(m_turned, 1)
        for cc in range(2):
            pe.transpose(bank(k, 6)[0:30, cc * P:(cc + 1) * P], k.glu[:, cc, SEQ:SEQ + 30], ident)
            last = pe.transpose(bank(k, 6)[0:NS, CC + cc * P:CC + (cc + 1) * P], k.glu_s[:, cc], ident)
        last.then_inc(g_turned, 1)
        pe.wait_ge(st_in, 64)
        for cc in range(2):
            for i in range(2):
                last = pe.transpose(bank(k, 7)[:, cc * 256 + i * 120:cc * 256 + (i + 1) * 120],
                                    strow[:, i, cc * P:(cc + 1) * P], ident[0:120, 0:120])
        last.then_inc(st_turned, 1)
        pe.wait_ge(m_kept, 6)
        pe.wait_ge(g_kept, 2)
        pe.wait_ge(st_kept, 1)

        def conv_row(t):
            R = rows_of(t)
            if t >= 2:
                pe.wait_ge(c_kept, t - 1)
            for cc in range(2):
                last = pe.transpose(bank(k, 3 + t % 2)[0:R, cc * P:(cc + 1) * P],
                                    k.conv[:, cc, t * P:t * P + R], ident)
            last.then_inc(c_turned, 1)

        def conv_back(t):
            R = rows_of(t)
            pe.wait_ge(c_act, t + 1)
            if t >= 2:
                pe.wait_ge(c_backk, t - 1)
            for cc in range(2):
                last = pe.transpose(bank(k, 5 + t % 2)[:, cc * P:cc * P + R], y[0:R, t % 2, cc * P:(cc + 1) * P],
                                    ident[0:R, 0:R])
            last.then_inc(c_back, 1)

        def spread(j):
            for g in range(NG):
                if j:
                    pe.wait_ge(f_used, NG * (j - 1) + g + 1)
                pe.matmul(bank(k, g), cst(k, "sel", NH)[:, j * P:(j + 1) * P], lT[:, g], start=True, stop=True
                          ).then_inc(f_spread, 1)

        def project(t):
            if t == 0:
                pe.wait_ge(k.wo_in, 32)
                pe.wait_ge(merged, NPAIR)
                pe.wait_ge(c_backk, NT)
            if t >= 2:
                pe.wait_ge(taken, 2 * (t - 1))
            for hh in range(2):
                for kk in range(6):
                    last = pe.matmul(bank(k, 3 + 2 * (t % 2) + hh), k.mixT[:, kk, t * P:(t + 1) * P],
                                     k.wo[kk // 4][:, kk % 4, 512 * hh:512 * hh + 512], start=kk == 0, stop=kk == 5)
                last.then_inc(mixed, 1)

        conv_row(0)
        pe.wait_ge(f_ready, 1)
        for t in range(NT):
            if t < NPAIR:
                spread(t)
            if t + 1 < NT:
                conv_row(t + 1)
            conv_back(t)
        project(0)
        project(1)
        pe.wait_ge(s_ready, 2 * NS)
        for g in range(NG):
            n = P if g < 2 else NK2
            last = pe.transpose(bank(k, 7)[0:NS * NH, g * P:g * P + n], S[0:n, g], ident[0:n, 0:n])
        last.then_inc(s_turned, 1)
        project(2)
        pe.wait_ge(sp_ready, 1)
        for g in range(NG):
            n = P if g < 2 else NK2
            last = pe.transpose(bank(k, 0)[0:n, g * 64:(g + 1) * 64], PRS[:, g * P:g * P + n], ident[0:64, 0:64])
        last.then_inc(sp_turned, 1)
        pe.wait_ge(ones_in, 1 + NS)
        for n in range(NS):
            if n == 0:
                project(3)
            pe.wait_ge(vprod_d, 2 * (n + 1))
            i = n % NI
            pe.matmul(bank(k, 1)[0:NS], onec[:, n], qb[:, i, 1], start=n == 0, stop=False)
            pe.matmul(bank(k, 1)[0:NS], onec[0:NK2, n], qe[:, i], start=False, stop=n == NS - 1).then_inc(v_summed, 1)
        pe.wait_ge(o_row, 1)
        for j in range(NPAIR):
            last = pe.transpose(bank(k, 0)[:, 192 + j * NS:192 + (j + 1) * NS], orow[:, j * P:(j + 1) * P],
                                ident[0:NS, 0:NS])
        last.then_inc(o_rowT, 1)

    @block.scalar
    def _(act):
        act.wait_ge(m_turned, 1)
        keep_heads(act.copy, lT, 3)
        act.wait_ge(g_turned, 1)
        act.copy(grow[:, 0], bank(k, 6)[0:30, 0:CC]).then_inc(g_kept, 1)
        act.copy(grow[0:NS, 1], bank(k, 6)[0:NS, CC:2 * CC]).then_inc(g_kept, 1)
        act.wait_ge(e_neg, 1)
        act.activation(mT[:], mT[:], ACT.Exp).then_inc(e_exp, 1)
        for t in range(NT):
            R = rows_of(t)
            act.wait_ge(c_lin, t + 1)
            if t >= 2:
                act.wait_ge(c_back, t - 1)
            act.activation(y[0:R, t % 2], crow[0:R], ACT.Silu).then_inc(c_act, 1)
            act.wait_ge(c_back, t + 1)
            src = bank(k, 5 + t % 2)[:, 0:CC].rearrange("p (c n) -> p c n", c=2)[:, :, 0:R]
            act.copy(k.mixT[:, 4:6, t * P:t * P + R], src).then_inc(c_backk, 1)
        act.wait_ge(e_neg, 2)
        act.activation(PRS[:], bank(k, 7)[0:64, 0:2 * P + NK2], ACT.Exp, bias=small[:, 1:2], scale=SCALE,
                       accum_out=small[:, 2:3]).then_inc(e_exp, 1)

    @block.vector
    def _(dve):
        ch = Chain(dve, k.dve_chain)
        ch.n = k.dve_n
        dve.wait_ge(m_turned, 1)
        keep_heads(dve.tensor_copy, mT, 0)
        dve.wait_ge(m_kept, 6)
        dve.wait_ge(st_turned, 1)
        dve.tensor_copy(stT[:], bank(k, 7).rearrange("p (c m) -> p c m", c=2)[:, :, 0:240]
                        .rearrange("p c (n w) -> p c n w", n=NS)).then_inc(st_kept, 1)
        dve.wait_ge(st_kept, 1)

        def sample_conv():
            for cc in range(2):
                last = dve.tensor_tensor(stT[:, cc], stT[:, cc], k.taps[:, cc:cc + 1, 0:CW - 1].to_broadcast([P, NS, CW - 1]),
                                         ALU.mult)
            ch.link(last)
            ch.link(dve.tensor_reduce(ssum[:], stT[:], AX, ALU.add))
            for cc in range(2):
                last = dve.scalar_tensor_tensor(out=ssum[:, cc], in0=k.glu_s[:, cc], scalar=k.taps[:, cc, CW - 1:CW],
                                                in1=ssum[:, cc], op0=ALU.mult, op1=ALU.add)
            ch.link(last)
            for cc in range(2):
                last = dve.tensor_scalar(k.conv[:, cc, SEQ:TOK], ssum[:, cc], k.taps[:, cc, CW:CW + 1], None, ALU.add)
            last.then_inc(st_kept, 1)

        def merge_shift():
            ch.link(dve.tensor_tensor(mm[:], mT[:, 0], mT[:, 1], ALU.min))
            ch.link(dve.tensor_tensor(mm[:], mm[:], mT[:, 2], ALU.min))
            for g in range(NG):
                last = dve.tensor_tensor(mT[:, g], mm[:], mT[:, g], ALU.subtract)
            last.then_inc(e_neg, 1)

        def merge_weights():
            dve.wait_ge(e_exp, 1)
            ch.link(dve.tensor_tensor(lT[:], lT[:], mT[:], ALU.mult))
            ch.link(dve.tensor_tensor(ll[:], lT[:, 0], lT[:, 1], ALU.add))
            ch.link(dve.tensor_tensor(ll[:], ll[:], lT[:, 2], ALU.add))
            ch.link(dve.reciprocal(ll[:], ll[:]))
            for g in range(NG):
                last = dve.tensor_tensor(lT[:, g], mT[:, g], ll[:], ALU.mult)
            last.then_inc(f_ready, 1)

        def conv_norm(t):
            R = rows_of(t)
            dve.wait_ge(c_turned, t + 1)
            row = bank(k, 3 + t % 2)[0:R, 0:CC]
            ch.link(dve.bn_stats(stats[0:R, t % 2, 0:6], row))
            ch.link(dve.bn_aggr(stats[0:R, t % 2, 6:8], stats[0:R, t % 2, 0:6]))
            dve.tensor_scalar(stats[0:R, t % 2, 7:8], stats[0:R, t % 2, 7:8], EPS, None, ALU.add).then_inc(c_var, 1)
            dve.wait_ge(c_pow, t + 1)
            if t:
                dve.wait_ge(c_act, t)
            ch.link(dve.tensor_scalar(crow[0:R], row, stats[0:R, t % 2, 6:7], stats[0:R, t % 2, 0:1],
                                      ALU.subtract, ALU.mult))
            dve.engine_nop().then_inc(c_kept, 1)
            ch.link(dve.tensor_tensor(crow[0:R], crow[0:R], lng[0:R, 0], ALU.mult))
            dve.tensor_tensor(crow[0:R], crow[0:R], lng[0:R, 1], ALU.add).then_inc(c_lin, 1)

        def sample_scores(n):
            i = n % NI
            dve.wait_ge(k_in[i], 7 * 16 * (n // NI + 1))
            ch.link(dve.tensor_tensor(qe[:, i], kve[:, i], qe[:, i], ALU.mult))
            dve.wait_ge(prod, n + 1)
            dve.tensor_reduce(S[:, 0:2, n * NH:(n + 1) * NH], qb[:, i].rearrange("p g (h e) -> p g h e", e=HD), AX,
                              ALU.add).then_inc(s_ready, 1)
            dve.tensor_reduce(S[0:NK2, 2, n * NH:(n + 1) * NH], qe[:, i].rearrange("p (h e) -> p h e", e=HD), AX,
                              ALU.add).then_inc(s_ready, 1)

        def merge(j):
            for g in range(NG):
                dve.wait_ge(f_spread, NG * j + g + 1)
                last = dve.tensor_tensor(part[:, j % 2, g], bank(k, g), k.oT[:, g, j], ALU.mult)
                last.then_inc(f_used, 1)
            dve.wait_ge(f_used, NG * (j + 1))
            ch.link(dve.tensor_tensor(part[:, j % 2, 0], part[:, j % 2, 0], part[:, j % 2, 1], ALU.add))
            dve.tensor_tensor(k.mixT[:, j, 0:SEQ], part[:, j % 2, 0], part[:, j % 2, 2], ALU.add).then_inc(merged, 1)

        def take(t):
            for hh in range(2):
                dve.wait_ge(mixed, 2 * t + hh + 1)
                z = k.h[:, t, 512 * hh:512 * hh + 512]
                dve.scalar_tensor_tensor(out=z, in0=z, scalar=ALPHA, in1=bank(k, 3 + 2 * (t % 2) + hh),
                                         op0=ALU.mult, op1=ALU.add).then_inc(taken, 1)

        merge_shift()
        sample_conv()
        dve.wait_ge(st_in, 64)
        conv_norm(0)
        merge_weights()
        sample_scores(0)
        for t in range(NT):
            if t < NPAIR:
                merge(t)
            if t + 1 < NT:
                conv_norm(t + 1)
        dve.wait_ge(k.x_again_in, 32)
        for n in range(1, NS):
            if n == NS // 2:
                take(0)
            sample_scores(n)
        take(1)
        dve.wait_ge(s_turned, 1)
        ch.link(dve.tensor_reduce(small[:, 0:1], bank(k, 7)[0:64, 0:2 * P + NK2], AX, ALU.max))
        dve.tensor_scalar(small[:, 1:2], small[:, 0:1], -SCALE, None, ALU.mult).then_inc(e_neg, 1)
        dve.wait_ge(e_exp, 2)
        ch.link(dve.reciprocal(small[:, 3:4], small[:, 2:3]))
        dve.tensor_scalar(PRS[:], PRS[:], small[:, 3:4], None, ALU.mult).then_inc(sp_ready, 1)
        dve.wait_ge(sp_turned, 1)
        dve.tensor_copy(PT_[:, 0:2], bank(k, 0)[:, 0:128].rearrange("p (g m) -> p g m", g=2)).then_inc(spT, 1)
        dve.tensor_copy(PT_[0:NK2, 2], bank(k, 0)[0:NK2, 128:192]).then_inc(spT, 1)
        dve.wait_ge(spT, 2)
        for n in range(NS):
            if n == NI:
                take(2)
            i = n % NI
            dve.wait_ge(v_in[i], 4 * 16 * (n // NI + 1))
            if n >= NI:
                dve.wait_ge(v_summed, n - NI + 1)
            w = PT_[:, 1, n * NH:(n + 1) * NH].unsqueeze(2).to_broadcast([P, NH, HD])
            dve.tensor_tensor(qb[:, i, 1].rearrange("p (h e) -> p h e", e=HD),
                              kv[:, i, 1].rearrange("p (h e) -> p h e", e=HD), w, ALU.mult).then_inc(vprod_g, 1)
            w = PT_[0:NK2, 2, n * NH:(n + 1) * NH].unsqueeze(2).to_broadcast([NK2, NH, HD])
            dve.tensor_tensor(qe[:, i].rearrange("p (h e) -> p h e", e=HD),
                              kve[:, i].rearrange("p (h e) -> p h e", e=HD), w, ALU.mult).then_inc(vprod_d, 1)
            dve.wait_ge(vprod_g, n + 1)
            dve.wait_ge(vprod, n + 1)
            dve.tensor_tensor(qb[:, i, 1], qb[:, i, 1], qb[:, i, 0], ALU.add).then_inc(vprod_d, 1)
        take(3)
        dve.wait_ge(v_summed, NS)
        dve.tensor_copy(orow[:], bank(k, 1)[0:NS]).then_inc(o_row, 1)
        dve.wait_ge(o_rowT, 1)
        dve.tensor_copy(k.mixT[:, 0:4, SEQ:TOK], bank(k, 0)[:, 192:192 + NPAIR * NS].rearrange("p (j n) -> p j n", n=NS)
                        ).then_inc(o_rowT_kept, 1)
        k.dve_n = ch.n

    @block.gpsimd
    def _(pool):
        pool.memset(onec[:], 0.0).then_inc(ones_in, 1)
        pool.wait_ge(ones_in, 1)
        for n in range(NS):
            pool.memset(onec[:, n, n:n + 1], 1.0).then_inc(ones_in, 1)

        def times_q(n):
            i = n % NI
            pool.wait_ge(k_in[i], 7 * 16 * (n // NI + 1))
            pool.tensor_tensor(qb[:, i], kv[:, i], qb[:, i], ALU.mult).then_inc(prod, 1)

        def rstd(t):
            R = rows_of(t)
            pool.wait_ge(c_var, t + 1)
            pool.tensor_tensor(stats[0:R, t % 2, 0:1], stats[0:R, t % 2, 7:8], cst(k, "mhalf", R), ALU.pow).then_inc(c_pow, 1)

        times_q(0)
        rstd(0)
        times_q(1)
        for t in range(1, NT):
            rstd(t)
            if t < 3:
                times_q(1 + t)
        for n in range(NI, NS):
            times_q(n)
        pool.wait_ge(spT, 2)
        for n in range(NS):
            i = n % NI
            pool.wait_ge(v_in[i], 4 * 16 * (n // NI + 1))
            pool.wait_ge(s_ready, 2 * NS)
            if n >= NI:
                pool.wait_ge(v_summed, n - NI + 1)
            w = PT_[:, 0, n * NH:(n + 1) * NH].unsqueeze(2).to_broadcast([P, NH, HD])
            pool.tensor_tensor(qb[:, i, 0].rearrange("p (h e) -> p h e", e=HD),
                               kv[:, i, 0].rearrange("p (h e) -> p h e", e=HD), w, ALU.mult).then_inc(vprod, 1)


class RowNorm:

    def __init__(self, k, st, name, g_dram, b_dram):
        self.k, self.name, self.g_dram, self.b_dram = k, name, g_dram, b_dram
        sb = lambda n, shape: st.enter_context(k.nc.sbuf_tensor(f"{name}_{n}", shape, F32))
        self.gb = sb("gain_shift", [P, 2, D])
        self.stats = sb("stats", [P, NT, 16])
        (self.gb_in, self.var, self.rstd, self.shift, self.normed, self.scaled, self.done) = (
            k.sem(f"{name}_{n}") for n in ("gain_in", "var", "rstd", "shift", "normed", "scaled", "done"))

    def load(self, sp):
        sp.dma_start(self.gb[:, 0], self.g_dram.partition_broadcast(P)).then_inc(self.gb_in, 16)
        sp.dma_start(self.gb[:, 1], self.b_dram.partition_broadcast(P)).then_inc(self.gb_in, 16)

    def moments(self, dve, ch, t):
        R, s = rows_of(t), self.stats
        for hh in range(2):
            last = dve.bn_stats(s[0:R, t, 6 * hh:6 * hh + 6], self.k.h[0:R, t, 512 * hh:512 * hh + 512])
        ch.link(last)
        ch.link(dve.bn_aggr(s[0:R, t, 12:14], s[0:R, t, 0:12]))
        dve.tensor_scalar(s[0:R, t, 13:14], s[0:R, t, 13:14], EPS, None, ALU.add).then_inc(self.var, 1)
        if t:
            self.gain(dve, t - 1)
        dve.wait_ge(self.rstd, t + 1)
        dve.scalar_tensor_tensor(out=s[0:R, t, 15:16], in0=s[0:R, t, 12:13], scalar=-1.0, in1=s[0:R, t, 14:15],
                                 op0=ALU.mult, op1=ALU.mult).then_inc(self.shift, 1)

    def power(self, pool, t):
        R, s = rows_of(t), self.stats
        pool.wait_ge(self.var, t + 1)
        pool.tensor_tensor(s[0:R, t, 14:15], s[0:R, t, 13:14], cst(self.k, "mhalf", R), ALU.pow).then_inc(self.rstd, 1)

    def normalise(self, act, t):
        R, s, h = rows_of(t), self.stats, self.k.h
        act.wait_ge(self.shift, t + 1)
        act.activation(h[0:R, t], h[0:R, t], ACT.Identity, bias=s[0:R, t, 15:16], scale=s[0:R, t, 14:15]
                       ).then_inc(self.normed, 1)

    def gain(self, dve, t):
        R, h = rows_of(t), self.k.h
        if t == 0:
            dve.wait_ge(self.gb_in, 32)
        dve.wait_ge(self.normed, t + 1)
        dve.tensor_tensor(h[0:R, t], h[0:R, t], self.gb[0:R, 0], ALU.mult).then_inc(self.scaled, 1)

    def offset(self, pool, t):
        R, h = rows_of(t), self.k.h
        pool.wait_ge(self.scaled, t + 1)
        if t == 0:
            pool.wait_ge(self.gb_in, 32)
        pool.tensor_tensor(h[0:R, t], h[0:R, t], self.gb[0:R, 1], ALU.add).then_inc(self.done, 1)


class Router:

    def __init__(self, k, st, l):
        self.k, self.l = k, l
        sb = lambda n, shape, dt=F32: st.enter_context(k.nc.sbuf_tensor(f"route{l}_{n}", shape, dt))
        F16 = mybir.dt.float16
        self.rw, self.rb = sb("w", [P, KT, NE]), sb("bias", [P, NE])
        self.hT = sb("hT", [P, KT, TOK])
        self.LG = sb("logits", [P, NT, NE])
        self.sc, self.sel, self.tmp = sb("scores", [P, NT, NE]), sb("selection", [P, NT, NE]), sb("tmp", [P, NT, NE])
        self.pairs, self.grp, self.gw = sb("pairs", [P, NT * 4, 6]), sb("groups", [P, NT, 4]), sb("group_pick", [P, NT, 4])
        self.oh, self.A = sb("one_hot", [P, 2, NT, NE]), sb("chosen", [P, NT, NE])
        self.C, self.tot = sb("earlier", [P, NT, NE]), sb("all_chosen", [P, NE])
        self.m5, self.rank = sb("per_token", [P, 4, NT]), sb("rank", [P, 2, 2, NT])
        self.beyond, self.part = sb("rank_beyond", [P, 6, 2 * NT]), sb("rank_part", [P, 5, 2 * NT])
        self.val = sb("token_value", [P, 2, NT, NE])
        self.valr = sb("token_value_by_part", [P, 2 * NT, 5, NE], F16)
        self.SL = sb("slot_one_hot", [P, 2 * NT, P], F16)
        self.flag = sb("flags", [P, 2, NE])
        (self.w_in, self.turned, self.kept, self.lg, self.shifted, self.exped, self.chosen,
         self.ranked, self.slots, self.tabled, self.ready) = (k.sem(f"route{l}_{n}") for n in (
             "w_in", "turned", "kept", "logits_ready", "shifted", "exped", "chosen_ready",
             "ranked", "slots", "tabled", "ready"))

    def load(self, sp):
        sp.dma_start(self.rw[:], self.k.A["router_w"].rearrange("(k p) e -> p k e", p=P)).then_inc(self.w_in, 16)
        sp.dma_start(self.rb[:], self.k.A["router_bias"].partition_broadcast(P)).then_inc(self.w_in, 16)

    def turn(self, pe, t, done):
        k, R = self.k, rows_of(t)
        pe.wait_ge(done, t + 1)
        if t:
            pe.wait_ge(self.kept, 2 * t)
        for kk in range(KT):
            last = pe.transpose(bank(k, 4 + kk // 4)[:, (kk % 4) * P:(kk % 4) * P + R],
                                k.h[0:R, t, kk * P:(kk + 1) * P], cst(k, "ident", R)[:, 0:R])
        last.then_inc(self.turned, 1)

    def keep(self, engine_copy, wait, t, half):
        k, R = self.k, rows_of(t)
        wait(self.turned, t + 1)
        src = bank(k, 4 + half).rearrange("p (k c) -> p k c", c=P)[:, :, 0:R]
        engine_copy(self.hT[:, 4 * half:4 * half + 4, t * P:t * P + R], src).then_inc(self.kept, 1)

    def logits(self, pe, t):
        k, R = self.k, rows_of(t)
        pe.wait_ge(self.kept, 2 * (t + 1))
        if t == 0:
            pe.wait_ge(self.w_in, 32)
        for kk in range(KT):
            last = pe.matmul(bank(k, 7)[0:R, t * NE:(t + 1) * NE], self.hT[:, kk, t * P:t * P + R], self.rw[:, kk],
                             start=kk == 0, stop=kk == KT - 1)
        last.then_inc(self.lg, 1)

    def pe_tables(self, pe):
        k = self.k
        pe.wait_ge(self.chosen, 1)
        flat = lambda x: x[:].rearrange("p t e -> p (t e)")
        pe.matmul(bank(k, 6)[:, 0:NT * NE], cst(k, "before"), flat(self.A), start=True, stop=False)
        pe.matmul(bank(k, 6)[:, 0:NT * NE], cst(k, "ones"), flat(self.C), start=False, stop=True)
        pe.matmul(bank(k, 6)[:, NT * NE:(NT + 1) * NE], cst(k, "ones"), self.tot[:], start=True, stop=True
                  ).then_inc(self.ranked, 1)
        pe.wait_ge(self.slots, 1)
        for n in range(2 * NT):
            last = pe.matmul(bank(k, 7)[:, 256:256 + 5 * NE], self.SL[:, n], self.valr[:, n].rearrange("p r e -> p (r e)"),
                             start=n == 0, stop=n == 2 * NT - 1)
        last.then_inc(self.tabled, 1)

    def act(self, act):
        act.wait_ge(self.shifted, 1)
        act.activation(self.sc[:], self.sc[:], ACT.Exp).then_inc(self.exped, 1)

    def dve(self, dve, ch):
        k, l, L = self.k, self.l, ch.link
        tt = dve.tensor_tensor
        b3 = lambda x, n: x.unsqueeze(2).to_broadcast([P, x.shape[1], n])
        tokens = lambda name, n: cst(k, name).unsqueeze(1).to_broadcast([P, NT, n])
        m5 = self.m5
        dve.memset(self.beyond[:, 0], 1.0)
        dve.memset(self.beyond[:, 5], 0.0)
        L(dve.memset(self.LG[:], 0.0))
        dve.wait_ge(self.lg, NT)
        dve.tensor_copy(self.LG[:, 0:PT], bank(k, 7)[:, 0:PT * NE].rearrange("p (t e) -> p t e", e=NE))
        L(dve.tensor_copy(self.LG[0:NS, PT], bank(k, 7)[0:NS, PT * NE:NT * NE]))
        L(dve.tensor_reduce(m5[:, 0], self.LG[:], AX, ALU.max))
        tt(self.sc[:], self.LG[:], b3(m5[:, 0], NE), ALU.subtract).then_inc(self.shifted, 1)
        dve.wait_ge(self.exped, 1)
        L(dve.tensor_reduce(m5[:, 1], self.sc[:], AX, ALU.add))
        L(dve.reciprocal(m5[:, 1], m5[:, 1]))
        L(tt(self.sc[:], self.sc[:], b3(m5[:, 1], NE), ALU.mult))
        dve.wait_ge(self.w_in, 32)
        L(tt(self.sel[:], self.sc[:], self.rb[:].unsqueeze(1).to_broadcast([P, NT, NE]), ALU.add))
        s4 = self.sel[:].rearrange("p t (g e) -> p (t g) e", e=4)
        tt(self.pairs[:, :, 0:3], s4[:, :, 0:3], s4[:, :, 1:4], ALU.add)
        tt(self.pairs[:, :, 3:5], s4[:, :, 0:2], s4[:, :, 2:4], ALU.add)
        L(tt(self.pairs[:, :, 5:6], s4[:, :, 0:1], s4[:, :, 3:4], ALU.add))
        L(dve.tensor_reduce(self.grp[:].rearrange("p t g -> p (t g)"), self.pairs[:], AX, ALU.max))

        def first_max(vals, pick, tmp, order, n):
            L(dve.tensor_reduce(m5[:, 2], vals, AX, ALU.max))
            L(tt(tmp, vals, b3(m5[:, 2], n), ALU.is_equal))
            L(tt(tmp, tmp, tokens(order, n), ALU.mult))
            L(dve.tensor_reduce(m5[:, 3], tmp, AX, ALU.max))
            L(tt(pick, tmp, b3(m5[:, 3], n), ALU.is_equal))

        first_max(self.grp[:], self.gw[:], self.grp[:], "rank4", 4)
        g4 = self.gw[:].unsqueeze(3).to_broadcast([P, NT, 4, 4])
        L(tt(self.sel[:].rearrange("p t (g e) -> p t g e", e=4), self.sel[:].rearrange("p t (g e) -> p t g e", e=4), g4,
             ALU.mult))
        L(dve.tensor_scalar(self.gw[:], self.gw[:], BIG, -BIG, ALU.mult, ALU.add))
        L(tt(self.sel[:].rearrange("p t (g e) -> p t g e", e=4), self.sel[:].rearrange("p t (g e) -> p t g e", e=4), g4,
             ALU.add))
        first_max(self.sel[:], self.oh[:, 0], self.tmp[:], "rank16", NE)
        L(dve.scalar_tensor_tensor(out=self.sel[:], in0=self.oh[:, 0], scalar=-4 * BIG, in1=self.sel[:], op0=ALU.mult,
                                   op1=ALU.add))
        first_max(self.sel[:], self.oh[:, 1], self.tmp[:], "rank16", NE)
        valid = cst(k, "valid").unsqueeze(2).to_broadcast([P, NT, NE])
        for j in range(2):
            last = tt(self.oh[:, j], self.oh[:, j], valid, ALU.mult)
        L(last)
        L(tt(self.A[:], self.oh[:, 0], self.oh[:, 1], ALU.add))
        L(dve.memset(self.C[:, 0], 0.0))
        for t in range(1, NT):
            L(tt(self.C[:, t], self.C[:, t - 1], self.A[:, t - 1], ALU.add))
        tt(self.tot[:], self.C[:, NT - 1], self.A[:, NT - 1], ALU.add).then_inc(self.chosen, 1)
        for j in range(2):
            L(tt(self.tmp[:], self.sc[:], self.oh[:, j], ALU.mult))
            L(dve.tensor_reduce(k.gates[l][:, j], self.tmp[:], AX, ALU.add))
        tv = cst(k, "tokval").rearrange("p (t j) -> p j t", j=2)
        for j in range(2):
            last = tt(self.val[:, j], self.oh[:, j], tv[:, j].unsqueeze(2).to_broadcast([P, NT, NE]), ALU.mult)
        L(last)
        dve.wait_ge(self.ranked, 1)
        rk = bank(k, 6)[:, 0:NT * NE].rearrange("p (t e) -> p t e", e=NE)
        for j in range(2):
            L(tt(self.tmp[:], self.oh[:, j], rk, ALU.mult))
            L(dve.tensor_reduce(self.rank[:, 0, j], self.tmp[:], AX, ALU.add))
        dve.tensor_copy(k.counts[:], bank(k, 6)[:, NT * NE:(NT + 1) * NE])
        rank, slot = (self.rank[:, i].rearrange("p j t -> p (j t)") for i in range(2))
        for r in range(1, 5):
            last = dve.tensor_scalar(self.beyond[:, r], rank, P * r - 0.5, None, ALU.is_gt)
        L(last)
        L(tt(self.part[:], self.beyond[:, 0:5], self.beyond[:, 1:6], ALU.subtract))
        L(tt(self.valr[:], self.val[:].rearrange("p j t e -> p (j t) e").unsqueeze(2).to_broadcast([P, 2 * NT, 5, NE]),
             self.part[:].rearrange("p r n -> p n r").unsqueeze(3).to_broadcast([P, 2 * NT, 5, NE]), ALU.mult))
        L(dve.tensor_reduce(slot, self.beyond[:, 1:5].rearrange("p r n -> p n r"), AX, ALU.add))
        L(dve.scalar_tensor_tensor(out=slot, in0=slot, scalar=float(-P), in1=rank, op0=ALU.mult, op1=ALU.add))
        tt(self.SL[:], cst(k, "slot").unsqueeze(1).to_broadcast([P, 2 * NT, P]),
           slot.unsqueeze(2).to_broadcast([P, 2 * NT, P]), ALU.is_equal).then_inc(self.slots, 1)
        dve.wait_ge(self.tabled, 1)
        L(dve.tensor_copy(k.table[:], bank(k, 7)[:, 256:256 + 5 * NE]))
        place(k, l, dve, ch, k.table[:, 0:NE], self.flag, 0).then_inc(self.ready, 1)


def place(k, l, dve, ch, table, f, col):
    cols = slice(col, col + table.shape[1])
    dve.tensor_scalar(f[:, 0], table, 0.0, 8192.0, ALU.is_equal, ALU.mult)
    ch.link(dve.tensor_scalar(f[:, 1], table, TOK + 0.5, float(TOK), ALU.is_gt, ALU.mult))
    ch.link(dve.scalar_tensor_tensor(out=f[:, 0], in0=table, scalar=-1.0, in1=f[:, 0], op0=ALU.add, op1=ALU.add))
    dve.tensor_copy(k.put[l][:, cols], f[:, 0])
    ch.link(dve.tensor_tensor(f[:, 1], f[:, 0], f[:, 1], ALU.subtract))
    return dve.tensor_copy(k.get[l][:, cols], f[:, 1])


def project_out(k, st):
    nc, A, sem = k.nc, k.A, k.sem
    wo = k.wo
    norm = RowNorm(k, st, "mixnorm0", A["ln_mix_g"][0], A["ln_mix_b"][0])
    route = Router(k, st, 0)
    mixed, taken, stored = (sem(n) for n in ("mixed0", "mixed0_taken", "h0_stored"))
    block = st.enter_context(nc.Block())

    @block.sync
    def _(sp):
        norm.load(sp)
        route.load(sp)
        first_experts(k, sp, 0, 0, 1)
        for t in range(NT):
            if t == NT - 1:
                sp.wait_ge(mixed, 2)
                first_experts(k, sp, 0, 1, 2)
            sp.wait_ge(norm.done, t + 1)
            sp.dma_start(k.h_scr[0][t * P:t * P + rows_of(t)], k.h[0:rows_of(t), t]).then_inc(stored, 16)
        sp.wait_ge(stored, 16 * NT)

    @block.tensor
    def _(pe):
        for hh in range(2):
            for kk in range(6):
                last = pe.matmul(bank(k, hh)[0:NS], k.mixT[:, kk, SEQ:TOK], wo[kk // 4][:, kk % 4, 512 * hh:512 * hh + 512],
                                 start=kk == 0, stop=kk == 5)
            last.then_inc(mixed, 1)
        for t in range(NT):
            route.turn(pe, t, norm.done)
            if t:
                route.logits(pe, t - 1)
        route.logits(pe, NT - 1)
        route.pe_tables(pe)

    @block.scalar
    def _(act):
        for t in range(NT + 2):
            if t < NT:
                norm.normalise(act, t)
            if t >= 2:
                route.keep(act.copy, act.wait_ge, t - 2, 0)
        route.act(act)

    @block.vector
    def _(dve):
        ch = Chain(dve, k.dve_chain)
        ch.n = k.dve_n
        for t in range(NT + 2):
            if t == PT:
                for hh in range(2):
                    dve.wait_ge(mixed, hh + 1)
                    z = k.h[0:NS, t, 512 * hh:512 * hh + 512]
                    dve.scalar_tensor_tensor(out=z, in0=z, scalar=ALPHA, in1=bank(k, hh)[0:NS],
                                             op0=ALU.mult, op1=ALU.add).then_inc(taken, 1)
                dve.wait_ge(taken, 2)
            if t < NT:
                norm.moments(dve, ch, t)
            if t == NT:
                norm.gain(dve, NT - 1)
            if t >= 2:
                route.keep(dve.tensor_copy, dve.wait_ge, t - 2, 1)
        route.dve(dve, ch)
        k.dve_n = ch.n

    @block.gpsimd
    def _(pool):
        for t in range(NT + 1):
            if t < NT:
                norm.power(pool, t)
            if t:
                norm.offset(pool, t - 1)


NW = 4


def load_expert(k, sp, l, slot, e, done):
    A = k.A
    w13, w2 = (k.w13a, k.w2a) if slot < 2 else (k.w13b, k.w2b)
    slot %= 2
    sp.dma_start(w13[:, slot, :, 0:DE], A["moe_w1"][l, e].rearrange("(k p) f -> p k f", p=P)).then_inc(done, 16)
    sp.dma_start(w13[:, slot, :, DE:2 * DE], A["moe_w3"][l, e].rearrange("(k p) f -> p k f", p=P)).then_inc(done, 16)
    sp.dma_start(w2[:, slot], A["moe_w2"][l, e].rearrange("(k p) n -> p k n", p=P)).then_inc(done, 16)


def first_experts(k, sp, l, e0, e1):
    for e in range(e0, e1):
        load_expert(k, sp, l, e, e, k.w_moe[l][e])


class FurtherPasses:

    def __init__(self, k, st, l):
        self.k, self.l = k, l
        sb = lambda name, shape: st.enter_context(k.nc.sbuf_tensor(f"further{l}_{name}", shape, F32))
        self.ex, self.cum, self.M = sb("exists", [P, 2, 4 * NE]), sb("cumulated", [P, 4 * NE]), sb("pick", [P, MAX_EXTRA, 4 * NE])
        self.M2, self.xf = sb("pick2", [P, MAX_EXTRA, 4 * NE]), sb("experts", [P, MAX_EXTRA + 1])
        self.den = sb("weight_sum", [P, 2, NT])
        self.T, self.flag = sb("table", [P, MAX_EXTRA]), sb("flags", [P, 2, MAX_EXTRA])

    def normalise_weights(self, dve, ch):
        k, gates, den, L, tt = self.k, self.k.gates[self.l], self.den, ch.link, dve.tensor_tensor
        dve.tensor_scalar(den[:, 1], cst(k, "valid"), -1.0, 1.0, ALU.mult, ALU.add)
        L(tt(den[:, 0], gates[:, 0], gates[:, 1], ALU.add))
        L(tt(den[:, 0], den[:, 0], den[:, 1], ALU.add))
        L(dve.reciprocal(den[:, 0], den[:, 0]))
        for j in range(2):
            last = tt(gates[:, j], gates[:, j], den[:, 0], ALU.mult)
        L(last)

    def dve(self, dve, ch):
        k, l, L, tt = self.k, self.l, ch.link, dve.tensor_tensor
        ex, cum = self.ex, self.cum
        for r in range(1, 5):
            last = dve.tensor_scalar(ex[:, 0, (r - 1) * NE:r * NE], k.counts[:], float(P * r), None, ALU.is_gt)
        L(last)
        L(dve.tensor_tensor_scan(cum[:], cst(k, "ones")[:, 0:4 * NE], ex[:, 0], 0.0, ALU.mult, ALU.add))
        L(tt(ex[:, 1], cum[:], ex[:, 0], ALU.subtract))
        over_j = lambda x: x.unsqueeze(1).to_broadcast([P, MAX_EXTRA, 4 * NE])
        L(tt(self.M[:], over_j(ex[:, 1]), cst(k, "slot")[:, 0:MAX_EXTRA].unsqueeze(2).to_broadcast([P, MAX_EXTRA, 4 * NE]),
             ALU.is_equal))
        L(tt(self.M[:], self.M[:], over_j(ex[:, 0]), ALU.mult))
        eidx = cst(k, "eidx").unsqueeze(1).unsqueeze(1).to_broadcast([P, MAX_EXTRA, 4, NE])
        L(tt(self.M2[:].rearrange("p j (r e) -> p j r e", e=NE), self.M[:].rearrange("p j (r e) -> p j r e", e=NE), eidx,
             ALU.mult))
        L(dve.tensor_reduce(self.xf[:, 0:MAX_EXTRA], self.M2[:], AX, ALU.add))
        L(dve.tensor_copy(self.xf[:, MAX_EXTRA:MAX_EXTRA + 1], cum[:, 4 * NE - 1:4 * NE]))
        L(dve.tensor_copy(k.extras[l][:], self.xf[:]))
        L(tt(self.M[:], self.M[:], over_j(k.table[:, NE:5 * NE]), ALU.mult))
        L(dve.tensor_reduce(self.T[:], self.M[:], AX, ALU.add))
        L(dve.memset(k.get[l][:, NE + MAX_EXTRA:NE + MAX_EXTRA + 1], 8192))
        return place(k, l, dve, ch, self.T[:], self.flag, NE)


def experts(k, st, l):
    nc, A = k.nc, k.A
    sb = lambda name, shape, dt=F32: st.enter_context(nc.sbuf_tensor(f"moe{l}_{name}", shape, dt))
    XG, XT = sb("rows", [P, NW, D]), sb("rowsT", [P, KT, P])
    HS, G, GT = sb("silu", [P, DE]), sb("gated", [P, DE]), sb("gatedT", [P, 2, P])
    Y = sb("results", [P, NW, D])
    gi, pi = sb("get_column", [P, NW], I32), sb("put_column", [P, NW], I32)
    sem = lambda n: k.sem(f"moe{l}_{n}")
    got, put = [sem(f"got{i}") for i in range(NW)], [sem(f"put{i}") for i in range(NW)]
    (cleared, columns, fetches, stores, x_turned, x_kept, h_done, silu_done, g_ready, g_turned, gT_kept, y_done, y_kept) = (
        sem(n) for n in ("cleared", "columns", "fetches", "stores", "x_turned", "x_kept", "h_done", "silu_done", "g_ready", "g_turned", "gT_kept",
                         "y_done", "y_kept"))
    (e_w, e_got, e_put, e_columns, e_x_turned, e_x_kept, e_h, e_silu, e_g, e_g_turned, e_gT, e_y, e_y_kept) = (
        sem("e_" + n) for n in ("w", "got", "put", "columns", "x_turned", "x_kept", "h_done", "silu_done", "g_ready",
                                "g_turned", "gT_kept", "y_done", "y_kept"))
    pass_sem = sem("carried")
    w_in = k.w_moe[l]
    w13 = lambda s: (k.w13a, k.w13b)[s // 2][:, s % 2]
    w2 = lambda s: (k.w2a, k.w2b)[s // 2][:, s % 2]
    further, further_ready = FurtherPasses(k, st, l), sem("further_ready")
    block = st.enter_context(nc.Block())

    def extra_passes(engine, body):
        engine.wait_ge(further_ready, 1)
        n = engine.value_load(k.extras[l][0:1, MAX_EXTRA:MAX_EXTRA + 1], min_val=0, max_val=MAX_EXTRA)
        with engine.If(n > 0):
            with engine.Fori(0, n) as j:
                body(j)

    @block.sync
    def _(sp):
        for i in range(NW):
            sp.wait_ge(got[i], 16)
        for e in range(k.n_ahead[l], NW):
            load_expert(k, sp, l, e, e, w_in[e])
        with sp.Fori(1, NE // NW) as q:
            for c in range(NW):
                rows = [A[n][l, bass.ds(4 * q + c, 1)].rearrange("o (k p) f -> p (o k) f", p=P)
                        for n in ("moe_w1", "moe_w3", "moe_w2")]
                b, s = (k.w13a, k.w13b)[c // 2], c % 2
                sp.wait_ge(y_done, 4 * q + (c - 3))
                sp.dma_start(b[:, s, :, 0:DE], rows[0]).then_inc(w_in[c], 16)
                sp.dma_start(b[:, s, :, DE:2 * DE], rows[1]).then_inc(w_in[c], 16)
                sp.dma_start(w2(c), rows[2]).then_inc(w_in[c], 16)
        sp.wait_ge(y_done, NE - 3)

        def body(j):
            e = sp.value_load(k.extras[l][0:1, bass.ds(j, 1)], min_val=0, max_val=NE - 1)
            rows = [A[n][l, bass.ds(e, 1)].rearrange("o (k p) f -> p (o k) f", p=P)
                    for n in ("moe_w1", "moe_w3", "moe_w2")]
            sp.wait_ge(e_y, j)
            sp.dma_start(k.w13a[:, 0, :, 0:DE], rows[0]).then_inc(e_w, 16)
            sp.dma_start(k.w13a[:, 0, :, DE:2 * DE], rows[1]).then_inc(e_w, 16)
            sp.dma_start(w2(0), rows[2]).then_inc(e_w, 16)
        extra_passes(sp, body)

    @block.tensor
    def _(pe):
        ident = cst(k, "ident")

        def turn_x(slot):
            for kk in range(KT):
                last = pe.transpose(bank(k, kk // 4)[:, (kk % 4) * P:(kk % 4 + 1) * P],
                                    XG[:, slot, kk * P:(kk + 1) * P], ident)
            return last

        def up(slot, b):
            for kk in range(KT):
                last = pe.matmul(bank(k, 2 + b), XT[:, kk], w13(slot)[:, kk], start=kk == 0, stop=kk == KT - 1)
            return last

        def turn_g():
            for f in range(2):
                last = pe.transpose(bank(k, 4)[:, f * P:(f + 1) * P], G[:, f * P:(f + 1) * P], ident)
            return last

        def down(slot):
            for hh in range(2):
                for f in range(2):
                    last = pe.matmul(bank(k, 5 + hh), GT[:, f], w2(slot)[:, f, 512 * hh:512 * hh + 512],
                                     start=f == 0, stop=f == 1)
            return last

        def step(q, c):
            i = 4 * q + c
            pe.wait_ge(x_kept, 2 * (i + 1))
            pe.wait_ge(w_in[c % 4], 48 * (q + c // 4 + 1))
            if not isinstance(i, int) or i >= 2:
                pe.wait_ge(g_ready, i - 1)
            up(c % 4, c % 2).then_inc(h_done, 1)
            if c < NE - 1:
                pe.wait_ge(got[(c + 1) % NW], 16 * (q + (c + 1) // NW + 1))
                turn_x((c + 1) % NW).then_inc(x_turned, 1)
            if not isinstance(i, int) or i >= 1:
                pe.wait_ge(gT_kept, i)
                if not isinstance(i, int) or i >= 2:
                    pe.wait_ge(y_kept, 2 * (i - 1))
                down((c - 1) % 4).then_inc(y_done, 1)
            pe.wait_ge(g_ready, i + 1)
            turn_g().then_inc(g_turned, 1)

        pe.wait_ge(got[0], 16)
        turn_x(0).then_inc(x_turned, 1)
        for c in range(3):
            step(0, c)
        with pe.Fori(0, 3) as q:
            for c in range(3, 7):
                step(q, c)
        step(0, NE - 1)
        pe.wait_ge(gT_kept, NE)
        pe.wait_ge(y_kept, 2 * (NE - 1))
        down((NE - 1) % 4).then_inc(y_done, 1)

        def body(j):
            pe.wait_ge(e_got, 16 * j + 16)
            turn_x(0).then_inc(e_x_turned, 1)
            pe.wait_ge(e_x_kept, 2 * j + 2)
            pe.wait_ge(e_w, 48 * j + 48)
            up(0, 0).then_inc(e_h, 1)
            pe.wait_ge(e_g, j + 1)
            turn_g().then_inc(e_g_turned, 1)
            pe.wait_ge(e_gT, j + 1)
            down(0).then_inc(e_y, 1)
        extra_passes(pe, body)

    @block.scalar
    def _(act):
        def keep_x():
            return act.copy(XT[:, 0:4], bank(k, 0))

        def silu(b):
            return act.activation(HS[:], bank(k, 2 + b)[:, 0:DE], ACT.Silu)

        def keep_y(slot):
            return act.copy(Y[:, slot, 0:512], bank(k, 5))

        def keep_last_y(q, c):
            i = 4 * q + c
            act.wait_ge(y_done, i)
            if not isinstance(i, int) or i >= NW + 1:
                act.wait_ge(put[(c - 1) % NW], 16 * (q + (c - 1) // NW))
            keep_y((c - 1) % NW).then_inc(y_kept, 1)

        def step(q, c):
            i = 4 * q + c
            act.wait_ge(h_done, i + 1)
            if not isinstance(i, int) or i >= 1:
                act.wait_ge(g_ready, i)
            silu(c % 2).then_inc(silu_done, 1)
            if c < NE - 1:
                act.wait_ge(x_turned, i + 2)
                keep_x().then_inc(x_kept, 1)
            if not isinstance(i, int) or i >= 1:
                keep_last_y(q, c)

        act.wait_ge(x_turned, 1)
        keep_x().then_inc(x_kept, 1)
        for c in range(3):
            step(0, c)
        with act.Fori(0, 3) as q:
            for c in range(3, 7):
                step(q, c)
        step(0, NE - 1)
        keep_last_y(0, NE)
        act.wait_ge(put[0], 16 * (NE // NW))

        def body(j):
            act.wait_ge(e_x_turned, j + 1)
            keep_x().then_inc(e_x_kept, 1)
            act.wait_ge(e_h, j + 1)
            silu(0).then_inc(e_silu, 1)
            act.wait_ge(e_y, j + 1)
            act.wait_ge(e_put, 16 * j)
            keep_y(0).then_inc(e_y_kept, 1)
        extra_passes(act, body)

    @block.vector
    def _(dve):
        def keep_x():
            return dve.tensor_copy(XT[:, 4:8], bank(k, 1))

        def gate(b):
            return dve.tensor_tensor(G[:], HS[:], bank(k, 2 + b)[:, DE:2 * DE], ALU.mult)

        def keep_g():
            return dve.tensor_copy(GT[:], bank(k, 4)[:, 0:2 * P])

        def keep_y(slot):
            return dve.tensor_copy(Y[:, slot, 512:1024], bank(k, 6))

        def keep_last_y(q, c):
            i = 4 * q + c
            dve.wait_ge(y_done, i)
            if not isinstance(i, int) or i >= NW + 1:
                dve.wait_ge(put[(c - 1) % NW], 16 * (q + (c - 1) // NW))
            keep_y((c - 1) % NW).then_inc(y_kept, 1)

        def step(q, c):
            i = 4 * q + c
            dve.wait_ge(silu_done, i + 1)
            if not isinstance(i, int) or i >= 1:
                dve.wait_ge(g_turned, i)
            gate(c % 2).then_inc(g_ready, 1)
            if c < NE - 1:
                dve.wait_ge(x_turned, i + 2)
                keep_x().then_inc(x_kept, 1)
            if not isinstance(i, int) or i >= 1:
                keep_last_y(q, c)
            dve.wait_ge(g_turned, i + 1)
            keep_g().then_inc(gT_kept, 1)

        for i in range(NW):
            dve.memset(XG[:, i], 0.0).then_inc(cleared, 1)
        dve.wait_ge(x_turned, 1)
        keep_x().then_inc(x_kept, 1)
        ch = Chain(dve, k.dve_chain)
        ch.n = k.dve_n
        further.dve(dve, ch).then_inc(further_ready, 1)
        further.normalise_weights(dve, ch)
        k.dve_n = ch.n
        for c in range(3):
            step(0, c)
        with dve.Fori(0, 3) as q:
            for c in range(3, 7):
                step(q, c)
        step(0, NE - 1)
        keep_last_y(0, NE)
        dve.wait_ge(put[0], 16 * (NE // NW))

        def body(j):
            dve.wait_ge(e_x_turned, j + 1)
            keep_x().then_inc(e_x_kept, 1)
            dve.wait_ge(e_silu, j + 1)
            gate(0).then_inc(e_g, 1)
            dve.wait_ge(e_g_turned, j + 1)
            keep_g().then_inc(e_gT, 1)
            dve.wait_ge(e_y, j + 1)
            dve.wait_ge(e_put, 16 * j)
            keep_y(0).then_inc(e_y_kept, 1)
        extra_passes(dve, body)

    @block.gpsimd
    def _(pool):
        def hold(s, value):
            pool.wait_ge(s, value)
            pool.sem_inc(pass_sem, 1)

        def take_get(col, slot, signal):
            pool.tensor_copy(gi[:, slot:slot + 1], k.get[l][:, col]).then_inc(signal, 1)

        def take_put(col, slot, signal):
            pool.tensor_copy(pi[:, slot:slot + 1], k.put[l][:, col]).then_inc(signal, 1)

        def gather(slot, signal):
            pool.indirect_dma_start(out=XG[:, slot], out_offset=None, in_=k.h_scr[l],
                                    in_offset=bass.IndirectOffsetOnAxis(ap=gi[:, slot:slot + 1], axis=0),
                                    bounds_check=TOK - 1, oob_is_err=False).then_inc(signal, 16)

        def scatter(slot, signal):
            pool.indirect_dma_start(out=k.y_scr[l], out_offset=bass.IndirectOffsetOnAxis(ap=pi[:, slot:slot + 1], axis=0),
                                    in_=Y[:, slot], in_offset=None, bounds_check=2 * TOK - 1, oob_is_err=False
                                    ).then_inc(signal, 16)

        for i in range(NW):
            take_get(slice(i, i + 1), i, columns)
        pool.wait_ge(columns, NW)
        for i in range(NW):
            pool.wait_ge(cleared, i + 1)
            gather(i, got[i])

        def step(q, c):
            i = NW * q + c
            if not isinstance(i, int) or i + NW <= NE:
                hold(x_turned, i + 1)
                take_get(bass.ds(i + NW, 1), c, fetches)
                hold(fetches, i + 1)
                gather(c, e_got if isinstance(i, int) and i + NW == NE else got[c])
            if not isinstance(i, int) or i >= NW:
                hold(put[c], 16 * q)
            take_put(bass.ds(i, 1), c, stores)
            hold(stores, i + 1)
            hold(y_kept, 2 * i + 2)
            scatter(c, put[c])

        for c in range(NW):
            step(0, c)
        with pool.Fori(1, NE // NW - 1) as q:
            for c in range(NW):
                step(q, c)
        pool.wait_ge(further_ready, 1)
        for c in range(NW):
            step(NE // NW - 1, c)
        for i in range(NW):
            pool.wait_ge(put[i], 16 * (NE // NW))
        pool.wait_ge(e_got, 16)

        def body(j):
            take_put(bass.ds(j + NE, 1), 0, e_columns)
            hold(e_columns, 2 * j + 1)
            hold(e_x_turned, j + 1)
            take_get(bass.ds(j + NE + 1, 1), 0, e_columns)
            hold(e_columns, 2 * j + 2)
            gather(0, e_got)
            hold(e_y_kept, 2 * j + 2)
            scatter(0, e_put)
            hold(e_put, 16 * j + 16)
            hold(e_got, 16 * j + 32)
        extra_passes(pool, body)


class Combine:

    def __init__(self, k, st, l):
        self.k, self.l = k, l
        self.y = st.enter_context(k.nc.sbuf_tensor(f"join{l}_results", [P, 2, 2, D], F32))
        self.y_in = [k.sem(f"join{l}_in0"), k.sem(f"join{l}_in1")]
        self.scaled, self.joined = k.sem(f"join{l}_scaled"), k.sem(f"join{l}_joined")

    def load(self, sp, t):
        R = rows_of(t)
        if t >= 2:
            sp.wait_ge(self.joined, t - 1)
        for j in range(2):
            a = j * TOK + t * P
            sp.dma_start(self.y[0:R, t % 2, j], self.k.y_scr[self.l][a:a + R]).then_inc(self.y_in[t % 2], 16)

    def scale(self, act, t):
        h = self.k.h[0:rows_of(t), t]
        act.mul(h, h, ALPHA).then_inc(self.scaled, 1)

    def join(self, dve, ch, t):
        R, k = rows_of(t), self.k
        dve.wait_ge(self.y_in[t % 2], 32 * (t // 2 + 1))
        dve.wait_ge(self.scaled, t + 1)
        for j in range(2):
            last = dve.scalar_tensor_tensor(out=k.h[0:R, t], in0=self.y[0:R, t % 2, j],
                                            scalar=k.gates[self.l][0:R, j, t:t + 1], in1=k.h[0:R, t],
                                            op0=ALU.mult, op1=ALU.add)
            if j == 0:
                ch.link(last)
        last.then_inc(self.joined, 1)
        dve.wait_ge(self.joined, t + 1)


def pool_mixer(k, st):
    nc, A, sem = k.nc, k.A, k.sem
    sb = lambda name, shape, dt=F32: st.enter_context(nc.sbuf_tensor(name, shape, dt))
    dT = sb("pooledT", [P, KT, TOK])
    pw = sb("pool_w", [P, 4, 2, 256])
    vec = sb("pool_bias_scale", [P, 2, D])
    with ExitStack() as early:
        esb = lambda name, shape: early.enter_context(nc.sbuf_tensor(name, shape, F32))
        join = Combine(k, early, 0)
        norm = RowNorm(k, early, "ffnnorm0", A["ln_ffn_g"][0], A["ln_ffn_b"][0])
        srow = esb("pool_state_rows", [15 * NS, D])
        band = esb("pool_bands", [P, len(WINDOWS), BAND])
        pooled, kept, s_in, v_in, ended = (sem(n) for n in ("pooled", "pooled_kept", "pool_state_in", "pool_w_in",
                                                            "pool_out"))
        block = early.enter_context(nc.Block())

        @block.sync
        def _(sp):
            for t in range(2):
                join.load(sp, t)
            norm.load(sp)
            sp.dma_start(band[:], A["consts"][:, NCONST:].rearrange("p (g c) -> p g c", c=BAND)).then_inc(s_in, 16)
            sp.dma_start(srow[:], A["state_pool"][0].rearrange("n w d -> (n w) d")).then_inc(s_in, 16)
            for t in range(2, NT):
                join.load(sp, t)
            sp.dma_start(pw[:], A["pool_w"][0].rearrange("g (c p) n -> p g c n", p=P)).then_inc(v_in, 16)
            sp.dma_start(vec[:, 0], A["pool_b"][0].rearrange("g n -> (g n)").partition_broadcast(P)).then_inc(v_in, 16)
            sp.dma_start(vec[:, 1], A["pool_scale"][0].partition_broadcast(P)).then_inc(v_in, 16)
            sp.dma_start(A["s_pool"][0, :, 0:14], A["state_pool"][0, :, 1:15]).then_inc(ended, 16)
            first_experts(k, sp, 1, 0, 2)
            sp.wait_ge(norm.done, NT)
            sp.dma_start(A["p_pool"][0, 0], k.h[P - 15:P, PT - 1]).then_inc(ended, 16)
            sp.dma_start(A["s_pool"][0, :, 14], k.h[0:NS, PT]).then_inc(ended, 16)
            sp.wait_ge(ended, 48)
            sp.wait_ge(v_in, 48)

        @block.tensor
        def _(pe):
            pe.wait_ge(s_in, 32)
            for t in range(NT):
                R = rows_of(t)
                pe.wait_ge(norm.done, t + 1)
                if t >= 2:
                    pe.wait_ge(kept, 2 * (t - 1))
                for kk in range(KT):
                    cols = slice(kk * P, (kk + 1) * P)
                    out = bank(k, 2 * (t % 2) + kk // 4)[:, (kk % 4) * P:(kk % 4) * P + R]
                    b = band[:, kk // 2]
                    if t == 0:
                        last = pe.matmul(out, k.h[:, t, cols], b[:, 0:P], start=True, stop=True)
                    elif t < PT:
                        pe.matmul(out, k.h[:, t, cols], b[:, P:2 * P], start=True, stop=False)
                        last = pe.matmul(out[:, 0:16], k.h[:, t - 1, cols], b[:, 2 * P:2 * P + 16], start=False,
                                         stop=True)
                    else:
                        o = 2 * P + 16
                        pe.matmul(out, srow[:, cols], b[0:15 * NS, o:o + NS], start=True, stop=False)
                        last = pe.matmul(out, k.h[0:NS, t, cols], b[0:NS, o + NS:o + 2 * NS], start=False, stop=True)
                last.then_inc(pooled, 1)

        def keep(copy, wait, t, half):
            R = rows_of(t)
            wait(pooled, t + 1)
            src = bank(k, 2 * (t % 2) + half).rearrange("p (k c) -> p k c", c=P)[:, :, 0:R]
            copy(dT[:, 4 * half:4 * half + 4, t * P:t * P + R], src).then_inc(kept, 1)

        @block.scalar
        def _(act):
            for t in range(NT):
                join.scale(act, t)
            for t in range(NT + 2):
                if t < NT:
                    norm.normalise(act, t)
                if t >= 2:
                    for half in range(2):
                        keep(act.copy, act.wait_ge, t - 2, half)

        @block.vector
        def _(dve):
            ch = Chain(dve, k.dve_chain)
            ch.n = k.dve_n
            for t in range(NT):
                join.join(dve, ch, t)
                norm.moments(dve, ch, t)
            norm.gain(dve, NT - 1)
            k.dve_n = ch.n

        @block.gpsimd
        def _(pool):
            for t in range(NT + 1):
                if t < NT:
                    norm.power(pool, t)
                if t:
                    norm.offset(pool, t - 1)

    k.end_stage()
    norm1 = RowNorm(k, st, "mixnorm1", A["ln_mix_g"][1], A["ln_mix_b"][1])
    route = Router(k, st, 1)
    tmp = sb("pool_rows", [P, 2, D])
    mixed, biased, scaled, joined, stored = (sem(n) for n in (
        "mixed1", "pool_biased", "pool_scaled", "mixed1_joined", "h1_stored"))
    block = st.enter_context(nc.Block())

    @block.sync
    def _(sp):
        norm1.load(sp)
        route.load(sp)
        first_experts(k, sp, 1, 2, NW)
        for t in range(NT):
            sp.wait_ge(norm1.done, t + 1)
            sp.dma_start(k.h_scr[1][t * P:t * P + rows_of(t)], k.h[0:rows_of(t), t]).then_inc(stored, 16)
        sp.wait_ge(stored, 16 * NT)

    @block.tensor
    def _(pe):
        def mix(t):
            R = rows_of(t)
            if t >= 2:
                pe.wait_ge(biased, t - 1)
            for g in range(4):
                for c in range(2):
                    last = pe.matmul(bank(k, 2 * (t % 2) + g // 2)[0:R, (g % 2) * 256:(g % 2 + 1) * 256],
                                     dT[:, 2 * g + c, t * P:t * P + R], pw[:, g, c], start=c == 0, stop=c == 1)
            last.then_inc(mixed, 1)

        for t in range(3):
            mix(t)
        for t in range(NT):
            if t + 3 < NT:
                mix(t + 3)
            route.turn(pe, t, norm1.done)
            if t:
                route.logits(pe, t - 1)
        route.logits(pe, NT - 1)
        route.pe_tables(pe)

    @block.scalar
    def _(act):
        for t in range(NT + 2):
            if t < NT:
                norm1.normalise(act, t)
            if t >= 2:
                route.keep(act.copy, act.wait_ge, t - 2, 0)
        route.act(act)

    @block.vector
    def _(dve):
        ch = Chain(dve, k.dve_chain)
        ch.n = k.dve_n
        for t in range(NT + 3):
            if t < NT:
                R = rows_of(t)
                dve.wait_ge(mixed, t + 1)
                if t >= 2:
                    dve.wait_ge(joined, t - 1)
                dve.tensor_tensor(tmp[0:R, t % 2], k.ps[0:R, 1024 * (t % 2):1024 * (t % 2) + D], vec[0:R, 0], ALU.add
                                  ).then_inc(biased, 1)
            if 1 <= t <= NT:
                R = rows_of(t - 1)
                h = k.h[0:R, t - 1]
                dve.wait_ge(scaled, t)
                dve.scalar_tensor_tensor(out=h, in0=h, scalar=ALPHA, in1=tmp[0:R, (t - 1) % 2], op0=ALU.mult, op1=ALU.add
                                         ).then_inc(joined, 1)
                dve.wait_ge(joined, t)
                norm1.moments(dve, ch, t - 1)
            if t == NT + 1:
                norm1.gain(dve, NT - 1)
            if t >= 3:
                route.keep(dve.tensor_copy, dve.wait_ge, t - 3, 1)
        route.dve(dve, ch)
        k.dve_n = ch.n

    @block.gpsimd
    def _(pool):
        for t in range(NT + 2):
            if t < NT:
                R = rows_of(t)
                pool.wait_ge(biased, t + 1)
                pool.tensor_tensor(tmp[0:R, t % 2], tmp[0:R, t % 2], vec[0:R, 1], ALU.mult).then_inc(scaled, 1)
            if 1 <= t <= NT:
                norm1.power(pool, t - 1)
            if t >= 2:
                norm1.offset(pool, t - 2)


def finish(k, st):
    nc, A = k.nc, k.A
    join = Combine(k, st, 1)
    norm = RowNorm(k, st, "ffnnorm1", A["ln_ffn_g"][1], A["ln_ffn_b"][1])
    stored = k.sem("y_stored")
    block = st.enter_context(nc.Block())

    @block.sync
    def _(sp):
        for t in range(NT):
            join.load(sp, t)
            if t == 1:
                norm.load(sp)
        for t in range(NT):
            sp.wait_ge(norm.done, t + 1)
            dst = A["y_prompt"][0, t * P:(t + 1) * P] if t < PT else A["y_sample"][:, 0]
            sp.dma_start(dst, k.h[0:rows_of(t), t]).then_inc(stored, 16)
        sp.wait_ge(stored, 16 * NT)

    @block.scalar
    def _(act):
        for t in range(NT):
            join.scale(act, t)
        for t in range(NT):
            norm.normalise(act, t)

    @block.vector
    def _(dve):
        ch = Chain(dve, k.dve_chain)
        ch.n = k.dve_n
        for t in range(NT):
            join.join(dve, ch, t)
            norm.moments(dve, ch, t)
        norm.gain(dve, NT - 1)

    @block.gpsimd
    def _(pool):
        for t in range(NT + 1):
            if t < NT:
                norm.power(pool, t)
            if t:
                norm.offset(pool, t - 1)

def program(nc, A, stages=9):
    with ExitStack() as top:
        k = Chip()
        k.nc, k.A, k.top = nc, A, top
        stage_sems = []

        def stage_sem(name):
            stage_sems.append(nc.alloc_semaphore(name=name))
            return stage_sems[-1]

        def end_stage():
            nc.clear_and_free_semaphores(stage_sems)
            stage_sems.clear()
            nc.all_engine_barrier()

        k.end_stage = end_stage
        k.sem = lambda name: top.enter_context(nc.semaphore(name))
        sb = lambda name, shape, dt=F32: top.enter_context(nc.sbuf_tensor(name, shape, dt))
        k.ps = top.enter_context(nc.psum_tensor("banks", [P, 8 * 512], F32))
        k.cst = sb("constants", [P, NCONST])
        k.q_scr = nc.dram_tensor("sample_q", [NS, NG, AW], F32).ap()
        k.kv_scr = nc.dram_tensor("sample_kv", [NS, NG, 2, AW], F32).ap()
        k.h_scr = [nc.dram_tensor(f"rows{l}", [TOK, D], F32).ap() for l in range(2)]
        k.h = sb("h", [P, NT, D])
        k.n_ahead = (2, NW)
        k.y_scr = [nc.dram_tensor(f"results{l}", [2 * TOK, D], F32).ap() for l in range(2)]
        k.w13a = sb("expert_w13_a", [P, 2, KT, 2 * DE])
        k.w2a = sb("expert_w2_a", [P, 2, 2, D])
        k.w_moe = [[k.sem(f"experts{l}_in{i}") for i in range(NW)] for l in range(2)]
        k.gates = [sb(f"gates{l}", [P, 2, NT]) for l in range(2)]
        k.put = [sb(f"result_rows{l}", [P, NE + MAX_EXTRA], I32) for l in range(2)]
        k.get = [sb(f"token_rows{l}", [P, NE + MAX_EXTRA + 1], I32) for l in range(2)]
        k.extras = [sb(f"extra_experts{l}", [P, MAX_EXTRA + 1], I32) for l in range(2)]
        k.table, k.counts = sb("slot_table", [P, 5 * NE]), sb("expert_counts", [P, NE])
        k.cst_in, k.copies = k.sem("constants_in"), k.sem("cache_copies")
        k.wo_in, k.x_again_in = k.sem("w_out_in"), k.sem("x_again_in")
        k.dve_chain, k.pool_chain, k.act_chain = k.sem("dve_chain"), k.sem("pool_chain"), k.sem("act_chain")
        k.dve_n = k.pool_n = k.act_n = 0
        k.sem = stage_sem
        with ExitStack() as mid:
            msb = lambda name, shape, dt=F32: mid.enter_context(nc.sbuf_tensor(name, shape, dt))
            k.oT = msb("oT", [P, NG, NPAIR, SEQ])
            k.glu = msb("gluT", [P, 2, 30 + SEQ])
            k.glu_s = msb("gluT_samples", [P, 2, NS])
            k.taps = msb("conv_taps", [P, 2, CW + 1])
            k.conv = msb("convT", [P, 2, TOK])
            k.nm = msb("neg_max", [P, NG, PT, NH])
            k.sums = msb("exp_sums", [P, NG, PT, NH])
            with ExitStack() as st:
                project_and_attend(k, st)
            end_stage()
            k.mixT = msb("mixT", [P, 6, TOK])
            k.wo = [k.w13a[:, 1].rearrange("p (a b) c -> p a (b c)", b=2), k.w2a[:, 1]]
            if stages > 1:
                with ExitStack() as st:
                    merge_and_convolve(k, st)
                end_stage()
            if stages > 2:
                with ExitStack() as st:
                    project_out(k, st)
                end_stage()
        with ExitStack() as mid:
            k.w13b = mid.enter_context(nc.sbuf_tensor("expert_w13_b", [P, 2, KT, 2 * DE], F32))
            k.w2b = mid.enter_context(nc.sbuf_tensor("expert_w2_b", [P, 2, 2, D], F32))
            for n, stage in ((4, lambda st: experts(k, st, 0)), (5, lambda st: pool_mixer(k, st)),
                             (6, lambda st: experts(k, st, 1)), (7, lambda st: finish(k, st))):
                if stages >= n:
                    with ExitStack() as st:
                        stage(st)
                    end_stage()


_INS = ["x_prompt", "x_sample", "cache_attn_w128", "cache_attn_w512", "cache_attn_w2048", "state_conv",
        "state_pool", "w_in", "b_in", "conv_w", "conv_b", "conv_ln_g", "conv_ln_b", "w_out", "pool_w", "pool_b",
        "pool_scale", "ln_mix_g", "ln_mix_b", "ln_ffn_g", "ln_ffn_b", "router_w", "router_bias", "moe_w1",
        "moe_w3", "moe_w2"]
_SHORT = {"cache_attn_w128": "cache0", "cache_attn_w512": "cache1", "cache_attn_w2048": "cache2"}
_OUTS = [("y_prompt", (1, 512, 1024)), ("y_sample", (8, 1, 1024)),
         ("p_attn0", (1, 1, 128, 2, 8, 64)), ("p_attn1", (1, 1, 512, 2, 8, 64)), ("p_attn2", (1, 1, 512, 2, 8, 64)),
         ("p_conv", (1, 1, 30, 256)), ("p_pool", (1, 1, 15, 1024)),
         ("s_attn0", (1, 8, 128, 2, 8, 64)), ("s_attn1", (1, 8, 512, 2, 8, 64)), ("s_attn2", (1, 8, 513, 2, 8, 64)),
         ("s_conv", (1, 8, 30, 256)), ("s_pool", (1, 8, 15, 1024))]


def kernel(**inputs):
    import numpy as _np
    import concourse.bacc as _bacc
    from concourse.bass_utils import run_bass_kernel_spmd as _run

    nc = _bacc.Bacc("TRN2", target_bir_lowering=False, num_devices=1)
    arrays, A = {}, {}
    for name in _INS:
        a = _np.ascontiguousarray(inputs[name])
        arrays[f"in_{name}"] = a
        A[_SHORT.get(name, name)] = nc.dram_tensor(f"in_{name}", a.shape, F32, kind="ExternalInput").ap()
    arrays["in_consts"] = CONST
    A["consts"] = nc.dram_tensor("in_consts", CONST.shape, F32, kind="ExternalInput").ap()
    for name, shape in _OUTS:
        A[name] = nc.dram_tensor(f"out_{name}", shape, F32, kind="ExternalOutput").ap()
    program(nc, A)
    r = _run(nc, [arrays], core_ids=[0])
    return tuple(r.results[0][f"out_{name}"] for name, _ in _OUTS)
```
